# Optimizing a Trainium2 kernel written in Bass

```python
import math
import jax, jax.numpy as jnp
from jax import lax
import numpy as np

D_MODEL = 1024
BATCH = 1
SEQ = 512
DEPTH = 1
DEC_BATCH = 8
DEC_SEQ = 4
PAST_LEN = 256
PAGE_SIZE = 128

N_META = 16
EPS = 1e-6
D_FF = 2816
NH_M = 4
DH_M = D_MODEL // NH_M
D_M = NH_M * DH_M
CONV_W = 4
CHUNK_M = 64
NH_D = 8
DH_D = D_MODEL // (2 * NH_D)
DK_D = 2 * DH_D
DV_D = 2 * DH_D
D_D = NH_D * DV_D
ROT_DIM = DH_D // 4
ROPE_THETA = 500000.0
Q_BLOCK = 128
IN_WIDTHS = (D_M, D_M, NH_M, NH_M, NH_D * DK_D, NH_D * DK_D, D_D, D_MODEL, D_MODEL)
N_IN = sum(IN_WIDTHS)

kernel_name = "mlstm_diffattn_gated_hybrid_step"

def rmsnorm(x, g):
    xf = x.astype(jnp.float32)
    y = xf * lax.rsqrt(jnp.mean(xf * xf, axis=-1, keepdims=True) + EPS)
    return (y * g.astype(jnp.float32)).astype(x.dtype)

def swiglu(x, w_gate, w_up, w_down):
    return (jax.nn.silu(x @ w_gate) * (x @ w_up)) @ w_down

def split_columns(p):
    outs, start = [], 0
    for width in IN_WIDTHS:
        outs.append(p[..., start:start + width])
        start += width
    return outs

def partial_rope(x, pos):
    half = ROT_DIM // 2
    inv_freq = ROPE_THETA ** (-jnp.arange(half, dtype=jnp.float32) / half)
    ang = pos.astype(jnp.float32)[:, None] * inv_freq[None, :]
    cos = jnp.cos(ang)[None, :, None, None, :]
    sin = jnp.sin(ang)[None, :, None, None, :]
    xf = x.astype(jnp.float32)
    x1, x2, rest = xf[..., :half], xf[..., half:ROT_DIM], xf[..., ROT_DIM:]
    out = jnp.concatenate([x1 * cos - x2 * sin, x2 * cos + x1 * sin, rest], axis=-1)
    return out.astype(x.dtype)

def causal_conv(u, buf, w, b):
    T = u.shape[1]
    ext = jnp.concatenate([buf.astype(u.dtype), u], axis=1)
    out = b
    for j in range(CONV_W):
        out = out + ext[:, j:j + T] * w[j]
    return out, ext[:, T:]

def mlstm_chunk(state, inp):
    C, n, m = state
    q, k, v, logi, logf = inp
    L = q.shape[2]
    b = jnp.cumsum(logf, axis=-1)
    causal = jnp.tril(jnp.ones((L, L), dtype=bool))
    d = jnp.where(causal, b[..., :, None] - b[..., None, :] + logi[..., None, :], -jnp.inf)
    inter = b + m[..., None]
    m_t = jnp.maximum(jnp.max(d, axis=-1), inter)
    w_intra = jnp.exp(d - m_t[..., None])
    w_inter = jnp.exp(inter - m_t)
    s = jnp.einsum("bhtk,bhsk->bhts", q, k) * w_intra
    num = jnp.einsum("bhts,bhsv->bhtv", s, v) + w_inter[..., None] * jnp.einsum("bhvk,bhtk->bhtv", C, q)
    den = jnp.sum(s, axis=-1) + w_inter * jnp.einsum("bhk,bhtk->bht", n, q)
    h = num / jnp.maximum(jnp.abs(den), jnp.exp(-m_t))[..., None]
    m_new = m_t[..., -1]
    w_state = jnp.exp(b[..., -1:] - b + logi - m_new[..., None])
    decay = jnp.exp(b[..., -1] + m - m_new)
    C_new = decay[..., None, None] * C + jnp.einsum("bhs,bhsv,bhsk->bhvk", w_state, v, k)
    n_new = decay[..., None] * n + jnp.einsum("bhs,bhsk->bhk", w_state, k)
    return (C_new, n_new, m_new), h

def diff_attention(q, k, v, q_pos, k_pos, lam, lambda_init, subln):
    s = jnp.einsum("bqhmd,bkhmd->bhmqk", q.astype(jnp.float32), k.astype(jnp.float32)) * (DH_D ** -0.5)
    s = jnp.where(k_pos[None, :] <= q_pos[:, None], s, -jnp.inf)
    p = jax.nn.softmax(s, axis=-1)
    a = p[:, :, 0] - lam * p[:, :, 1]
    o = jnp.einsum("bhqk,bkhv->bqhv", a, v.astype(jnp.float32))
    return rmsnorm(o, subln) * (1.0 - lambda_init)

def hybrid_layer(x, pos, past_k, past_v, past_pos, C0, n0, m0, buf0, lw, layer_idx, prompt):
    (ffn1_norm, ffn1_w_gate, ffn1_w_up, ffn1_w_down, mix_norm, w_in, conv_w, conv_b,
     w_mq, w_mk, w_mv, b_igate, b_fgate, mlstm_norm, lambda_q1, lambda_k1,
     lambda_q2, lambda_k2, subln, w_proj_a, w_proj_b, w_out,
     ffn2_norm, ffn2_w_gate, ffn2_w_up, ffn2_w_down) = lw
    f32 = jnp.float32
    B, T, _ = x.shape
    lambda_init = 0.8 - 0.6 * math.exp(-0.3 * layer_idx)

    x = x + 0.5 * swiglu(rmsnorm(x, ffn1_norm), ffn1_w_gate, ffn1_w_up, ffn1_w_down)

    h = rmsnorm(x, mix_norm)
    xm, om, i_pre, f_pre, qd, kd, vd, g_a, g_b = split_columns(h @ w_in)

    c, conv_new = causal_conv(xm, buf0, conv_w, conv_b)
    c = jax.nn.silu(c).reshape(B, T, NH_M, DH_M)
    xh = xm.reshape(B, T, NH_M, DH_M)
    qm = jnp.einsum("bthd,hde->bhte", c, w_mq).astype(f32)
    km = jnp.einsum("bthd,hde->bhte", c, w_mk).astype(f32) * (DH_M ** -0.5)
    vm = jnp.einsum("bthd,hde->bhte", xh, w_mv).astype(f32)
    logi = jnp.swapaxes((i_pre + b_igate).astype(f32), 1, 2)
    logf = jnp.swapaxes(jax.nn.log_sigmoid((f_pre + b_fgate).astype(f32)), 1, 2)
    state = (C0.astype(f32), n0.astype(f32), m0.astype(f32))
    seqs = (qm, km, vm, logi, logf)
    if prompt:
        state, h_lead = mlstm_chunk(state, tuple(a[:, :, :N_META] for a in seqs))
        n_chunks = (T - N_META) // CHUNK_M
        chunks = tuple(
            jnp.moveaxis(a[:, :, N_META:].reshape(a.shape[:2] + (n_chunks, CHUNK_M) + a.shape[3:]), 2, 0)
            for a in seqs)
        state, h_rest = lax.scan(mlstm_chunk, state, chunks)
        h_rest = jnp.moveaxis(h_rest, 0, 2).reshape(B, NH_M, T - N_META, DH_M)
        hm = jnp.concatenate([h_lead, h_rest], axis=2)
    else:
        state, hm = mlstm_chunk(state, seqs)
    C_new, n_new, m_new = state
    hm = rmsnorm(jnp.swapaxes(hm, 1, 2), mlstm_norm) * jax.nn.sigmoid(om.astype(f32)).reshape(B, T, NH_M, DH_M)
    y_a = hm.reshape(B, T, D_M).astype(x.dtype) @ w_proj_a

    lam = (jnp.exp(jnp.sum(lambda_q1.astype(f32) * lambda_k1.astype(f32)))
           - jnp.exp(jnp.sum(lambda_q2.astype(f32) * lambda_k2.astype(f32))) + lambda_init)
    qd = partial_rope(qd.reshape(B, T, NH_D, 2, DH_D), pos)
    kd = partial_rope(kd.reshape(B, T, NH_D, 2, DH_D), pos)
    vd = vd.reshape(B, T, NH_D, DV_D)
    if prompt:
        o_lead = diff_attention(qd[:, :N_META], kd[:, :N_META], vd[:, :N_META],
                                pos[:N_META], pos[:N_META], lam, lambda_init, subln)
        n_blocks = (T - N_META) // Q_BLOCK
        q_blocks = jnp.moveaxis(qd[:, N_META:].reshape(B, n_blocks, Q_BLOCK, NH_D, 2, DH_D), 1, 0)
        pos_blocks = pos[N_META:].reshape(n_blocks, Q_BLOCK)
        o_rest = lax.map(lambda qp: diff_attention(qp[0], kd, vd, qp[1], pos, lam, lambda_init, subln),
                         (q_blocks, pos_blocks))
        o_rest = jnp.moveaxis(o_rest, 0, 1).reshape(B, T - N_META, NH_D, DV_D)
        o = jnp.concatenate([o_lead, o_rest], axis=1)
    else:
        k_all = jnp.concatenate([past_k.reshape(B, -1, NH_D, 2, DH_D).astype(kd.dtype), kd], axis=1)
        v_all = jnp.concatenate([past_v.astype(vd.dtype), vd], axis=1)
        k_pos = jnp.concatenate([past_pos, pos])
        o = diff_attention(qd, k_all, v_all, pos, k_pos, lam, lambda_init, subln)
    y_b = o.reshape(B, T, D_D).astype(x.dtype) @ w_proj_b

    merged = jax.nn.sigmoid(g_a) * y_a + jax.nn.sigmoid(g_b) * y_b
    x = x + merged @ w_out

    x = x + 0.5 * swiglu(rmsnorm(x, ffn2_norm), ffn2_w_gate, ffn2_w_up, ffn2_w_down)
    new_state = (kd.reshape(B, T, NH_D, DK_D), vd, C_new, n_new, m_new, conv_new)
    return x, new_state

def setup_inputs(seed: int = 0) -> dict:
    key = jax.random.key(seed)
    ks = iter(jax.random.split(key, 48))
    f32 = jnp.float32

    def nrm(shape, scale):
        return jax.random.normal(next(ks), shape, f32) * scale

    def gain(shape):
        return 1.0 + nrm(shape, 0.02)

    n_pages = PAST_LEN // PAGE_SIZE
    n_used = DEC_BATCH * n_pages
    n_pool = (n_used * 5) // 4
    x_prompt = nrm((BATCH, SEQ, D_MODEL), 1.0)
    x_sample = nrm((DEC_BATCH, DEC_SEQ, D_MODEL), 1.0)
    cache_k = nrm((DEPTH, n_pool, PAGE_SIZE, NH_D, DK_D), 1.0)
    cache_v = nrm((DEPTH, n_pool, PAGE_SIZE, NH_D, DV_D), 1.0)
    page_table = jax.random.permutation(next(ks), n_pool)[:n_used].reshape(DEC_BATCH, n_pages).astype(jnp.int32)
    state_C = nrm((DEPTH, DEC_BATCH, NH_M, DH_M, DH_M), 0.1)
    state_n = nrm((DEPTH, DEC_BATCH, NH_M, DH_M), 0.1)
    state_m = nrm((DEPTH, DEC_BATCH, NH_M), 0.5)
    state_conv = nrm((DEPTH, DEC_BATCH, CONV_W - 1, D_M), 1.0)
    return {
        "x_prompt": x_prompt,
        "x_sample": x_sample,
        "cache_k": cache_k,
        "cache_v": cache_v,
        "page_table": page_table,
        "state_C": state_C,
        "state_n": state_n,
        "state_m": state_m,
        "state_conv": state_conv,
        "meta_tokens": nrm((N_META, D_MODEL), 1.0),
        "ffn1_norm": gain((DEPTH, D_MODEL)),
        "ffn1_w_gate": nrm((DEPTH, D_MODEL, D_FF), D_MODEL ** -0.5),
        "ffn1_w_up": nrm((DEPTH, D_MODEL, D_FF), D_MODEL ** -0.5),
        "ffn1_w_down": nrm((DEPTH, D_FF, D_MODEL), D_FF ** -0.5),
        "mix_norm": gain((DEPTH, D_MODEL)),
        "w_in": nrm((DEPTH, D_MODEL, N_IN), D_MODEL ** -0.5),
        "conv_w": nrm((DEPTH, CONV_W, D_M), CONV_W ** -0.5),
        "conv_b": nrm((DEPTH, D_M), 0.02),
        "w_mq": nrm((DEPTH, NH_M, DH_M, DH_M), DH_M ** -0.5),
        "w_mk": nrm((DEPTH, NH_M, DH_M, DH_M), DH_M ** -0.5),
        "w_mv": nrm((DEPTH, NH_M, DH_M, DH_M), DH_M ** -0.5),
        "b_igate": nrm((DEPTH, NH_M), 0.1),
        "b_fgate": 3.0 + nrm((DEPTH, NH_M), 0.5),
        "mlstm_norm": gain((DEPTH, NH_M, DH_M)),
        "lambda_q1": nrm((DEPTH, DH_D), 0.1),
        "lambda_k1": nrm((DEPTH, DH_D), 0.1),
        "lambda_q2": nrm((DEPTH, DH_D), 0.1),
        "lambda_k2": nrm((DEPTH, DH_D), 0.1),
        "subln": gain((DEPTH, DV_D)),
        "w_proj_a": nrm((DEPTH, D_M, D_MODEL), D_M ** -0.5),
        "w_proj_b": nrm((DEPTH, D_D, D_MODEL), D_D ** -0.5),
        "w_out": nrm((DEPTH, D_MODEL, D_MODEL), D_MODEL ** -0.5),
        "ffn2_norm": gain((DEPTH, D_MODEL)),
        "ffn2_w_gate": nrm((DEPTH, D_MODEL, D_FF), D_MODEL ** -0.5),
        "ffn2_w_up": nrm((DEPTH, D_MODEL, D_FF), D_MODEL ** -0.5),
        "ffn2_w_down": nrm((DEPTH, D_FF, D_MODEL), D_FF ** -0.5),
        "final_norm": gain((D_MODEL,)),
    }

def reference(x_prompt, x_sample, cache_k, cache_v, page_table, state_C, state_n, state_m, state_conv,
              meta_tokens, ffn1_norm, ffn1_w_gate, ffn1_w_up, ffn1_w_down, mix_norm, w_in,
              conv_w, conv_b, w_mq, w_mk, w_mv, b_igate, b_fgate, mlstm_norm,
              lambda_q1, lambda_k1, lambda_q2, lambda_k2, subln, w_proj_a, w_proj_b, w_out,
              ffn2_norm, ffn2_w_gate, ffn2_w_up, ffn2_w_down, final_norm):
    bp = x_prompt.shape[0]
    bs, n_pages = page_table.shape
    past_len = n_pages * cache_k.shape[2]
    meta = jnp.broadcast_to(meta_tokens.astype(x_prompt.dtype)[None], (bp, N_META, D_MODEL))
    xp = jnp.concatenate([meta, x_prompt], axis=1)
    pos_p = jnp.arange(xp.shape[1], dtype=jnp.int32)
    pos_s = past_len + jnp.arange(x_sample.shape[1], dtype=jnp.int32)
    past_pos = jnp.arange(past_len, dtype=jnp.int32)
    C0p = jnp.zeros((bp, NH_M, DH_M, DH_M), jnp.float32)
    n0p = jnp.zeros((bp, NH_M, DH_M), jnp.float32)
    m0p = jnp.zeros((bp, NH_M), jnp.float32)
    buf0p = jnp.zeros((bp, CONV_W - 1, D_M), x_prompt.dtype)
    xs = x_sample
    st_p, st_s = [], []
    for l in range(DEPTH):
        lw = (ffn1_norm[l], ffn1_w_gate[l], ffn1_w_up[l], ffn1_w_down[l], mix_norm[l], w_in[l],
              conv_w[l], conv_b[l], w_mq[l], w_mk[l], w_mv[l], b_igate[l], b_fgate[l], mlstm_norm[l],
              lambda_q1[l], lambda_k1[l], lambda_q2[l], lambda_k2[l], subln[l],
              w_proj_a[l], w_proj_b[l], w_out[l],
              ffn2_norm[l], ffn2_w_gate[l], ffn2_w_up[l], ffn2_w_down[l])
        xp, sp = hybrid_layer(xp, pos_p, None, None, None, C0p, n0p, m0p, buf0p, lw, l, True)
        past_k = cache_k[l][page_table].reshape(bs, past_len, NH_D, DK_D)
        past_v = cache_v[l][page_table].reshape(bs, past_len, NH_D, DV_D)
        xs, ss = hybrid_layer(xs, pos_s, past_k, past_v, past_pos, state_C[l], state_n[l], state_m[l],
                              state_conv[l], lw, l, False)
        st_p.append(sp)
        st_s.append(ss)
    y_prompt = rmsnorm(xp[:, N_META:], final_norm)
    y_sample = rmsnorm(xs, final_norm)
    k_p, v_p, C_p, n_p, m_p, conv_p = [jnp.stack(a) for a in zip(*st_p)]
    k_s, v_s, C_s, n_s, m_s, conv_s = [jnp.stack(a) for a in zip(*st_s)]
    return (y_prompt, y_sample, k_p, v_p, C_p, n_p, m_p, conv_p, k_s, v_s, C_s, n_s, m_s, conv_s)


_drawn_inputs = setup_inputs


def setup_inputs(seed=0):
    import zlib

    import numpy as np

    out = dict(_drawn_inputs(seed))
    spreads = {}
    factors = {'ffn1_norm': 3.945,
     'b_igate': 3.548,
     'mlstm_norm': 8.0,
     'lambda_q1': 8.0,
     'lambda_k1': 8.0,
     'subln': 7.397,
     'ffn2_norm': 7.588,
     'final_norm': 2.669}
    for name, (base, spread) in spreads.items():
        noise = np.random.default_rng([zlib.crc32(name.encode()), seed]).standard_normal(out[name].shape)
        drawn = base * np.exp(spread * noise) if base else spread * noise
        out[name] = __import__('jax').numpy.asarray(drawn.astype(out[name].dtype))
    for name, factor in factors.items():
        out[name] = (out[name] * factor).astype(out[name].dtype)
    return out
```

```python
from contextlib import ExitStack

import numpy as np

import concourse.bass as bass
from concourse import mybir

D = 1024
SEQ, NMETA, NB, DSEQ = 512, 16, 8, 4
PAST, PAGE = 256, 128
DFF = 2816
HM, DHM = 4, 256
HD, DHD = 8, 64
ROT, THETA = 16, 500000.0
EPS = 1e-6
LAMBDA_INIT = 0.2
NP_ = SEQ + NMETA
NS = NB * DSEQ
T = NP_ + NS
H2 = T // 2
DT = D // 128
FT = DFF // 128
KD = FT // 2
N_POOL = NB * (PAST // PAGE) * 5 // 4
OFF_XM, OFF_OM, OFF_GATE = 0, D, 2 * D
OFF_QKV = 2 * D + 2 * HM
OFF_GA = OFF_QKV + 3 * D
OFF_GB = OFF_GA + D
SPLIT = 256
BLOCKS = [(0, 128), (128, 128), (256, 128), (384, 128), (512, 16), (NP_, NS)]
WOFF = [0, 528, 928, 1200, 1344, 1360]
EXT = 3 + NP_ + NB * 7
NEG = -1.0e30
G_FFN1, G_MIX, G_FFN2, G_FINAL, G_CW, G_CB, G_ML, G_SUB, G_N = 0, 8, 16, 24, 32, 64, 72, 80, 81
C_ID, C_CAUSAL, C_NEG, C_ROT = 0, 128, 256, 384
C_BLK = 512
C_BM = C_BLK + NS
C_SEL = C_BM + NB
C_WM = C_SEL + HM * 128
C_SA = C_WM + 60
C_M0 = C_SA + NS
C_M1 = C_M0 + 1
C_EPS = C_M1 + 1
C_N = C_EPS + 1
C_COS, C_SIN = C_N, C_N + T
C_ALL = C_SIN + T

OUTS = [((1, SEQ, D)), ((NB, DSEQ, D)), ((1, 1, NP_, HD, 128)), ((1, 1, NP_, HD, 128)),
        ((1, 1, HM, DHM, DHM)), ((1, 1, HM, DHM)), ((1, 1, HM)), ((1, 1, 3, D)),
        ((1, NB, DSEQ, HD, 128)), ((1, NB, DSEQ, HD, 128)), ((1, NB, HM, DHM, DHM)),
        ((1, NB, HM, DHM)), ((1, NB, HM)), ((1, NB, 3, D))]


def constants():
    c = np.zeros((128, C_ALL), np.float32)
    i = np.arange(128)
    c[:, C_ID:C_ID + 128] = np.eye(128)
    c[:, C_CAUSAL:C_CAUSAL + 128] = i[:, None] <= i[None, :]
    c[:, C_NEG:C_NEG + 128] = np.where(i[None, :] <= i[:, None], 0.0, NEG)
    half = ROT // 2
    for base in (0, 64):
        for j in range(half):
            c[base + j + half, C_ROT + base + j] = -1.0
            c[base + j, C_ROT + base + j + half] = 1.0
    pos = np.concatenate([np.arange(NP_), np.tile(PAST + np.arange(DSEQ), NB)]).astype(np.float32)
    freq = (np.float32(THETA) ** (-np.arange(half, dtype=np.float32) / np.float32(half))).astype(np.float32)
    ang = pos[None, :] * freq[:, None]
    c[:, C_COS:C_COS + T] = 1.0
    for base in (0, 64):
        for o in (0, half):
            c[base + o:base + o + half, C_COS:C_COS + T] = np.cos(ang)
            c[base + o:base + o + half, C_SIN:C_SIN + T] = np.sin(ang)
    s = np.arange(NS)
    c[0:NS, C_BLK:C_BLK + NS] = (s[:, None] // DSEQ == s[None, :] // DSEQ) & (s[:, None] <= s[None, :])
    c[0:NS, C_BM:C_BM + NB] = s[:, None] // DSEQ == np.arange(NB)[None, :]
    for h in range(HM):
        c[h, C_SEL + 128 * h:C_SEL + 128 * (h + 1)] = 1.0
    r = np.arange(64)
    w = np.full((64, 60), NEG)
    for k in range(DSEQ):
        w[:, 28 + k] = np.where(k <= r % DSEQ, 0.0, NEG)
    c[0:64, C_WM:C_WM + 60] = w
    c[r, C_SA + (r // 8) * DSEQ + r % DSEQ] = 1.0
    c[0:64, C_M0] = (r // DSEQ) % 2 == 0
    c[0:64, C_M1] = (r // DSEQ) % 2 == 1
    c[:, C_EPS] = EPS
    return c


def build(nc, ins, outs, const_ap):
    f32, f32r, i32 = mybir.dt.float32, mybir.dt.float32r, mybir.dt.int32
    ACT = mybir.ActivationFunctionType
    ALU = mybir.AluOpType
    AX = mybir.AxisListType
    (y_prompt, y_sample, k_prompt, v_prompt, C_prompt, n_prompt, m_prompt, conv_prompt,
     k_sample, v_sample, C_sample, n_sample, m_sample, conv_sample) = outs

    ctx = ExitStack()
    with ctx:
        cursor = [16512]

        def at(name, shape, dt, offset=None):
            size = int(np.prod(shape[1:])) * 4
            if offset is None:
                offset = cursor[0]
                cursor[0] += (size + 31) // 32 * 32
            return nc.alloc_sbuf_tensor_at(name, shape, dt, offset=offset)

        X = at("X", [128, DT, T], f32)
        xn_hi = at("xn_hi", [128, DT, T], f32r)
        xn_lo = at("xn_lo", [128, DT, T], f32r)
        slots = cursor[0]
        raw = [at(f"raw{s}", [128, KD, 128], f32) for s in range(2)]
        w_hi = [at(f"w_hi{s}", [128, KD, 128], f32r) for s in range(2)]
        w_lo = [at(f"w_lo{s}", [128, KD, 128], f32r) for s in range(2)]
        slots_end = cursor[0]
        con = at("con", [128, C_N], f32)
        ones = at("ones", [128, 128], f32)
        gcol = at("gcol", [128, G_N], f32)
        tA = at("tA", [128, T], f32)
        tB = at("tB", [128, T], f32)
        rstd = at("rstd", [128, T], f32)
        small = at("small", [128, 64], f32)
        R = cursor[0]
        mlw = at("mlw", [128, 3, 2 * HM, DHM], f32, slots)
        kpage = at("kpage", [128, 2, 2, D], f32, slots)
        vpage = at("vpage", [128, 2, D], f32, slots + 16384)
        kout = at("kout", [128, 2, D], f32, slots)
        h_hi = at("h_hi", [128, FT, T], f32r, R)
        h_lo = at("h_lo", [128, FT, T], f32r, R + FT * T * 4)
        xtok = at("xtok", [112, 5, D], f32, R)
        vecs = at("vecs", [G_N, 128], f32, R + 5 * D * 4)
        lrow = at("lrow", [1, 4, DHD], f32, R + 5 * D * 4 + 512)
        lprod = at("lprod", [1, 4 * DHD], f32, R + 5 * D * 4 + 512 + 1024)
        TB4 = DT * T * 4
        RQ = R + EXT * DT * 4 + TB4
        E = at("E", [128, DT, EXT], f32, R)
        cc = at("cc", [128, DT, T], f32, R + EXT * DT * 4)
        qm = at("qm", [128, DT, T], f32, RQ)
        km = at("km", [128, DT, T], f32, RQ + TB4)
        RV = RQ + 2 * TB4
        vtok = at("vtok", [128, 6, D], f32, RV)
        RW = RV + 6 * D * 4
        rows = at("rows", [HM, 5, T], f32, RW)
        ktok = at("ktok", [128, 6, D], f32, R)
        P6 = at("P6", [128, 1392], f32, R + 6 * D * 4)
        tC = at("tC", [128, 2, T], f32, R + 6 * D * 4 + 5568)
        small2 = at("small2", [128, 512], f32, RW + 5 * T * 4)
        page_sb = at("page_sb", [1, 16], i32, RW + 5 * T * 4 + 2048)
        REND = 229344
        gw = at("gw", [128, DT, 36], f32, RQ)
        gw_hi = at("gw_hi", [128, DT, 36], f32r, RQ + 1152)
        gw_lo = at("gw_lo", [128, DT, 36], f32r, RQ + 2304)
        sconv = at("sconv", [24, D], f32, RQ + 4096)
        cvt = at("cvt", [128, DT, 27], f32, slots + 24576)
        cvo = at("cvo", [27, D], f32, slots + 24576 + 1024)
        xs = at("xs", [128, DT, NS], f32, slots + 24576 + 1024 + 4096)
        Cb = at("Cb", [128, 4, 2, DHM], f32, slots)
        CT = at("CT", [128, 2, 2, DHM], f32, slots + 8192)
        kwb = at("kwb", [128, NB, DHM], f32, slots + 12288)
        nst = at("nst", [NB, HM, DHM], f32, slots + 20480)
        nrow = at("nrow", [NS, DHM], f32, slots + 24576)
        cpo = at("cpo", [128, 2, DHM], f32, slots + 25600)
        npo = at("npo", [1, D], f32, slots + 27648)
        assert slots + 27648 + 4096 <= slots_end
        hm_hi = at("hm_hi", [128, DT, T], f32r, R)
        hm_lo = at("hm_lo", [128, DT, T], f32r, R + TB4)
        M = at("M", [128, DT, T], f32, RQ + TB4)
        qkv = at("qkv", [128, 3 * DT, T], f32, R)
        assert R + 3 * TB4 <= RQ + TB4
        Pat = [at(f"Pat{i}", [128, 2, NP_], f32, R + 2 * TB4 + 2 * NP_ * 4 * i if i < 2 else slots + 24576)
               for i in range(3)]
        qz = at("qz", [128, 2, 2, T], f32, R + 2 * TB4 + 4 * NP_ * 4)
        assert (4 * NP_ + 4 * T) * 4 <= TB4
        Qbd = at("Qbd", [128, NB, HD, 64], f32, R + 2 * TB4)
        trig = at("trig", [128, 2, T], f32, RW)
        AT = at("AT", [128, 5, NP_], f32, RW)
        AT3 = at("AT3", [128, 2, 3, NS], f32, RW)
        Psm = at("Psm", [64, 2, PAST + NS], f32, RW + 1024)
        KT4 = 4 * (PAST + NS) * 4
        KT = [[at(f"KT{b}{i}", [128, 4, PAST + NS], f32, o) for i, o in enumerate(where)] for b, where in
              enumerate(((slots + 24576, slots + 24576 + KT4), (R - 256 - 3 * T * 4, RW + 3328)))]
        assert slots + 24576 + 2 * KT4 <= slots_end and KT4 <= 3 * T * 4 and 3328 + KT4 <= 5 * T * 4
        o_hi = at("o_hi", [128, DT, T], f32r, R + TB4)
        o_lo = at("o_lo", [128, DT, T], f32r, R + 2 * TB4)
        m_hi = at("m_hi", [128, DT, T], f32r, R)
        m_lo = at("m_lo", [128, DT, T], f32r, RV)
        assert RW + 5 * T * 4 + 2048 + 64 <= REND, (RW + 5 * T * 4 + 2112, REND)
        assert R + 2 * FT * T * 4 <= REND

        ps = ctx.enter_context(nc.psum_tensor("ps", [128, 8, 512], f32))

        neglam = small[:, 0:1]
        mv = small[0:64, 1:2]
        bgate = small[0:HM, 2:4]
        lam2 = small[0:1, 4:7]
        m0row = small[0:HM, 8:16]
        mout = small[0:HM, 16:25]
        gsub = small[:, 25:26]
        rowmax = small[:, 26:34]
        rowsum = small[:, 34:42]
        rinv = small[:, 42:50]
        srm = small[0:64, 50:56]
        acol = small2[:, 0:48].rearrange("p (k w h) -> p k w h", k=6, w=2)
        wrow = small2[0:HM, 48:80]
        wlast = wrow.rearrange("p (b t) -> p b t", t=DSEQ)[:, :, DSEQ - 1]
        wbc = small2[:, 80:208].rearrange("p (h s) -> p h s", h=HM)
        dec8 = small2[0:NB, 208:212]
        nT = small2[:, 244:308].rearrange("p (k s) -> p k s", k=2)
        qs = at("qs", [128, DT, NS], f32, slots + 31744)
        nqs = tB[:, 0:256].rearrange("p (i s) -> p i s", i=DT)
        inter = tB[:, 256:512].rearrange("p (i s) -> p i s", i=DT)
        assert slots + 31744 + 1024 <= slots_end

        ident = con[:, C_ID:C_ID + 128]

        def sem(name):
            return ctx.enter_context(nc.semaphore(name))

        pe_stage, act_stage, dve_stage = sem("pe_stage"), sem("act_stage"), sem("dve_stage")
        loaded = [sem(f"loaded{s}") for s in range(2)]
        hi_done = [sem(f"hi_done{s}") for s in range(2)]
        lo_done = [sem(f"lo_done{s}") for s in range(2)]
        mm_done = [sem(f"mm_done{s}") for s in range(2)]
        ring_full, ring_act, ring_dve = sem("ring_full"), sem("ring_act"), sem("ring_dve")
        evac = [sem(f"evac{s}") for s in range(2)]
        tile_hi, tile_lo, om_prod = sem("tile_hi"), sem("tile_lo"), sem("om_prod")
        act_step, dve_step = sem("act_step"), sem("dve_step")

        def panel(w, row0, nk, col):
            return w[row0:row0 + 128 * nk, bass.ds(col, 128)].rearrange("(k p) n -> p k n", p=128)

        win = ins["w_in"][0]

        in_c = sem("in_c")

        class Phase:
            def __init__(self, name, n, nk, w, width, col=(0, 0), row=(0, 0)):
                self.n, self.nk, self.w, self.width, self.col, self.row = n, nk, w, width, col, row

        def feed_forward(tag):
            wg, wu, wd = (ins[f"ffn{tag}_{x}"][0] for x in ("w_gate", "w_up", "w_down"))
            return (Phase(f"up{tag}", FT, DT, (wg, wu), 128),
                    Phase(f"down{tag}", DT, KD, (wd, wd), 128, row=(0, KD * 128)))

        def two_tiles(name, n, w, off):
            return Phase(name, n, DT, (w, w), 256, (off, off + 128))

        up1, down1 = feed_forward(1)
        up2, down2 = feed_forward(2)
        p_xm = two_tiles("xm", DT // 2, win, OFF_XM)
        p_om = two_tiles("om", DT // 2, win, OFF_OM)
        p_qkv = two_tiles("qkv", 3 * DT // 2, win, OFF_QKV)
        p_wo = two_tiles("wo", DT // 2, ins["w_out"][0], 0)
        p_a = Phase("pa", DT, DT, (win, ins["w_proj_a"][0]), 128, (OFF_GA, 0))
        p_b = Phase("pb", DT, DT, (win, ins["w_proj_b"][0]), 128, (OFF_GB, 0))
        order = [up1, down1, p_xm, p_om, p_a, p_qkv, p_b, p_wo, up2, down2]
        panels = evs = los = 1
        his = 0
        for i, p in enumerate(order):
            p.before, panels = panels, panels + p.n
            p.ev0, evs = evs, evs + (p.n // 2 if p in (down1, down2) else p.n)
            p.lo0, los = los, los + {up1: 1, up2: 1, p_om: 2, p_b: 2}.get(p, 0) * p.n
            p.hi0, his = his, his + (p.n if p in (up1, up2, p_b) else 0)
            p.next = order[i + 1] if i + 1 < len(order) else None
        def late(p):
            return p in (p_om, p_b)

        def load(sp, p, j, s):
            col = j * p.width + p.col[s]
            if not isinstance(j, int):
                col = sp.snap(col)
            sp.wait_ge(lo_done[s], j + p.before)
            sp.dma_start(raw[s][:, 0:p.nk, :], panel(p.w[s], p.row[s], p.nk, col)).then_inc(loaded[s], 16)

        def split_hi(act, p, j, s):
            act.wait_ge(loaded[s], (j + p.before) * 16)
            act.wait_ge(mm_done[s], j + p.before)
            act.activation(w_hi[s][:, 0:p.nk, :], raw[s][:, 0:p.nk, :], ACT.Copy).then_inc(hi_done[s], 1)

        def split_lo(v, p, j, s):
            v.wait_ge(hi_done[s], j + p.before)
            v.tensor_tensor(w_lo[s][:, 0:p.nk, :], raw[s][:, 0:p.nk, :],
                            w_hi[s][:, 0:p.nk, :].bitcast(f32), ALU.subtract).then_inc(lo_done[s], 1)

        def product(pe, p, j, s, bank, x_hi, x_lo, k0=0, first=True, last=True):
            pe.wait_ge(lo_done[s], j + (p.before + 1))
            for half in range(2):
                cols = slice(half * H2, (half + 1) * H2)
                for k in range(p.nk):
                    for a, (w, x) in enumerate(((w_hi, x_hi), (w_hi, x_lo), (w_lo, x_hi))):
                        mm = pe.matmul(ps[:, bank + half, 0:H2], w[s][:, k, :], x[:, k0 + k, cols],
                                       start=first and k == 0 and a == 0,
                                       stop=last and k == p.nk - 1 and a == 2)
            mm.then_inc(mm_done[s], 1)

        def two(bank):
            return ps[:, bank:bank + 2, 0:H2]

        def tok(t):
            return t.rearrange("p (b n) -> p b n", b=2)

        def dyn(t, j):
            return t[:, bass.ds(j, 1), :].rearrange("p o (b n) -> p (o b) n", b=2)

        def loop(eng, p, body, step=1):
            n = p.n // step
            with eng.Fori(0, n - 1) as j:
                body(j, p, j + 1)
            body(n - 1, *((p.next, 0) if p.next is not None and not late(p.next) else (None, 0)))

        STAGES = ["load", "norm1", "up1", "down1", "norm2", "xm", "project", "states", "heads", "om",
                  "a_qkv", "rotary", "attend", "sample", "subln", "b", "out", "norm3", "up2", "down2", "last"]

        def begin(eng, name):
            for s in (pe_stage, act_stage, dve_stage):
                eng.wait_ge(s, STAGES.index(name))

        def end(eng, s):
            eng.drain().then_inc(s, 1)

        RING = {
            "load": ["a" if i % 2 else "d" for i in range(DT)] + ["d"],
            "project": (["d"] + ["a"] * 6 + ["a"] + ["d"]
                        + ["a", "a"] * DT + ["d"] * 6),
            "states": ["a"],
            "rotary": ["d"] * 16 + ["a", "d"] * 6,
            "sample": ["a", "d", "a", "d", "a"] + ["a", "d", "a", "d", "a", "d", "d"] * (NB - 1) + ["d", "d"],
            "subln": ["a"] * HD,
            "last": ["a", "d", "a", "d", "a"],
        }
        jobs, first_job = [], {}
        for key, who in RING.items():
            first_job[key] = len(jobs)
            jobs += who

        def ring_bank(n):
            return 2 * (n % 4)

        def score_job(b):
            return first_job["sample"] + (7 * b - 2 if b else 0)

        def value_job(b):
            return first_job["sample"] + (7 * b + 10 if b < NB - 1 else 7 * NB - 2)

        def v_pages(b):
            return kpage[:, NB % 2, :, :] if b == NB - 1 else vpage

        def ring_done(eng, n):
            eng.wait_ge(ring_act if jobs[n] == "a" else ring_dve, jobs[:n + 1].count(jobs[n]))

        def ring_free(pe, n):
            if n >= 4:
                ring_done(pe, n - 4)

        def ring_wait(eng, n):
            eng.wait_ge(ring_full, n + 1)
            return ring_bank(n)

        def wide(bank, rows_, cols):
            return ps[0:rows_, bank:bank + 2, :].rearrange("p b n -> p (b n)")[:, 0:cols]

        in_x, in_small = sem("in_x"), sem("in_small")
        in_g, in_mlw, in_page, in_sc = sem("in_g"), sem("in_mlw"), sem("in_page"), sem("in_sc")
        in_state = [sem(f"in_state{i}") for i in range(4)]
        in_k = [sem(f"in_k{i}") for i in range(2)]
        in_v = [sem(x) for x in ("in_v", "in_v_last")]
        in_n, in_trig = sem("in_n"), sem("in_trig")
        stored = sem("stored")
        st_state = [sem(f"st_state{i}") for i in range(4)]
        st_k = [sem(f"st_k{i}") for i in range(2)]
        st_c = sem("st_c")
        ones_ready, lam_row, lam_exp, lam_neg = sem("ones_ready"), sem("lam_row"), sem("lam_exp"), sem("lam_neg")
        sq_ready, sq_used, rstd_ready = sem("sq_ready"), sem("sq_used"), sem("rstd_ready")
        xt_ready, xhi_ready, xlo_done = sem("xt_ready"), sem("xhi_ready"), sem("xlo_done")
        gw_zero, ghi, glo, gates_full, gates_read = (sem("gw_zero"), sem("ghi"), sem("glo"), sem("gates_full"),
                                                     sem("gates_read"))
        xs_ready, cvt_ready, conv_ready, c_ready = sem("xs_ready"), sem("cvt_ready"), sem("conv_ready"), sem("c_ready")
        row_arg, row_fun, m_ready = sem("row_arg"), sem("row_fun"), sem("m_ready")
        qs_ready, kwb_ready = sem("qs_ready"), sem("kwb_ready")
        ct_full, ct_ready, cu_full, c_new, iq_full = sem("ct_full"), sem("ct_ready"), sem("cu_full"), sem("c_new"), sem("iq_full")
        nn_full, n_new, nf_full, n_fin, cf_full, c_fin = (sem("nn_full"), sem("n_new"), sem("nf_full"), sem("n_fin"),
                                                          sem("cf_full"), sem("c_fin"))
        bc_full, bc_ready, wt_ready, we_ready = sem("bc_full"), sem("bc_ready"), sem("wt_ready"), sem("we_ready")
        sc_full, p_ready, num_full, sqh_ready = sem("sc_full"), sem("p_ready"), sem("num_full"), sem("sqh_ready")
        ssh_full, u_ready, ln_ready, fac_ready, hm_ready = (sem("ssh_full"), sem("u_ready"), sem("ln_ready"),
                                                            sem("fac_ready"), sem("hm_ready"))
        rot_ready, qz_ready, s_full, max_ready, e_ready = (sem("rot_ready"), sem("qz_ready"), sem("s_full"),
                                                           sem("max_ready"), sem("e_ready"))
        a_ready, at_full, at_ready, o_full, o_ready = (sem("a_ready"), sem("at_full"), sem("at_ready"),
                                                       sem("o_full"), sem("o_ready"))
        qbd_ready, smax_ready, sp_ready = sem("qbd_ready"), sem("smax_ready"), sem("sp_ready")
        osq_ready, ofac_ready, on_ready, ohi_ready = sem("osq_ready"), sem("ofac_ready"), sem("on_ready"), sem("ohi_ready")
        t2 = [tA, tB]
        pairs = [(h, b) for h in range(HM) for b in range(NB)]
        block = ctx.enter_context(nc.Block())

        @block.sync
        def _(sp):
            xp = ins["x_prompt"][0]
            sp.dma_start(con[:, :], const_ap[:, 0:C_N]).then_inc(in_c, 16)
            sp.dma_start(xtok[0:16, 0, :], ins["meta_tokens"]).then_inc(in_x, 16)
            sp.dma_start(xtok[16:112, 0, :], xp[0:96, :]).then_inc(in_x, 16)
            for t in range(1, 4):
                sp.dma_start(xtok[:, t, :], xp[112 * t - 16:112 * t + 96, :]).then_inc(in_x, 16)
            sp.dma_start(xtok[0:80, 4, :], xp[432:512, :]).then_inc(in_x, 16)
            sp.dma_start(xtok[80:112, 4, :], ins["x_sample"].rearrange("b t d -> (b t) d")).then_inc(in_x, 16)
            for col, a in ((G_FFN1, ins["ffn1_norm"][0]), (G_MIX, ins["mix_norm"][0]),
                           (G_FFN2, ins["ffn2_norm"][0]), (G_FINAL, ins["final_norm"]),
                           (G_CB, ins["conv_b"][0])):
                sp.dma_start(vecs[col:col + 8, :], a.rearrange("(i p) -> i p", p=128)).then_inc(in_small, 16)
            sp.dma_start(vecs[G_CW:G_CW + 32, :],
                         ins["conv_w"][0].rearrange("j (i p) -> (j i) p", p=128)).then_inc(in_small, 16)
            sp.dma_start(vecs[G_ML:G_ML + 8, :],
                         ins["mlstm_norm"][0].rearrange("h (i p) -> (h i) p", p=128)).then_inc(in_small, 16)
            sp.dma_start(vecs[G_SUB:G_SUB + 1, :], ins["subln"]).then_inc(in_small, 16)
            for i, name in enumerate(("lambda_q1", "lambda_k1", "lambda_q2", "lambda_k2")):
                sp.dma_start(lrow[0:1, i, :], ins[name]).then_inc(in_small, 16)
            with nc.allow_non_contiguous_dma(reason="a few words"):
                sp.dma_start(bgate[:, 0:1], ins["b_igate"].rearrange("a h -> h a")).then_inc(in_small, 16)
                sp.dma_start(bgate[:, 1:2], ins["b_fgate"].rearrange("a h -> h a")).then_inc(in_small, 16)
                sp.dma_start(m0row, ins["state_m"][0].rearrange("b h -> h b")).then_inc(in_small, 16)

            def stream(p, first=0):
                with sp.Fori(first, p.n) as j:
                    load(sp, p, j, 0)
                    load(sp, p, j, 1)

            def stream_short(p):
                for j in range(p.n):
                    load(sp, p, j, 0)
                    load(sp, p, j, 1)

            stream(up1)
            stream(down1)
            load(sp, p_xm, 0, 0)
            load(sp, p_xm, 0, 1)
            begin(sp, "norm2")
            sp.wait_ge(gw_zero, 1)
            for c, o in ((0, OFF_GATE), (32, OFF_GATE + HM)):
                sp.dma_start(gw[:, :, c:c + HM],
                             win[:, o:o + HM].rearrange("(k p) n -> p k n", p=128)).then_inc(in_g, 16)
            stream(p_xm, 1)
            sp.dma_start(sconv[:, :], ins["state_conv"][0].rearrange("b j d -> (b j) d")).then_inc(in_sc, 16)
            sp.dma_start(page_sb[0:1, :], ins["page_table"].rearrange("b g -> (b g)").unsqueeze(0)).then_inc(in_page, 16)
            begin(sp, "project")
            for i, name in enumerate(("w_mv", "w_mq", "w_mk")):
                sp.dma_start(mlw[:, i, :, :], ins[name][0].rearrange("h (k p) n -> p (h k) n", p=128)).then_inc(in_mlw, 16)
            ring_done(sp, first_job["project"] + 7)
            sp.dma_start(conv_prompt[0, 0], cvo[0:3, :]).then_inc(stored, 16)
            sp.dma_start(conv_sample[0].rearrange("b j d -> (b j) d"), cvo[3:27, :]).then_inc(stored, 16)
            sp.wait_ge(m_ready, 1)
            with nc.allow_non_contiguous_dma(reason="a few words"):
                sp.dma_start(m_prompt[0].rearrange("a h -> h a"), mout[:, 0:1]).then_inc(stored, 16)
                sp.dma_start(m_sample[0].rearrange("b h -> h b"), mout[:, 1:9]).then_inc(stored, 16)
            begin(sp, "states")
            sp.wait_ge(stored, 64)
            sp.dma_start(nst[:, :, :], ins["state_n"][0]).then_inc(in_n, 16)
            sp.dma_start(nrow[:, :], ins["state_n"][0].rearrange("b h d -> (b h) d")).then_inc(in_n, 16)
            for n in range(len(pairs) + 2):
                if n < len(pairs):
                    h, b = pairs[n]
                    if n >= 4:
                        sp.wait_ge(st_state[n % 4], 16 * (n // 4))
                    sp.dma_start(Cb[:, n % 4, :, :], ins["state_C"][0, b, h].rearrange("(v p) k -> p v k", p=128)
                                 ).then_inc(in_state[n % 4], 16)
                if n >= 2:
                    h, b = pairs[n - 2]
                    sp.wait_ge(c_new, n - 1)
                    sp.dma_start(C_sample[0, b, h].rearrange("(v p) k -> p v k", p=128),
                                 Cb[:, (n - 2) % 4, :, :]).then_inc(st_state[(n - 2) % 4], 16)
            sp.wait_ge(n_new, 1)
            sp.dma_start(n_sample[0], nst[:, :, :]).then_inc(stored, 16)
            for h in range(HM):
                sp.wait_ge(c_fin, h + 1)
                sp.dma_start(C_prompt[0, 0, h].rearrange("(v p) k -> p v k", p=128), cpo[:, :, :]).then_inc(st_c, 16)
            sp.wait_ge(n_fin, 1)
            sp.dma_start(n_prompt[0].rearrange("a h d -> a (h d)"), npo[:, :]).then_inc(stored, 16)
            for i in range(4):
                sp.wait_ge(st_state[i], 16 * len(pairs) // 4)
            sp.wait_ge(st_c, 16 * HM)
            sp.wait_ge(stored, 16 * 6)
            begin(sp, "heads")
            stream(p_om)
            stream_short(p_a)
            begin(sp, "om")
            sp.dma_start(trig[:, :, :], const_ap[:, C_COS:C_ALL].rearrange("p (c t) -> p c t", c=2)).then_inc(in_trig, 16)
            stream(p_qkv)
            for part in range(2):
                for i, (t0, n) in enumerate(BLOCKS):
                    ring_done(sp, first_job["rotary"] + 16 + 6 * part + i)
                    if part == 0:
                        dst = v_prompt[0, 0, t0:t0 + n] if i < 5 else v_sample[0].rearrange("b t h d -> (b t) h d")
                        sp.dma_start(dst.rearrange("t h d -> t (h d)"), vtok[0:n, i, :]).then_inc(stored, 16)
                    else:
                        dst = k_prompt[0, 0, t0:t0 + n] if i < 5 else k_sample[0].rearrange("b t h d -> (b t) h d")
                        sp.dma_start(dst.rearrange("t h d -> t (h d)"), kout[0:n, i % 2, :]).then_inc(st_k[i % 2], 16)
            sp.wait_ge(st_k[0], 48)
            sp.wait_ge(st_k[1], 48)
            begin(sp, "attend")
            sp.wait_ge(in_page, 16)

            def page(b, g):
                return bass.ds(sp.value_load(page_sb[0:1, 2 * b + g:2 * b + g + 1], min_val=0, max_val=N_POOL - 1), 1)

            def load_k(b):
                if b >= 2:
                    sp.wait_ge(ring_full, score_job(b - 2) + 4)
                for g in range(2):
                    sp.dma_start(kpage[:, b % 2, g, :], ins["cache_k"][0][page(b, g)]
                                 .rearrange("o t h d -> (o t) (h d)")).then_inc(in_k[b % 2], 16)

            def load_v(b):
                if b == NB - 1:
                    sp.wait_ge(ring_full, score_job(b - 1) + 4)
                elif b >= 1:
                    sp.wait_ge(ring_full, value_job(b - 1) + 2)
                for g in range(2):
                    sp.dma_start(v_pages(b)[:, g, :], ins["cache_v"][0][page(b, g)]
                                 .rearrange("o t h d -> (o t) (h d)")).then_inc(in_v[b == NB - 1], 16)
            load_k(0)
            load_k(1)
            load_v(0)
            load_k(2)
            for b in range(1, NB):
                if b + 2 < NB:
                    load_k(b + 2)
                load_v(b)
            begin(sp, "subln")
            stream_short(p_b)
            stream(p_wo)
            stream(up2)
            stream(down2)
            for t in range(5):
                ring_done(sp, first_job["last"] + t)
                if t == 0:
                    sp.dma_start(y_prompt[0, 0:96, :], xtok[16:112, 0, :]).then_inc(stored, 16)
                elif t < 4:
                    sp.dma_start(y_prompt[0, 112 * t - 16:112 * t + 96, :], xtok[:, t, :]).then_inc(stored, 16)
                else:
                    sp.dma_start(y_prompt[0, 432:512, :], xtok[0:80, 4, :]).then_inc(stored, 16)
                    sp.dma_start(y_sample.rearrange("b t d -> (b t) d"), xtok[80:112, 4, :]).then_inc(stored, 16)
            sp.wait_ge(stored, 16 * (6 + 6 + 6))

        @block.tensor
        def _(pe):
            def transpose(out, in_, k):
                return pe.transpose(out, in_, con[0:k, C_ID:C_ID + k])

            def transpose8(n, in_of, nt, k=128):
                for i in range(DT):
                    mm = transpose(ps[0:nt, ring_bank(n) + i // 4, 128 * (i % 4):128 * (i % 4) + 128], in_of(i), k)
                mm.then_inc(ring_full, 1)

            def norm(r):
                for i in range(DT):
                    pe.wait_ge(sq_ready, DT * r + i + 1)
                    for half in range(2):
                        mm = pe.matmul(ps[:, 4 + half, 0:H2], ones[:, :], t2[i % 2][:, half * H2:(half + 1) * H2],
                                       start=i == 0, stop=i == DT - 1)
                    mm.then_inc(sq_used, 1)

            def up(p):
                def body(j, _q, _jn):
                    pe.wait_ge(evac[0], j + p.ev0)
                    product(pe, p, j, 0, 0, xn_hi, xn_lo)
                    pe.wait_ge(evac[1], j + p.ev0)
                    product(pe, p, j, 1, 2, xn_hi, xn_lo)
                loop(pe, p, body)

            def down(p):
                def body(j, _q, _jn):
                    for e in range(2):
                        pe.wait_ge(evac[e], j + p.ev0)
                        product(pe, p, j * 2 + e, 0, 2 * e, h_hi, h_lo, 0, True, False)
                        product(pe, p, j * 2 + e, 1, 2 * e, h_hi, h_lo, KD, False, True)
                loop(pe, p, body, 2)

            def pair(p, xs_):
                def body(j, _q, _jn):
                    for s in range(2):
                        pe.wait_ge(evac[s], j + p.ev0)
                        product(pe, p, j, s, 2 * s, *xs_[s])
                loop(pe, p, body)

            xn = (xn_hi, xn_lo)

            for s in range(2):
                pe.drain().then_inc(mm_done[s], 1)
            pe.wait_ge(in_c, 16)
            pe.wait_ge(in_x, 16 * 7)
            for i in range(DT):
                ring_free(pe, i)
                for t in range(5):
                    mm = transpose(ps[:, ring_bank(i) + t // 4, 112 * (t % 4):112 * (t % 4) + 112],
                                   xtok[:, t, 128 * i:128 * i + 128], 112)
                mm.then_inc(ring_full, 1)
            ring_free(pe, DT)
            pe.wait_ge(in_small, 16 * 15)
            transpose(ps[:, ring_bank(DT), 0:G_N], vecs[:, :], G_N)
            pe.wait_ge(ones_ready, 1)
            pe.wait_ge(lam_neg, 1)
            pe.matmul(ps[:, ring_bank(DT) + 1, 0:1], ones[0:1, :], lam2[:, 2:3], start=True, stop=True).then_inc(ring_full, 1)
            end(pe, pe_stage)

            begin(pe, "norm1")
            norm(0)
            end(pe, pe_stage)
            begin(pe, "up1")
            up(up1)
            end(pe, pe_stage)
            begin(pe, "down1")
            down(down1)
            end(pe, pe_stage)
            begin(pe, "norm2")
            norm(1)
            end(pe, pe_stage)

            begin(pe, "xm")
            pair(p_xm, (xn, xn))
            pe.wait_ge(glo, 1)
            for half in range(2):
                cols = slice(half * H2, (half + 1) * H2)
                for k in range(DT):
                    for a, (w, x) in enumerate(((gw_hi, xn_hi), (gw_hi, xn_lo), (gw_lo, xn_hi))):
                        mm = pe.matmul(ps[0:36, 4 + half, 0:H2], w[:, k, :], x[:, k, cols],
                                       start=k == 0 and a == 0, stop=k == DT - 1 and a == 2)
            mm.then_inc(gates_full, 1)
            end(pe, pe_stage)

            begin(pe, "project")
            n = first_job["project"]
            ring_free(pe, n)
            pe.wait_ge(in_sc, 16)
            pe.wait_ge(gates_read, 2)
            for i in range(DT):
                mm = transpose(ps[:, ring_bank(n), 24 * i:24 * i + 24], sconv[:, 128 * i:128 * i + 128], 24)
            mm.then_inc(ring_full, 1)
            n += 1
            pe.wait_ge(in_mlw, 48)
            for blk, (t0, nt) in enumerate(BLOCKS):
                ring_free(pe, n)
                if blk == 5:
                    pe.wait_ge(xs_ready, 1)
                for h in range(HM):
                    for k in range(2):
                        i = 2 * h + k
                        x = E[:, i, 3 + t0:3 + t0 + nt] if blk < 5 else xs[:, i, :]
                        mm = pe.matmul(ps[0:nt, ring_bank(n) + h // 2, DHM * (h % 2):DHM * (h % 2) + DHM],
                                       x, mlw[:, 0, i, :], start=k == 0, stop=k == 1)
                mm.then_inc(ring_full, 1)
                n += 1
            ring_free(pe, n)
            pe.wait_ge(cvt_ready, 1)
            transpose8(n, lambda i: cvt[:, i, :], 27)
            n += 1
            ring_free(pe, n)
            pe.wait_ge(row_fun, 4)
            for blk, (t0, nt) in enumerate(BLOCKS):
                for w, r in enumerate((1, 0)):
                    transpose(ps[0:nt, ring_bank(n), 8 * blk + 4 * w:8 * blk + 4 * w + 4], rows[:, r, t0:t0 + nt], HM)
            transpose(ps[0:NB, ring_bank(n), 64:68], wlast, HM)
            for h in range(HM):
                mm = pe.matmul(ps[:, ring_bank(n) + 1, 32 * h:32 * h + 32],
                               con[0:HM, C_SEL + 128 * h:C_SEL + 128 * h + 128], wrow, start=True, stop=True)
            mm.then_inc(ring_full, 1)
            n += 1
            for i in range(DT):
                h, m = i // 2, i % 2
                pe.wait_ge(c_ready, 2 * h + 2)
                for w in range(2):
                    ring_free(pe, n)
                    for half in range(2):
                        for k in range(2):
                            mm = pe.matmul(ps[:, ring_bank(n) + half, 0:H2],
                                           mlw[:, 1 + w, 2 * h + k, 128 * m:128 * m + 128],
                                           cc[:, 2 * h + k, half * H2:(half + 1) * H2], start=k == 0, stop=k == 1)
                    mm.then_inc(ring_full, 1)
                    n += 1
            ring_done(pe, n - 1)
            for blk, (t0, nt) in enumerate(BLOCKS):
                ring_free(pe, n)
                transpose8(n, lambda i: km[:, i, t0:t0 + nt], nt)
                n += 1
            end(pe, pe_stage)

            begin(pe, "states")
            pe.wait_ge(in_n, 32)
            for k in range(2):
                mm = transpose(ps[:, ring_bank(n), 32 * k:32 * k + 32], nrow[:, 128 * k:128 * k + 128], NS)
            mm.then_inc(ring_full, 1)
            ring_done(pe, n)
            pe.wait_ge(qs_ready, 1)

            def state_q(n):
                h, b = pairs[n]
                pe.wait_ge(ct_ready, n + 1)
                for vt in range(2):
                    for kt in range(2):
                        c0 = NS * (2 * h + vt) + DSEQ * b
                        mm = pe.matmul(ps[:, 6, c0:c0 + DSEQ], CT[:, n % 2, kt, 128 * vt:128 * vt + 128],
                                       qs[:, 2 * h + kt, DSEQ * b:DSEQ * b + DSEQ], start=kt == 0, stop=kt == 1)
                mm.then_inc(iq_full, 1)

            for n, (h, b) in enumerate(pairs):
                pe.wait_ge(in_state[n % 4], 16 * (n // 4 + 1))
                if n >= 2:
                    pe.wait_ge(ct_ready, n - 1)
                for vt in range(2):
                    for kt in range(2):
                        c0 = kt * DHM + vt * 128
                        mm = transpose(ps[:, n % 2, c0:c0 + 128], Cb[:, n % 4, vt, 128 * kt:128 * kt + 128], 128)
                mm.then_inc(ct_full, 1)
                if n >= 2:
                    pe.wait_ge(c_new, n - 1)
                if b == 0:
                    pe.wait_ge(kwb_ready, h + 1)
                for vt in range(2):
                    mm = pe.matmul(ps[:, 2 + n % 2, DHM * vt:DHM * vt + DHM],
                                   vtok[:, 5, DHM * h + 128 * vt:DHM * h + 128 * vt + 128],
                                   kwb[:, b, :], start=True, stop=True)
                mm.then_inc(cu_full, 1)
                if n >= 1:
                    state_q(n - 1)
            state_q(len(pairs) - 1)
            for half in range(2):
                mm = pe.matmul(ps[0:NB, 4 + half, :], con[0:NS, C_BM:C_BM + NB],
                               ktok[0:NS, 5, 512 * half:512 * half + 512], start=True, stop=True)
            mm.then_inc(nn_full, 1)
            for h in range(HM):
                if h >= 1:
                    pe.wait_ge(c_fin, h)
                for vt in range(2):
                    for blk in range(5):
                        nt = 128
                        mm = pe.matmul(ps[:, 7, DHM * vt:DHM * vt + DHM],
                                       vtok[0:nt, blk, DHM * h + 128 * vt:DHM * h + 128 * vt + 128],
                                       ktok[0:nt, blk, DHM * h:DHM * h + DHM], start=blk == 0, stop=blk == 4)
                mm.then_inc(cf_full, 1)
            pe.wait_ge(n_new, 1)
            for half in range(2):
                for blk in range(5):
                    nt = BLOCKS[blk][1]
                    mm = pe.matmul(ps[0:1, 4 + half, :], ones[0:nt, 0:1],
                                   ktok[0:nt, blk, 512 * half:512 * half + 512], start=blk == 0, stop=blk == 4)
            mm.then_inc(nf_full, 1)
            end(pe, pe_stage)

            begin(pe, "heads")
            for h in range(HM):
                if h >= 1:
                    pe.wait_ge(u_ready, h)
                for w in range(2):
                    if w == 1:
                        pe.wait_ge(bc_ready, 2 * h + 1)
                    for half in range(2):
                        mm = pe.matmul(ps[:, half, 0:H2], con[0:HM, C_SEL + 128 * h:C_SEL + 128 * h + 128],
                                       rows[:, 2 + w, half * H2:(half + 1) * H2], start=True, stop=True)
                    mm.then_inc(bc_full, 1)
                pe.wait_ge(bc_ready, 2 * h + 2)

                def score(out, blk, q0, nq):
                    t0, nt = BLOCKS[blk]
                    for k in range(2):
                        mm = pe.matmul(out, km[:, 2 * h + k, t0:t0 + nt], qm[:, 2 * h + k, q0:q0 + nq],
                                       start=k == 0, stop=k == 1)
                    return mm
                score(ps[:, 0, 0:SPLIT], 0, 0, SPLIT)
                score(ps[:, 1, 0:NP_ - SPLIT], 0, SPLIT, NP_ - SPLIT).then_inc(sc_full, 1)
                for blk in range(1, 6):
                    t0, nt = BLOCKS[blk]
                    nq = NP_ - t0 if blk < 5 else NS
                    pe.wait_ge(p_ready, 6 * h + max(blk - 1, 1))
                    score(ps[0:nt, (blk + 1) % 2, 0:nq], blk, t0, nq).then_inc(sc_full, 1)
                if h >= 1:
                    pe.wait_ge(hm_ready, h)
                for blk, (t0, nt) in enumerate(BLOCKS):
                    pe.wait_ge(p_ready, 6 * h + blk + 1)
                    for o in range(3):
                        w = vtok[0:nt, blk, DHM * h + 128 * o:DHM * h + 128 * o + 128] if o < 2 else ones[0:nt, :]
                        b = 2 + 2 * o
                        if blk == 5:
                            out = ps[:, b + 1, NP_ - SPLIT:T - SPLIT]
                            pe.matmul(out, w, P6[0:nt, WOFF[5]:WOFF[5] + NS], start=False, stop=True,
                                      skip_group_check=True)
                            if o < 2:
                                mm = pe.matmul(out, ident, inter[:, 2 * h + o, :], start=False, stop=True,
                                               skip_group_check=True)
                            else:
                                for k in range(2):
                                    mm = pe.matmul(out, ones[:, :], nqs[:, 2 * h + k, :], start=False, stop=k == 1,
                                                   skip_group_check=True)
                            continue
                        if t0 < SPLIT:
                            pe.matmul(ps[:, b, t0:SPLIT], w, P6[0:nt, WOFF[blk]:WOFF[blk] + SPLIT - t0],
                                      start=blk == 0, stop=True, skip_group_check=True)
                        q0 = max(t0, SPLIT)
                        pe.matmul(ps[:, b + 1, q0 - SPLIT:NP_ - SPLIT], w,
                                  P6[0:nt, WOFF[blk] + q0 - t0:WOFF[blk] + NP_ - t0],
                                  start=blk == 0, stop=True, skip_group_check=True)
                mm.then_inc(num_full, 1)
                for o in range(2):
                    pe.wait_ge(sqh_ready, 2 * h + o + 1)
                    for half in range(2):
                        mm = pe.matmul(ps[:, half, 0:H2], ones[:, :], tC[:, o, half * H2:(half + 1) * H2],
                                       start=o == 0, stop=o == 1, skip_group_check=True)
                mm.then_inc(ssh_full, 1)
            end(pe, pe_stage)

            begin(pe, "om")
            pair(p_om, (xn, xn))
            end(pe, pe_stage)
            begin(pe, "a_qkv")
            pair(p_a, (xn, (hm_hi, hm_lo)))
            for s in range(2):
                pe.wait_ge(evac[s], p_a.ev0 + p_a.n)
            pair(p_qkv, (xn, xn))
            end(pe, pe_stage)

            begin(pe, "rotary")
            n = first_job["rotary"]
            for i in range(2 * DT):
                ring_free(pe, n)
                for half in range(2):
                    mm = pe.matmul(ps[:, ring_bank(n) + half, 0:H2], con[:, C_ROT:C_ROT + 128],
                                   qkv[:, i, half * H2:(half + 1) * H2], start=True, stop=True)
                mm.then_inc(ring_full, 1)
                n += 1
            for part in (2, 1):
                if part == 1:
                    pe.wait_ge(rot_ready, 2 * DT)
                for blk, (t0, nt) in enumerate(BLOCKS):
                    ring_free(pe, n)
                    transpose8(n, lambda i: qkv[:, DT * part + i, t0:t0 + nt], nt)
                    n += 1
            end(pe, pe_stage)

            begin(pe, "attend")
            def scores(g):
                h, i = divmod(g, 5)
                q0, nq = BLOCKS[i]
                nk = q0 + nq
                pe.wait_ge(qz_ready, h + 1)
                if i < 2 and h >= 1:
                    pe.wait_ge(e_ready, 5 * h)
                elif i in (2, 3):
                    pe.wait_ge(e_ready, g - 1)
                elif i == 4:
                    pe.wait_ge(e_ready, g)
                for m in range(2):
                    q = qz[:, h % 2, m, q0:q0 + nq]
                    if i < 4:
                        out = ps[0:nq, 2 * (i % 2) + m, :]
                        pe.matmul(out[:, 0:nk], q, qkv[:, DT + h, 0:nk], start=True, stop=True)
                    else:
                        pe.matmul(ps[0:nq, 2 * m, 0:264], q, qkv[:, DT + h, 0:264], start=True, stop=True)
                        out = ps[0:nq, 2 * m + 1, :]
                        pe.matmul(out[:, 0:264], q, qkv[:, DT + h, 264:NP_], start=True, stop=True)
                    c0 = q0 if i < 4 else 248
                    mm = pe.matmul(out[:, c0:c0 + nq], con[0:nq, C_ID:C_ID + nq], con[0:nq, C_NEG:C_NEG + nq],
                                   start=False, stop=True, skip_group_check=True)
                mm.then_inc(s_full, 1)

            def transposed(g):
                h, i = divmod(g, 5)
                q0, nq = BLOCKS[i]
                pe.wait_ge(a_ready, g + 1)
                if g >= 2:
                    pe.wait_ge(at_ready, g - 1)
                for j in range(i + 1):
                    nk = BLOCKS[j][1]
                    mm = transpose(ps[0:nk, 4 + g % 2, nq * j:nq * j + nq],
                                   Pat[g % 3][0:nq, 0, 128 * j:128 * j + nk], nq)
                mm.then_inc(at_full, 1)

            def output(h):
                pe.wait_ge(at_ready, 5 * h + 5)
                if h >= 1:
                    pe.wait_ge(o_ready, h)
                for blk in range(5):
                    t0, nt = BLOCKS[blk]
                    w = vtok[0:nt, blk, 128 * h:128 * h + 128]
                    if t0 < SPLIT:
                        pe.matmul(ps[:, 6, t0:SPLIT], w, AT[0:nt, blk, t0:SPLIT], start=blk == 0, stop=True,
                                  skip_group_check=True)
                    q0 = max(t0, SPLIT)
                    mm = pe.matmul(ps[:, 7, q0 - SPLIT:NP_ - SPLIT], w, AT[0:nt, blk, q0:NP_],
                                   start=blk == 0, stop=True, skip_group_check=True)
                mm.then_inc(o_full, 1)

            G = 5 * HD
            for g in range(G + 3):
                early = g % 5 in (0, 4)
                if early and 2 <= g < G + 2:
                    transposed(g - 2)
                if g < G:
                    scores(g)
                if g >= 3 and (g - 3) % 5 == 4:
                    output((g - 3) // 5)
                if not early and 2 <= g < G + 2:
                    transposed(g - 2)
            end(pe, pe_stage)

            begin(pe, "sample")
            pe.wait_ge(qbd_ready, 1)

            def sample_scores(b):
                n = score_job(b)
                pe.wait_ge(in_k[b % 2], 32 * (b // 2 + 1))
                for g in range(2):
                    for q in range(2):
                        ring_free(pe, n)
                        for i in range(4):
                            hh = 4 * q + i
                            mm = transpose(ps[:, ring_bank(n), 128 * i:128 * i + 128],
                                           kpage[:, b % 2, g, 128 * hh:128 * hh + 128], 128)
                        mm.then_inc(ring_full, 1)
                        n += 1
                ring_done(pe, n - 2)
                ring_done(pe, n - 1)
                for hh in range(HD):
                    pe.matmul(ps[0:64, ring_bank(n), 0:PAST + NS], Qbd[:, b, hh, :], KT[b % 2][hh // 4][:, hh % 4, :],
                              start=hh == 0, stop=hh == HD - 1)
                pe.matmul(ps[0:64, ring_bank(n), PAST:PAST + NS], con[0:64, C_ID:C_ID + 64],
                          con[0:64, C_WM + 28 - 4 * b:C_WM + 60 - 4 * b], start=False, stop=True,
                          skip_group_check=True).then_inc(ring_full, 1)

            def sample_output(b):
                n = value_job(b)
                ring_free(pe, n)
                pe.wait_ge(sp_ready, b + 1)
                for g in range(3):
                    nk = 128 if g < 2 else NS
                    mm = pe.matmul(ps[0:nk, ring_bank(n), NS * g:NS * g + NS], Psm[:, b % 2, 128 * g:128 * g + nk],
                                   con[0:64, C_SA:C_SA + NS], start=True, stop=True)
                mm.then_inc(ring_full, 1)
                n += 1
                ring_free(pe, n)
                ring_done(pe, n - 1)
                pe.wait_ge(in_v[b == NB - 1], 32 * (b + 1 if b < NB - 1 else 1))
                for hh in range(HD):
                    for g in range(3):
                        nk = 128 if g < 2 else NS
                        w = v_pages(b)[:, g, 128 * hh:128 * hh + 128] if g < 2 else vtok[0:NS, 5, 128 * hh:128 * hh + 128]
                        mm = pe.matmul(ps[:, ring_bank(n), DSEQ * hh:DSEQ * hh + DSEQ], w,
                                       AT3[0:nk, b % 2, g, DSEQ * hh:DSEQ * hh + DSEQ], start=g == 0, stop=g == 2)
                mm.then_inc(ring_full, 1)

            for b in range(NB + 1):
                if b < NB:
                    sample_scores(b)
                if b >= 1:
                    sample_output(b - 1)
            end(pe, pe_stage)
            n = first_job["subln"]

            begin(pe, "subln")
            for h in range(HD):
                ring_free(pe, n)
                pe.wait_ge(osq_ready, h + 1)
                for half in range(2):
                    mm = pe.matmul(ps[:, ring_bank(n) + half, 0:H2], ones[:, :], t2[h % 2][:, half * H2:(half + 1) * H2],
                                   start=True, stop=True)
                mm.then_inc(ring_full, 1)
                n += 1
            end(pe, pe_stage)

            begin(pe, "b")
            pair(p_b, (xn, (o_hi, o_lo)))
            end(pe, pe_stage)
            begin(pe, "out")
            pair(p_wo, ((m_hi, m_lo), (m_hi, m_lo)))
            end(pe, pe_stage)
            begin(pe, "norm3")
            norm(2)
            end(pe, pe_stage)
            begin(pe, "up2")
            up(up2)
            end(pe, pe_stage)
            begin(pe, "down2")
            down(down2)
            end(pe, pe_stage)
            begin(pe, "last")
            norm(3)
            pe.wait_ge(xt_ready, 4 * DT)
            for t in range(5):
                ring_free(pe, n)
                transpose8(n, lambda i: X[:, i, 112 * t:112 * t + 112], 112)
                n += 1

        @block.scalar
        def _(act):
            def copy(out, in_, scale=1.0):
                return act.activation(out, in_, ACT.Copy, scale=scale)

            def prepare(p, j, s):
                if p is not None:
                    split_hi(act, p, j, s)

            def norm(r, final=False):
                for i in range(DT):
                    if i >= 2:
                        act.wait_ge(sq_used, DT * r + i - 1)
                    act.activation(t2[i % 2][:, :], X[:, i, :], ACT.Square).then_inc(sq_ready, 1)
                act.wait_ge(sq_used, DT * (r + 1))
                act.activation(tok(rstd[:, :]), two(4), ACT.Ln, bias=con[:, C_EPS:C_EPS + 1],
                               scale=1.0 / D).then_inc(rstd_ready, 1)
                act.wait_ge(rstd_ready, 2 * r + 1)
                act.activation(rstd[:, :], rstd[:, :], ACT.Exp, scale=-0.5).then_inc(rstd_ready, 1)
                if not final:
                    for i in range(DT):
                        act.wait_ge(xt_ready, DT * r + i + 1)
                        copy(xn_hi[:, i, :], t2[i % 2][:, :]).then_inc(xhi_ready, 1)

            def gated(p, func, to_hi):
                act.activation(small[0:1, 60:61], con[0:1, 0:1], func)

                def body(j, q, jn):
                    prepare(q, jn, 0)
                    act.wait_ge(mm_done[0], j + (p.before + 1))
                    act.wait_ge(evac[1], j + p.ev0)
                    act.activation(tok(tA[:, :]), two(0), func).then_inc(evac[0], 1)
                    prepare(q, jn, 1)
                    if to_hi is not None:
                        act.wait_ge(evac[1], j + (p.ev0 + 1))
                        copy(dyn(to_hi, j), tok(tB[:, :])).then_inc(tile_hi, 1)
                loop(act, p, body)

            def down(p):
                def body(j, q, jn):
                    for s in range(2):
                        split_hi(act, p, j * 2 + 1, s)
                    for s in range(2):
                        prepare(q, jn * 2, s)
                loop(act, p, body, 2)

            def plain(p, out=None):
                def body(j, q, jn):
                    prepare(q, jn, 0)
                    if out is not None:
                        act.wait_ge(mm_done[0], j + (p.before + 1))
                        out(j)
                    prepare(q, jn, 1)
                loop(act, p, body)

            def at_copy(h, i):
                q0, nq = BLOCKS[i]
                g = 5 * h + i
                act.wait_ge(at_full, g + 1)
                if i == 0 and h >= 1:
                    act.wait_ge(o_full, h)
                src = ps[:, 4 + g % 2, :]
                nj = min(i + 1, 4)
                c = copy(AT[:, 0:nj, q0:q0 + nq], src[:, 0:nq * nj].rearrange("p (j q) -> p j q", q=nq))
                if i == 4:
                    c = copy(AT[0:nq, 4, q0:q0 + nq], src[0:nq, 4 * nq:5 * nq])
                c.then_inc(at_ready, 1)

            for i in range(DT):
                if jobs[i] == "a":
                    b = ring_wait(act, i)
                    copy(X[:, i, 0:448], ps[:, b, 0:448])
                    copy(X[:, i, 448:560], ps[:, b + 1, 0:112]).then_inc(ring_act, 1)
            act.wait_ge(lam_row, 1)
            act.activation(lam2[:, 0:2], lam2[:, 0:2], ACT.Exp).then_inc(lam_exp, 1)
            end(act, act_stage)
            begin(act, "norm1")
            norm(0)
            for s in range(2):
                split_hi(act, up1, 0, s)
            end(act, act_stage)
            begin(act, "up1")
            gated(up1, ACT.Silu, h_hi)
            end(act, act_stage)
            begin(act, "down1")
            down(down1)
            end(act, act_stage)
            begin(act, "norm2")
            norm(1)
            act.wait_ge(in_g, 32)
            copy(gw_hi[:, :, :], gw[:, :, :]).then_inc(ghi, 1)
            end(act, act_stage)

            begin(act, "xm")

            def xm_out(j):
                e = E[:, bass.ds(j * 2, 1), :].rearrange("p o n -> p (o n)")
                copy(e[:, 3:3 + H2], ps[:, 0, 0:H2])
                copy(e[:, 3 + H2:3 + NP_], ps[:, 1, 0:NP_ - H2])
                copy(e[:, 3 + NP_:EXT].rearrange("p (b s) -> p b s", s=7)[:, :, 3:7],
                     ps[:, 1, NP_ - H2:H2].rearrange("p (b t) -> p b t", t=DSEQ)).then_inc(evac[0], 1)
            plain(p_xm, xm_out)
            end(act, act_stage)

            begin(act, "project")
            n = first_job["project"]
            act.wait_ge(row_arg, 1)
            act.activation(rows[:, 2, :], rows[:, 2, :], ACT.Exp).then_inc(row_fun, 1)
            act.wait_ge(row_fun, 1)
            act.activation(rows[:, 2, :], rows[:, 2, :], ACT.Ln, bias=1.0).then_inc(row_fun, 1)
            act.wait_ge(row_arg, 2)
            act.activation(rows[:, 0, :], rows[:, 0, :], ACT.Exp).then_inc(row_fun, 1)
            act.activation(wrow, wrow, ACT.Exp).then_inc(row_fun, 1)
            for m in range(1, 8):
                if jobs[n + m] == "a":
                    b = ring_wait(act, n + m)
                    nt = BLOCKS[m - 1][1] if m < 7 else 27
                    copy(vtok[0:nt, m - 1, :] if m < 7 else cvo[:, :], wide(b, nt, D)).then_inc(ring_act, 1)
            for h in range(HM + 1):
                if h < HM:
                    for i in (2 * h, 2 * h + 1):
                        act.wait_ge(conv_ready, i + 1)
                        act.activation(cc[:, i, :], cc[:, i, :], ACT.Silu).then_inc(c_ready, 1)
                if h >= 1:
                    for i in (2 * h - 2, 2 * h - 1):
                        b = ring_wait(act, n + 9 + 2 * i)
                        copy(tok(qm[:, i, :]), two(b)).then_inc(ring_act, 1)
                        b = ring_wait(act, n + 10 + 2 * i)
                        copy(tok(km[:, i, :]), two(b), DHM ** -0.5).then_inc(ring_act, 1)
            end(act, act_stage)

            begin(act, "states")
            b = ring_wait(act, first_job["states"])
            copy(nT, ps[:, b, 0:64].rearrange("p (k s) -> p k s", k=2)).then_inc(ring_act, 1)
            for n in range(len(pairs)):
                act.wait_ge(ct_full, n + 1)
                if n >= 2:
                    act.wait_ge(iq_full, n - 1)
                copy(CT[:, n % 2, :, :].rearrange("p a b -> p (a b)"), ps[:, n % 2, :]).then_inc(ct_ready, 1)
            act.wait_ge(iq_full, len(pairs))
            copy(inter.rearrange("p i s -> p (i s)"), ps[:, 6, 0:256])
            for h in range(HM):
                act.wait_ge(cf_full, h + 1)
                if h >= 1:
                    act.wait_ge(st_c, 16 * h)
                copy(cpo[:, :, :].rearrange("p a b -> p (a b)"), ps[:, 7, :]).then_inc(c_fin, 1)
            end(act, act_stage)

            begin(act, "heads")
            for h in range(HM):
                act.wait_ge(bc_full, 2 * h + 1)
                if h >= 1:
                    act.wait_ge(hm_ready, h)
                copy(tok(tA[:, :]), two(0)).then_inc(bc_ready, 1)
                act.wait_ge(bc_full, 2 * h + 2)
                act.activation(tok(rstd[:, :]), two(0), ACT.Exp).then_inc(bc_ready, 1)
                act.wait_ge(wt_ready, h + 1)
                act.activation(P6[:, 0:WOFF[4]], P6[:, 0:WOFF[4]], ACT.Exp)
                act.activation(P6[0:16, WOFF[4]:WOFF[5]], P6[0:16, WOFF[4]:WOFF[5]], ACT.Exp)
                act.activation(P6[0:NS, WOFF[5]:], P6[0:NS, WOFF[5]:], ACT.Exp).then_inc(we_ready, 1)
                act.wait_ge(num_full, h + 1)
                for o in range(2):
                    act.activation(tC[:, o, 0:SPLIT], ps[:, 2 + 2 * o, 0:SPLIT], ACT.Square)
                    act.activation(tC[:, o, SPLIT:T], ps[:, 3 + 2 * o, 0:T - SPLIT], ACT.Square).then_inc(sqh_ready, 1)
                act.wait_ge(u_ready, h + 1)
                act.activation(rstd[:, :], rstd[:, :], ACT.Ln).then_inc(ln_ready, 1)
                act.wait_ge(ln_ready, h + 1)
                act.activation(rstd[:, :], rstd[:, :], ACT.Exp, scale=-0.5).then_inc(fac_ready, 1)
            for s in range(2):
                split_hi(act, p_om, 0, s)
            end(act, act_stage)

            begin(act, "om")

            def om_body(j, q, jn):
                for s in range(2):
                    prepare(q, jn, s)
                    act.wait_ge(mm_done[s], j + (p_om.before + 1))
                    act.wait_ge(tile_lo, j * 2 + (s + p_om.lo0))
                    act.activation(tok(t2[s][:, :]), two(2 * s), ACT.Sigmoid).then_inc(evac[s], 1)
                    act.wait_ge(om_prod, j * 2 + (s + 1))
                    copy(dyn(hm_hi, j * 2 + s), tok(t2[s][:, :])).then_inc(ohi_ready, 1)
            loop(act, p_om, om_body)
            end(act, act_stage)
            begin(act, "a_qkv")
            gated(p_a, ACT.Sigmoid, None)
            act.wait_ge(mm_done[1], p_a.before + p_a.n)
            plain(p_qkv, lambda j: copy(dyn(qkv, j * 2), two(0)).then_inc(evac[0], 1))
            end(act, act_stage)

            begin(act, "rotary")
            for m in range(12):
                n = first_job["rotary"] + 16 + m
                if jobs[n] == "a":
                    blk = m % 6
                    nt = BLOCKS[blk][1]
                    b = ring_wait(act, n)
                    if m >= 8:
                        act.wait_ge(st_k[blk % 2], 16 * (blk // 2))
                    copy(vtok[0:nt, blk, :] if m < 6 else kout[0:nt, blk % 2, :], wide(b, nt, D)).then_inc(ring_act, 1)
            end(act, act_stage)

            begin(act, "attend")
            for g in range(5 * HD + 3):
                if g < 5 * HD:
                    h, i = divmod(g, 5)
                    q0, nq = BLOCKS[i]
                    act.wait_ge(max_ready, g + 1)
                    if g >= 3:
                        act.wait_ge(at_full, g - 2)
                    c = 2 * (g % 4)
                    for m in range(2):
                        src = ps[0:nq, 2 * (i % 2) + m, 0:q0 + nq] if i < 4 else ps[0:nq, 2 * m:2 * m + 2, 0:264]
                        dst = Pat[g % 3][0:nq, m, 0:q0 + nq]
                        if i == 4:
                            dst = dst.rearrange("p (b n) -> p b n", b=2)
                        e = act.activation(dst, src, ACT.Exp, bias=rowmax[0:nq, c + m:c + m + 1],
                                           accum_out=rowsum[0:nq, c + m:c + m + 1])
                    e.then_inc(e_ready, 1)
                if 2 <= g < 5 * HD + 2:
                    at_copy(*divmod(g - 2, 5))
                if g >= 3 and (g - 3) % 5 == 4:
                    h = (g - 3) // 5
                    act.wait_ge(o_full, h + 1)
                    copy(qkv[:, h, 0:SPLIT], ps[:, 6, 0:SPLIT])
                    copy(qkv[:, h, SPLIT:NP_], ps[:, 7, 0:NP_ - SPLIT]).then_inc(o_ready, 1)
            end(act, act_stage)

            begin(act, "sample")
            for b in range(NB):
                n = score_job(b)
                for g in range(2):
                    bank = ring_wait(act, n + 2 * g)
                    copy(KT[b % 2][0][:, :, 128 * g:128 * g + 128],
                         ps[:, bank, :].rearrange("p (h n) -> p h n", h=4)).then_inc(ring_act, 1)
                act.wait_ge(smax_ready, b + 1)
                if b >= 2:
                    act.wait_ge(ring_full, value_job(b - 2) + 1)
                c = 3 * (b % 2)
                act.activation(Psm[:, b % 2, :], ps[0:64, ring_bank(n + 4), 0:PAST + NS], ACT.Exp,
                               bias=srm[:, c:c + 1], accum_out=srm[:, c + 1:c + 2]).then_inc(ring_act, 1)
            end(act, act_stage)

            begin(act, "subln")
            for h in range(HD + 1):
                if h < HD:
                    if h >= 2:
                        act.wait_ge(ring_full, first_job["subln"] + h - 1)
                    act.activation(t2[h % 2][:, :], qkv[:, h, :], ACT.Square).then_inc(osq_ready, 1)
                if h >= 1:
                    m = h - 1
                    bank = ring_wait(act, first_job["subln"] + m)
                    if m >= 1:
                        act.wait_ge(on_ready, m)
                    act.activation(tok(rstd[:, :]), two(bank), ACT.Ln, bias=con[:, C_EPS:C_EPS + 1],
                                   scale=1.0 / 128).then_inc(ring_act, 1)
                    ring_done(act, first_job["subln"] + m)
                    act.activation(rstd[:, :], rstd[:, :], ACT.Exp, scale=-0.5).then_inc(ofac_ready, 1)
                    act.wait_ge(on_ready, m + 1)
                    copy(o_hi[:, m, :], qkv[:, m, :]).then_inc(xhi_ready, 1)
            for s in range(2):
                split_hi(act, p_b, 0, s)
            end(act, act_stage)

            begin(act, "b")
            gated(p_b, ACT.Sigmoid, m_hi)
            end(act, act_stage)
            begin(act, "out")
            plain(p_wo)
            end(act, act_stage)
            begin(act, "norm3")
            norm(2)
            end(act, act_stage)
            begin(act, "up2")
            gated(up2, ACT.Silu, h_hi)
            end(act, act_stage)
            begin(act, "down2")
            down(down2)
            end(act, act_stage)
            begin(act, "last")
            norm(3, final=True)
            for t in range(5):
                n = first_job["last"] + t
                if jobs[n] == "a":
                    copy(xtok[:, t, :], wide(ring_wait(act, n), 112, D)).then_inc(ring_act, 1)

        @block.vector
        def _(v):
            steps = [0]

            def link(ins_):
                steps[0] += 1
                ins_.then_inc(dve_step, 1)
                v.wait_ge(dve_step, steps[0])

            def prepare(p, j, s):
                if p is not None:
                    split_lo(v, p, j, s)

            def norm(r, gain, hi0, final=False):
                v.wait_ge(rstd_ready, 2 * r + 2)

                def lo(i):
                    v.wait_ge(xhi_ready, hi0 + i + 1)
                    v.tensor_tensor(xn_lo[:, i, :], t2[i % 2][:, :], xn_hi[:, i, :].bitcast(f32),
                                    ALU.subtract).then_inc(xlo_done, 1)
                for i in range(DT):
                    out = X[:, i, :] if final else t2[i % 2][:, :]
                    if i >= 2 and not final:
                        v.wait_ge(xlo_done, DT * r + i - 1)
                    v.scalar_tensor_tensor(out, X[:, i, :], gcol[:, gain + i:gain + i + 1], rstd[:, :],
                                           ALU.mult, ALU.mult).then_inc(xt_ready, 1)
                    if i >= 1 and not final:
                        lo(i - 1)
                if not final:
                    lo(DT - 1)

            def up(p, lo_of):
                def body(j, q, jn):
                    prepare(q, jn, 0)
                    v.wait_ge(evac[0], j + (p.ev0 + 1))
                    v.wait_ge(mm_done[1], j + (p.before + 1))
                    v.wait_ge(tile_lo, j + p.lo0)
                    v.tensor_tensor(tok(tB[:, :]), two(2), tok(tA[:, :]), ALU.mult).then_inc(evac[1], 1)
                    prepare(q, jn, 1)
                    v.wait_ge(tile_hi, j + (p.hi0 + 1))
                    v.tensor_tensor(dyn(h_lo, j), tok(tB[:, :]), dyn(h_hi, j).bitcast(f32),
                                    ALU.subtract).then_inc(tile_lo, 1)
                loop(v, p, body)

            def down(p):
                def add(j, e):
                    v.wait_ge(mm_done[1], j * 2 + (e + p.before + 1))
                    v.scalar_tensor_tensor(dyn(X, j * 2 + e), two(2 * e), 0.5, dyn(X, j * 2 + e),
                                           ALU.mult, ALU.add).then_inc(evac[e], 1)

                def body(j, q, jn):
                    for s in range(2):
                        split_lo(v, p, j * 2 + 1, s)
                    add(j, 0)
                    for s in range(2):
                        prepare(q, jn * 2, s)
                    add(j, 1)
                loop(v, p, body, 2)

            for s in range(2):
                v.drain().then_inc(lo_done[s], 1)
                v.drain().then_inc(evac[s], 1)
            v.drain().then_inc(tile_lo, 1)
            v.memset(ones[:, :], 1.0).then_inc(ones_ready, 1)
            for i in range(DT):
                if jobs[i] == "d":
                    b = ring_wait(v, i)
                    v.tensor_copy(X[:, i, 0:448], ps[:, b, 0:448])
                    v.tensor_copy(X[:, i, 448:560], ps[:, b + 1, 0:112]).then_inc(ring_dve, 1)
            v.wait_ge(in_small, 16 * 15)
            lr = lrow[:, :, :].rearrange("p (a c) d -> p a c d", c=2)
            lp = lprod[:, 0:2 * DHD].rearrange("p (a d) -> p a d", a=2)
            link(v.tensor_tensor(lp, lr[:, :, 0, :], lr[:, :, 1, :], ALU.mult))
            v.reduce_sum(lam2[:, 0:2], lp, AX.X).then_inc(lam_row, 1)
            v.wait_ge(lam_exp, 1)
            v.scalar_tensor_tensor(lam2[:, 2:3], lam2[:, 1:2], LAMBDA_INIT, lam2[:, 0:1],
                                   ALU.subtract, ALU.subtract).then_inc(lam_neg, 1)
            b = ring_wait(v, DT)
            v.tensor_copy(neglam, ps[:, b + 1, 0:1])
            link(v.tensor_copy(gcol[:, :], ps[:, b, 0:G_N]))
            v.tensor_scalar(gsub, gcol[:, G_SUB:G_SUB + 1], 1.0 - LAMBDA_INIT, None, ALU.mult)
            v.scalar_tensor_tensor(mv, con[0:64, C_M1:C_M1 + 1], neglam[0:64, :], con[0:64, C_M0:C_M0 + 1],
                                   ALU.mult, ALU.add).then_inc(ring_dve, 1)
            end(v, dve_stage)
            begin(v, "norm1")
            norm(0, G_FFN1, 0)
            for s in range(2):
                split_lo(v, up1, 0, s)
            end(v, dve_stage)
            begin(v, "up1")
            up(up1, h_lo)
            end(v, dve_stage)
            begin(v, "down1")
            down(down1)
            end(v, dve_stage)
            begin(v, "norm2")
            v.memset(gw[:, :, :], 0.0).then_inc(gw_zero, 1)
            norm(1, G_MIX, DT)
            v.wait_ge(ghi, 1)
            v.tensor_tensor(gw_lo[:, :, :], gw[:, :, :], gw_hi[:, :, :].bitcast(f32), ALU.subtract).then_inc(glo, 1)
            v.memset(E[:, :, 0:3], 0.0)
            end(v, dve_stage)

            begin(v, "xm")

            def xm_body(j, q, jn):
                prepare(q, jn, 0)
                prepare(q, jn, 1)
                v.wait_ge(mm_done[1], j + (p_xm.before + 1))
                e = E[:, bass.ds(j * 2 + 1, 1), :].rearrange("p o n -> p (o n)")
                v.tensor_copy(e[:, 3:3 + H2], ps[:, 2, 0:H2])
                v.tensor_copy(e[:, 3 + H2:3 + NP_], ps[:, 3, 0:NP_ - H2])
                v.tensor_copy(e[:, 3 + NP_:EXT].rearrange("p (b s) -> p b s", s=7)[:, :, 3:7],
                              ps[:, 3, NP_ - H2:H2].rearrange("p (b t) -> p b t", t=DSEQ)).then_inc(evac[1], 1)
            loop(v, p_xm, xm_body)
            end(v, dve_stage)

            begin(v, "project")
            n = first_job["project"]
            r = [rows[:, i, :] for i in range(5)]
            v.wait_ge(gates_full, 1)
            v.tensor_scalar(tok(r[4]), ps[0:4, 4:6, 0:H2], bgate[:, 0:1], None, ALU.add).then_inc(gates_read, 1)
            v.tensor_copy(tok(r[0]), ps[32:36, 4:6, 0:H2]).then_inc(gates_read, 1)
            es = E[:, :, 3 + NP_:EXT].rearrange("p i (b s) -> p i b s", s=7)
            b = ring_wait(v, n)
            v.tensor_copy(es[:, :, :, 0:3], ps[:, b, 0:192].rearrange("p (i b j) -> p i b j", i=DT, j=3)).then_inc(ring_dve, 1)
            v.memset(vtok[:, 4:6, :], 0.0)
            v.tensor_copy(xs[:, :, :].rearrange("p i (b t) -> p i b t", t=DSEQ), es[:, :, :, 3:7]).then_inc(xs_ready, 1)
            v.tensor_copy(cvt[:, :, 0:3], E[:, :, NP_:NP_ + 3])
            v.tensor_copy(cvt[:, :, 3:27].rearrange("p i (b j) -> p i b j", j=3), es[:, :, :, 4:7]).then_inc(cvt_ready, 1)

            def sam(x):
                return x[:, NP_:T].rearrange("p (b t) -> p b t", t=DSEQ)
            v.wait_ge(gates_read, 2)
            link(v.tensor_scalar(r[0], r[0], bgate[:, 1:2], None, ALU.add))
            link(v.tensor_scalar(r[1], r[0], 0.0, None, ALU.min))
            v.scalar_tensor_tensor(r[2], r[1], 2.0, r[0], ALU.mult, ALU.subtract).then_inc(row_arg, 1)
            link(v.memset(r[3], 1.0))
            v.memset(sam(r[3])[:, :, 0:1], 0.0)
            v.wait_ge(row_fun, 2)
            link(v.tensor_tensor(r[1], r[1], r[2], ALU.subtract))
            link(v.tensor_tensor_scan(r[0], r[3], r[1], 0.0, ALU.mult, ALU.add))
            link(v.tensor_tensor(r[1], r[4], r[0], ALU.subtract))
            v.tensor_copy(r[2], r[1])
            link(v.memset(r[3], 0.0))
            v.memset(sam(r[3])[:, :, 0:1], NEG)
            link(v.tensor_tensor(sam(r[2])[:, :, 0], sam(r[1])[:, :, 0], m0row, ALU.max))
            link(v.tensor_tensor_scan(r[4], r[3], r[2], 0.0, ALU.add, ALU.max))
            link(v.tensor_tensor(r[3], r[0], r[4], ALU.add))
            v.tensor_copy(mout[:, 0:1], r[3][:, NP_ - 1:NP_])
            v.tensor_copy(mout[:, 1:9], sam(r[3])[:, :, DSEQ - 1]).then_inc(m_ready, 1)
            v.tensor_scalar(r[2], r[4], -1.0, None, ALU.mult)
            v.tensor_tensor(wrow.rearrange("p (b t) -> p b t", t=DSEQ),
                            m0row.unsqueeze(2).to_broadcast([HM, NB, DSEQ]), sam(r[4]), ALU.subtract)
            v.tensor_scalar(r[0][:, 0:NP_], r[1][:, 0:NP_], r[4][:, NP_ - 1:NP_], None, ALU.subtract)
            v.tensor_tensor(sam(r[0]), sam(r[1]), sam(r[4])[:, :, DSEQ - 1:DSEQ].to_broadcast([HM, NB, DSEQ]),
                            ALU.subtract).then_inc(row_arg, 1)
            v.wait_ge(m_ready, 1)
            v.tensor_scalar(r[3], r[3], -1.0, None, ALU.mult)
            for i in range(DT):
                outs_ = (cc[:, i, 0:NP_], cc[:, i, NP_:T].rearrange("p (b t) -> p b t", t=DSEQ))
                for j in range(4):
                    w = gcol[:, G_CW + 8 * j + i:G_CW + 8 * j + i + 1]
                    for k, o in enumerate(outs_):
                        x = E[:, i, j:j + NP_] if k == 0 else es[:, i, :, j:j + DSEQ]
                        if j == 0:
                            c = v.tensor_scalar(o, x, w, gcol[:, G_CB + i:G_CB + i + 1], ALU.mult, ALU.add)
                        else:
                            c = v.scalar_tensor_tensor(o, x, w, o, ALU.mult, ALU.add)
                    if j < 3:
                        link(c)
                c.then_inc(conv_ready, 1)
                if i == 3:
                    bank = ring_wait(v, n + 8)
                    a32 = small2[:, 0:48]
                    v.tensor_copy(a32[:, 0:32], ps[:, bank, 0:32])
                    v.tensor_copy(a32[0:16, 32:40], ps[0:16, bank, 32:40])
                    v.tensor_copy(a32[0:NS, 40:48], ps[0:NS, bank, 40:48])
                    v.tensor_copy(dec8, ps[0:NB, bank, 64:68])
                    v.tensor_copy(small2[:, 80:208], ps[:, bank + 1, 0:128]).then_inc(ring_dve, 1)
            v.wait_ge(ring_full, n + 25)
            link(v.memset(ktok[:, 4, :], 0.0))
            for blk, (t0, nt) in enumerate(BLOCKS):
                bank = ring_wait(v, n + 25 + blk)
                v.tensor_tensor(ktok[0:nt, blk, :].rearrange("p (h d) -> p h d", h=HM),
                                wide(bank, nt, D).rearrange("p (h d) -> p h d", h=HM),
                                acol[0:nt, blk, 1, :].unsqueeze(2).to_broadcast([nt, HM, DHM]),
                                ALU.mult).then_inc(ring_dve, 1)
            end(v, dve_stage)

            begin(v, "states")
            v.memset(kwb[32:64, :, :], 0.0)
            v.memset(kwb[64:128, :, :], 0.0)
            link(v.tensor_tensor(qs[:, :, :].rearrange("p (h k) s -> p h k s", k=2),
                                 qm[:, :, NP_:T].rearrange("p (h k) s -> p h k s", k=2),
                                 wbc.unsqueeze(2).to_broadcast([128, HM, 2, NS]), ALU.mult))
            ring_done(v, first_job["states"])
            for h in range(HM):
                c = v.tensor_tensor(nqs[:, 2 * h:2 * h + 2, :].rearrange("p k (b t) -> p k b t", t=DSEQ),
                                    qs[:, 2 * h:2 * h + 2, :].rearrange("p k (b t) -> p k b t", t=DSEQ),
                                    nT.rearrange("p k (b h) -> p k b h", h=HM)[:, :, :, h:h + 1].to_broadcast([128, 2, NB, DSEQ]),
                                    ALU.mult)
            c.then_inc(qs_ready, 1)
            link(v.tensor_tensor(nst[:, :, :], nst[:, :, :], dec8.unsqueeze(2).to_broadcast([NB, HM, DHM]), ALU.mult))
            for n, (h, b) in enumerate(pairs):
                if b == 0:
                    if h >= 1:
                        v.wait_ge(cu_full, NB * h)
                    v.tensor_tensor(kwb[0:NS, :, :],
                                    ktok[0:NS, 5, DHM * h:DHM * h + DHM].unsqueeze(1).to_broadcast([NS, NB, DHM]),
                                    con[0:NS, C_BM:C_BM + NB].unsqueeze(2).to_broadcast([NS, NB, DHM]),
                                    ALU.mult).then_inc(kwb_ready, 1)
                v.wait_ge(cu_full, n + 1)
                st = Cb[:, n % 4, :, :].rearrange("p a b -> p (a b)")
                v.scalar_tensor_tensor(st, st, wbc[:, h, DSEQ * b + DSEQ - 1:DSEQ * b + DSEQ], ps[:, 2 + n % 2, :],
                                       ALU.mult, ALU.add).then_inc(c_new, 1)
            v.wait_ge(nn_full, 1)
            v.tensor_tensor(nst[:, :, :].rearrange("p h d -> p (h d)"), nst[:, :, :].rearrange("p h d -> p (h d)"),
                            wide(4, NB, D), ALU.add).then_inc(n_new, 1)
            v.wait_ge(nf_full, 1)
            v.tensor_copy(npo[:, :], wide(4, 1, D)).then_inc(n_fin, 1)
            end(v, dve_stage)

            begin(v, "heads")
            for h in range(HM):
                v.wait_ge(bc_ready, 2 * h + 1)
                if h >= 1:
                    v.wait_ge(num_full, h)
                for blk, (t0, nt) in enumerate(BLOCKS):
                    nq_ = NP_ - t0 if blk < 5 else NS
                    c = v.tensor_scalar(P6[0:nt, WOFF[blk]:WOFF[blk] + nq_], tA[0:nt, t0:t0 + nq_],
                                        acol[0:nt, blk, 0, h:h + 1], 0.0, ALU.add, ALU.min)
                c.then_inc(wt_ready, 1)
                v.wait_ge(we_ready, h + 1)
                for blk, (t0, nt) in enumerate(BLOCKS):
                    mask = con[0:nt, C_CAUSAL:C_CAUSAL + nt] if blk < 5 else con[0:NS, C_BLK:C_BLK + NS]
                    d = P6[0:nt, WOFF[blk]:WOFF[blk] + nt]
                    c = v.tensor_tensor(d, d, mask, ALU.mult)
                link(c)
                for blk, (t0, nt) in enumerate(BLOCKS):
                    nq_ = NP_ - t0 if blk < 5 else NS
                    v.wait_ge(sc_full, 6 * h + blk + 1)
                    if blk == 0:
                        v.tensor_tensor(P6[:, 0:SPLIT], ps[:, 0, 0:SPLIT], P6[:, 0:SPLIT], ALU.mult)
                        v.tensor_tensor(P6[:, SPLIT:NP_], ps[:, 1, 0:NP_ - SPLIT], P6[:, SPLIT:NP_],
                                        ALU.mult).then_inc(p_ready, 1)
                    else:
                        p = P6[0:nt, WOFF[blk]:WOFF[blk] + nq_]
                        v.tensor_tensor(p, ps[0:nt, (blk + 1) % 2, 0:nq_], p, ALU.mult).then_inc(p_ready, 1)
                v.wait_ge(num_full, h + 1)
                v.wait_ge(bc_ready, 2 * h + 2)
                for half, (c0, c1) in enumerate(((0, SPLIT), (SPLIT, T))):
                    c = v.scalar_tensor_tensor(rstd[:, c0:c1], ps[:, 6 + half, 0:c1 - c0], -1.0, rstd[:, c0:c1],
                                               ALU.mult, ALU.max)
                link(c)
                for half, (c0, c1) in enumerate(((0, SPLIT), (SPLIT, T))):
                    c = v.tensor_tensor(rstd[:, c0:c1], ps[:, 6 + half, 0:c1 - c0], rstd[:, c0:c1], ALU.max)
                link(c)
                link(v.scalar_tensor_tensor(rstd[:, :], rstd[:, :], EPS, rstd[:, :], ALU.mult, ALU.mult))
                v.wait_ge(ssh_full, h + 1)
                v.scalar_tensor_tensor(tok(rstd[:, :]), two(0), 1.0 / DHM, tok(rstd[:, :]),
                                       ALU.mult, ALU.add).then_inc(u_ready, 1)
                v.wait_ge(fac_ready, h + 1)
                for o in range(2):
                    g = gcol[:, G_ML + 2 * h + o:G_ML + 2 * h + o + 1]
                    for half, (c0, c1) in enumerate(((0, SPLIT), (SPLIT, T))):
                        c = v.scalar_tensor_tensor(qm[:, 2 * h + o, c0:c1], ps[:, 2 + 2 * o + half, 0:c1 - c0], g,
                                                   rstd[:, c0:c1], ALU.mult, ALU.mult)
                c.then_inc(hm_ready, 1)
            for s in range(2):
                split_lo(v, p_om, 0, s)
            end(v, dve_stage)

            begin(v, "om")

            def om_body(j, q, jn):
                for s in range(2):
                    prepare(q, jn, s)
                    v.wait_ge(evac[s], j + (p_om.ev0 + 1))
                    v.tensor_tensor(tok(t2[s][:, :]), tok(t2[s][:, :]), dyn(qm, j * 2 + s), ALU.mult).then_inc(om_prod, 1)
                    v.wait_ge(ohi_ready, j * 2 + (s + 1))
                    v.tensor_tensor(dyn(hm_lo, j * 2 + s), tok(t2[s][:, :]), dyn(hm_hi, j * 2 + s).bitcast(f32),
                                    ALU.subtract).then_inc(tile_lo, 1)
            loop(v, p_om, om_body)
            end(v, dve_stage)

            begin(v, "a_qkv")

            def a_body(j, q, jn):
                prepare(q, jn, 0)
                v.wait_ge(evac[0], j + (p_a.ev0 + 1))
                v.wait_ge(mm_done[1], j + (p_a.before + 1))
                v.tensor_tensor(dyn(M, j), two(2), tok(tA[:, :]), ALU.mult).then_inc(evac[1], 1)
                prepare(q, jn, 1)
            loop(v, p_a, a_body)
            v.wait_ge(mm_done[1], p_a.before + p_a.n)

            def qkv_body(j, q, jn):
                prepare(q, jn, 0)
                prepare(q, jn, 1)
                v.wait_ge(mm_done[1], j + (p_qkv.before + 1))
                v.tensor_copy(dyn(qkv, j * 2 + 1), two(2)).then_inc(evac[1], 1)
            loop(v, p_qkv, qkv_body)
            end(v, dve_stage)

            begin(v, "rotary")
            v.wait_ge(in_trig, 16)
            cos, sin = trig[:, 0, :], trig[:, 1, :]
            for i in range(2 * DT):
                bank = ring_wait(v, first_job["rotary"] + i)
                v.tensor_tensor(tok(t2[i % 2][:, :]), two(bank), tok(sin), ALU.mult).then_inc(ring_dve, 1)
                link(v.tensor_tensor(qkv[:, i, :], qkv[:, i, :], cos, ALU.mult))
                v.tensor_tensor(qkv[:, i, :], qkv[:, i, :], t2[i % 2][:, :], ALU.add).then_inc(rot_ready, 1)
            for m in range(12):
                n = first_job["rotary"] + 16 + m
                if jobs[n] == "d":
                    blk = m % 6
                    nt = BLOCKS[blk][1]
                    bank = ring_wait(v, n)
                    if m >= 8:
                        v.wait_ge(st_k[blk % 2], 16 * (blk // 2))
                    v.tensor_copy(vtok[0:nt, blk, :] if m < 6 else kout[0:nt, blk % 2, :], wide(bank, nt, D)).then_inc(ring_dve, 1)
            end(v, dve_stage)

            begin(v, "attend")
            for b in range(2):
                v.memset(qz[64:128, b, 0, :], 0.0)
                v.memset(qz[0:64, b, 1, :], 0.0)

            def scaled_q(h):
                if h >= 2:
                    v.wait_ge(s_full, 5 * (h - 1))
                v.tensor_scalar(qz[0:64, h % 2, 0, 0:NP_], qkv[0:64, h, 0:NP_], DHD ** -0.5, None, ALU.mult)
                v.tensor_scalar(qz[64:128, h % 2, 1, 0:NP_], qkv[64:128, h, 0:NP_], DHD ** -0.5, None,
                                ALU.mult).then_inc(qz_ready, 1)

            def combine(g):
                i = g % 5
                q0, nq_ = BLOCKS[i]
                c = 2 * (g % 4)
                nk = q0 + nq_
                v.wait_ge(e_ready, g + 1)
                link(v.reciprocal(rinv[0:nq_, c:c + 2], rowsum[0:nq_, c:c + 2]))
                v.tensor_scalar(Pat[g % 3][0:nq_, 0, 0:nk], Pat[g % 3][0:nq_, 0, 0:nk], rinv[0:nq_, c:c + 1], None, ALU.mult)
                link(v.tensor_tensor(rinv[0:nq_, c + 1:c + 2], rinv[0:nq_, c + 1:c + 2], neglam[0:nq_, :], ALU.mult))
                v.scalar_tensor_tensor(Pat[g % 3][0:nq_, 0, 0:nk], Pat[g % 3][0:nq_, 1, 0:nk], rinv[0:nq_, c + 1:c + 2],
                                       Pat[g % 3][0:nq_, 0, 0:nk], ALU.mult, ALU.add).then_inc(a_ready, 1)

            scaled_q(0)
            for g in range(5 * HD):
                h, i = g // 5, g % 5
                q0, nq_ = BLOCKS[i]
                v.wait_ge(s_full, g + 1)
                c = 2 * (g % 4)
                if i < 4:
                    v.tensor_reduce(rowmax[0:nq_, c:c + 2], ps[0:nq_, 2 * (i % 2):2 * (i % 2) + 2, 0:q0 + nq_], AX.X, ALU.max,
                                    negate=True).then_inc(max_ready, 1)
                else:
                    v.tensor_reduce(rowmax[0:nq_, c:c + 2],
                                    ps[0:nq_, 0:4, 0:264].rearrange("p (m b) n -> p m b n", b=2), AX.XY, ALU.max,
                                    negate=True).then_inc(max_ready, 1)
                if i == 2 and h + 1 < HD:
                    scaled_q(h + 1)
                if g >= 1:
                    combine(g - 1)
            combine(5 * HD - 1)
            end(v, dve_stage)

            begin(v, "sample")
            link(v.memset(Qbd[:, :, :, :], 0.0))
            for h in range(HD):
                for m in range(2):
                    q = qkv[64 * m:64 * m + 64, h, NP_:T].rearrange("p (b t) -> p b t", t=DSEQ)
                    v.tensor_scalar(Qbd[64 * m:64 * m + 64, :, h, 8 * h + 4 * m:8 * h + 4 * m + 4], q,
                                    DHD ** -0.5, None, ALU.mult)
            for b in range(2):
                for i in range(2):
                    c = v.tensor_copy(KT[b][i][:, :, PAST:PAST + NS], qkv[:, DT + 4 * i:DT + 4 * i + 4, NP_:T])
            c.then_inc(qbd_ready, 1)
            for b in range(NB + 1):
                if b >= 1:
                    c = 3 * ((b - 1) % 2)
                    ring_done(v, score_job(b - 1) + 4)
                    link(v.reciprocal(srm[:, c + 2:c + 3], srm[:, c + 1:c + 2]))
                    v.tensor_scalar(Psm[:, (b - 1) % 2, :], Psm[:, (b - 1) % 2, :], srm[:, c + 2:c + 3], mv, ALU.mult,
                                    ALU.mult).then_inc(sp_ready, 1)
                if b < NB:
                    n = score_job(b)
                    for g in range(2):
                        bank = ring_wait(v, n + 2 * g + 1)
                        v.tensor_copy(KT[b % 2][1][:, :, 128 * g:128 * g + 128],
                                      ps[:, bank, :].rearrange("p (h n) -> p h n", h=4)).then_inc(ring_dve, 1)
                    bank = ring_wait(v, n + 4)
                    c = 3 * (b % 2)
                    v.reduce_max(srm[:, c:c + 1], ps[0:64, bank, 0:PAST + NS], AX.X, negate=True).then_inc(smax_ready, 1)
                if b >= 1:
                    n = value_job(b - 1)
                    bank = ring_wait(v, n)
                    v.tensor_copy(AT3[:, (b - 1) % 2, 0:2, :], ps[:, bank, 0:64].rearrange("p (g s) -> p g s", g=2))
                    v.tensor_copy(AT3[0:NS, (b - 1) % 2, 2, :], ps[0:NS, bank, 64:96]).then_inc(ring_dve, 1)
                    bank = ring_wait(v, n + 1)
                    v.tensor_copy(qkv[:, 0:DT, NP_ + 4 * b - 4:NP_ + 4 * b],
                                  ps[:, bank, 0:32].rearrange("p (h t) -> p h t", t=DSEQ)).then_inc(ring_dve, 1)
            end(v, dve_stage)

            begin(v, "subln")
            for m in range(HD):
                v.wait_ge(ofac_ready, m + 1)
                v.scalar_tensor_tensor(qkv[:, m, :], qkv[:, m, :], gsub, rstd[:, :], ALU.mult, ALU.mult).then_inc(on_ready, 1)
                v.wait_ge(xhi_ready, 2 * DT + m + 1)
                v.tensor_tensor(o_lo[:, m, :], qkv[:, m, :], o_hi[:, m, :].bitcast(f32), ALU.subtract)
            for s in range(2):
                split_lo(v, p_b, 0, s)
            end(v, dve_stage)

            begin(v, "b")

            def b_body(j, q, jn):
                prepare(q, jn, 0)
                v.wait_ge(evac[0], j + (p_b.ev0 + 1))
                v.wait_ge(mm_done[1], j + (p_b.before + 1))
                v.wait_ge(tile_lo, j * 2 + p_b.lo0)
                v.tensor_tensor(tok(tB[:, :]), two(2), tok(tA[:, :]), ALU.mult).then_inc(tile_lo, 1)
                v.wait_ge(tile_lo, j * 2 + (p_b.lo0 + 1))
                v.tensor_tensor(tok(tB[:, :]), tok(tB[:, :]), dyn(M, j), ALU.add).then_inc(evac[1], 1)
                prepare(q, jn, 1)
                v.wait_ge(tile_hi, j + (p_b.hi0 + 1))
                v.tensor_tensor(dyn(m_lo, j), tok(tB[:, :]), dyn(m_hi, j).bitcast(f32),
                                ALU.subtract).then_inc(tile_lo, 1)
            loop(v, p_b, b_body)
            end(v, dve_stage)

            begin(v, "out")

            def wo_body(j, q, jn):
                for s in range(2):
                    prepare(q, jn, s)
                    v.wait_ge(mm_done[s], j + (p_wo.before + 1))
                    v.tensor_tensor(dyn(X, j * 2 + s), two(2 * s), dyn(X, j * 2 + s), ALU.add).then_inc(evac[s], 1)
            loop(v, p_wo, wo_body)
            end(v, dve_stage)
            begin(v, "norm3")
            norm(2, G_FFN2, 3 * DT)
            end(v, dve_stage)
            begin(v, "up2")
            up(up2, h_lo)
            end(v, dve_stage)
            begin(v, "down2")
            down(down2)
            end(v, dve_stage)
            begin(v, "last")
            norm(3, G_FINAL, 0, final=True)
            for t in range(5):
                n = first_job["last"] + t
                if jobs[n] == "d":
                    v.tensor_copy(xtok[:, t, :], wide(ring_wait(v, n), 112, D)).then_inc(ring_dve, 1)


_INS = ["x_prompt", "x_sample", "cache_k", "cache_v", "page_table", "state_C", "state_n", "state_m", "state_conv",
        "meta_tokens", "ffn1_norm", "ffn1_w_gate", "ffn1_w_up", "ffn1_w_down", "mix_norm", "w_in",
        "conv_w", "conv_b", "w_mq", "w_mk", "w_mv", "b_igate", "b_fgate", "mlstm_norm",
        "lambda_q1", "lambda_k1", "lambda_q2", "lambda_k2", "subln", "w_proj_a", "w_proj_b", "w_out",
        "ffn2_norm", "ffn2_w_gate", "ffn2_w_up", "ffn2_w_down", "final_norm"]


def kernel(**inputs):
    import concourse.bacc as _bacc
    from concourse.bass_utils import run_bass_kernel_spmd as _run

    nc = _bacc.Bacc("TRN2", target_bir_lowering=False, num_devices=1)
    arrays, aps = {}, {}
    for name in _INS:
        a = np.ascontiguousarray(inputs[name])
        arrays[f"in_{name}"] = a
        aps[name] = nc.dram_tensor(f"in_{name}", a.shape, mybir.dt.from_np(a.dtype), kind="ExternalInput").ap()
    c = constants()
    arrays["constants"] = c
    const_ap = nc.dram_tensor("constants", c.shape, mybir.dt.float32, kind="ExternalInput").ap()
    outs = [nc.dram_tensor(f"out_{i}", shape, mybir.dt.float32, kind="ExternalOutput").ap()
            for i, shape in enumerate(OUTS)]
    build(nc, aps, outs, const_ap)
    r = _run(nc, [arrays], core_ids=[0])
    return tuple(r.results[0][f"out_{i}"] for i in range(len(OUTS)))
```

```python
from contextlib import ExitStack

import numpy as np

import concourse.bass as bass
from concourse import mybir

D = 1024
SEQ, NMETA, NB, DSEQ = 512, 16, 8, 4
PAST, PAGE = 256, 128
DFF = 2816
HM, DHM = 4, 256
HD, DHD = 8, 64
ROT, THETA = 16, 500000.0
EPS = 1e-6
LAMBDA_INIT = 0.2
NP_ = SEQ + NMETA
NS = NB * DSEQ
T = NP_ + NS
H2 = T // 2
DT = D // 128
FT = DFF // 128
KD = FT // 2
N_POOL = NB * (PAST // PAGE) * 5 // 4
OFF_XM, OFF_OM, OFF_GATE = 0, D, 2 * D
OFF_QKV = 2 * D + 2 * HM
OFF_GA = OFF_QKV + 3 * D
OFF_GB = OFF_GA + D
SPLIT = 256
BLOCKS = [(0, 128), (128, 128), (256, 128), (384, 128), (512, 16), (NP_, NS)]
WOFF = [0, 528, 928, 1200, 1344, 1360]
EXT = 3 + NP_ + NB * 7
NEG = -1.0e30
G_FFN1, G_MIX, G_FFN2, G_FINAL, G_CW, G_CB, G_ML, G_SUB, G_N = 0, 8, 16, 24, 32, 64, 72, 80, 81
C_ID, C_CAUSAL, C_NEG, C_ROT = 0, 128, 256, 384
C_BLK = 512
C_BM = C_BLK + NS
C_SEL = C_BM + NB
C_WM = C_SEL + HM * 128
C_SA = C_WM + 60
C_M0 = C_SA + NS
C_M1 = C_M0 + 1
C_EPS = C_M1 + 1
C_Q = C_EPS + 1
C_QT = C_Q + 32
C_Q0 = C_QT + 16
C_Q1 = C_Q0 + 1
C_N = C_Q1 + 1
C_COS, C_SIN = C_N, C_N + T
C_ALL = C_SIN + T

OUTS = [((1, SEQ, D)), ((NB, DSEQ, D)), ((1, 1, NP_, HD, 128)), ((1, 1, NP_, HD, 128)),
        ((1, 1, HM, DHM, DHM)), ((1, 1, HM, DHM)), ((1, 1, HM)), ((1, 1, 3, D)),
        ((1, NB, DSEQ, HD, 128)), ((1, NB, DSEQ, HD, 128)), ((1, NB, HM, DHM, DHM)),
        ((1, NB, HM, DHM)), ((1, NB, HM)), ((1, NB, 3, D))]


def constants():
    c = np.zeros((128, C_ALL), np.float32)
    i = np.arange(128)
    c[:, C_ID:C_ID + 128] = np.eye(128)
    c[:, C_CAUSAL:C_CAUSAL + 128] = i[:, None] <= i[None, :]
    c[:, C_NEG:C_NEG + 128] = np.where(i[None, :] <= i[:, None], 0.0, NEG)
    half = ROT // 2
    for base in (0, 64):
        for j in range(half):
            c[base + j + half, C_ROT + base + j] = -1.0
            c[base + j, C_ROT + base + j + half] = 1.0
    pos = np.concatenate([np.arange(NP_), np.tile(PAST + np.arange(DSEQ), NB)]).astype(np.float32)
    freq = (np.float32(THETA) ** (-np.arange(half, dtype=np.float32) / np.float32(half))).astype(np.float32)
    ang = pos[None, :] * freq[:, None]
    c[:, C_COS:C_COS + T] = 1.0
    for base in (0, 64):
        for o in (0, half):
            c[base + o:base + o + half, C_COS:C_COS + T] = np.cos(ang)
            c[base + o:base + o + half, C_SIN:C_SIN + T] = np.sin(ang)
    s = np.arange(NS)
    c[0:NS, C_BLK:C_BLK + NS] = (s[:, None] // DSEQ == s[None, :] // DSEQ) & (s[:, None] <= s[None, :])
    c[0:NS, C_BM:C_BM + NB] = s[:, None] // DSEQ == np.arange(NB)[None, :]
    for h in range(HM):
        c[h, C_SEL + 128 * h:C_SEL + 128 * (h + 1)] = 1.0
    r = np.arange(64)
    w = np.full((64, 60), NEG)
    for k in range(DSEQ):
        w[:, 28 + k] = np.where(k <= r % DSEQ, 0.0, NEG)
    c[0:64, C_WM:C_WM + 60] = w
    c[r, C_SA + (r // 8) * DSEQ + r % DSEQ] = 1.0
    c[0:64, C_M0] = (r // DSEQ) % 2 == 0
    c[0:64, C_M1] = (r // DSEQ) % 2 == 1
    c[:, C_EPS] = EPS
    both = np.tile(np.eye(NMETA), 2)
    c[0:16, C_Q:C_Q + 32] = both
    c[0:32, C_QT:C_QT + 16] = both.T
    c[0:16, C_Q0] = 1.0
    c[16:32, C_Q1] = 1.0
    return c


def build(nc, ins, outs, const_ap):
    f32, f32r, i32 = mybir.dt.float32, mybir.dt.float32r, mybir.dt.int32
    ACT = mybir.ActivationFunctionType
    ALU = mybir.AluOpType
    AX = mybir.AxisListType
    (y_prompt, y_sample, k_prompt, v_prompt, C_prompt, n_prompt, m_prompt, conv_prompt,
     k_sample, v_sample, C_sample, n_sample, m_sample, conv_sample) = outs

    ctx = ExitStack()
    with ctx:
        cursor = [16512]

        def at(name, shape, dt, offset=None):
            size = int(np.prod(shape[1:])) * 4
            if offset is None:
                offset = cursor[0]
                cursor[0] += (size + 31) // 32 * 32
            return nc.alloc_sbuf_tensor_at(name, shape, dt, offset=offset)

        X = at("X", [128, DT, T], f32)
        xn_hi = at("xn_hi", [128, DT, T], f32r)
        xn_lo = at("xn_lo", [128, DT, T], f32r)
        slots = cursor[0]
        raw = [at(f"raw{s}", [128, KD, 128], f32) for s in range(2)]
        w_hi = [at(f"w_hi{s}", [128, KD, 128], f32r) for s in range(2)]
        w_lo = [at(f"w_lo{s}", [128, KD, 128], f32r) for s in range(2)]
        slots_end = cursor[0]
        con = at("con", [128, C_N], f32)
        ones = at("ones", [128, 128], f32)
        gcol = at("gcol", [128, G_N], f32)
        tA = at("tA", [128, T], f32)
        tB = at("tB", [128, T], f32)
        rstd = at("rstd", [128, T], f32)
        small = at("small", [128, 64], f32)
        R = cursor[0]
        mlw = at("mlw", [128, 3, 2 * HM, DHM], f32, slots)
        pages = at("pages", [128, 3, 2, D], f32, slots)
        kout = at("kout", [128, 2, D], f32, slots)
        h_hi = at("h_hi", [128, FT, T], f32r, R)
        h_lo = at("h_lo", [128, FT, T], f32r, R + FT * T * 4)
        xtok = at("xtok", [112, 5, D], f32, R)
        vecs = at("vecs", [G_N, 128], f32, R + 5 * D * 4)
        lrow = at("lrow", [1, 4, DHD], f32, R + 5 * D * 4 + 512)
        lprod = at("lprod", [1, 4 * DHD], f32, R + 5 * D * 4 + 512 + 1024)
        TB4 = DT * T * 4
        RQ = R + EXT * DT * 4 + TB4
        E = at("E", [128, DT, EXT], f32, R)
        cc = at("cc", [128, DT, T], f32, R + EXT * DT * 4)
        qm = at("qm", [128, DT, T], f32, RQ)
        km = at("km", [128, DT, T], f32, RQ + TB4)
        RV = RQ + 2 * TB4
        vtok = at("vtok", [128, 6, D], f32, RV)
        RW = RV + 6 * D * 4
        rows = at("rows", [HM, 5, T], f32, RW)
        ktok = at("ktok", [128, 6, D], f32, R)
        P6 = at("P6", [128, 1392], f32, R + 6 * D * 4)
        tC = at("tC", [128, 2, T], f32, R + 6 * D * 4 + 5568)
        small2 = at("small2", [128, 512], f32, RW + 5 * T * 4)
        page_sb = at("page_sb", [1, 16], i32, RW + 5 * T * 4 + 2048)
        REND = 229344
        gw = at("gw", [128, DT, 36], f32, RQ)
        gw_hi = at("gw_hi", [128, DT, 36], f32r, RQ + 1152)
        gw_lo = at("gw_lo", [128, DT, 36], f32r, RQ + 2304)
        sconv = at("sconv", [24, D], f32, RQ + 4096)
        cvt = at("cvt", [128, DT, 27], f32, slots + 24576)
        cvo = at("cvo", [27, D], f32, slots + 24576 + 1024)
        xs = at("xs", [128, DT, NS], f32, slots + 24576 + 1024 + 4096)
        Cb = at("Cb", [128, 4, 2, DHM], f32, slots)
        CT = at("CT", [128, 2, 2, DHM], f32, slots + 8192)
        kwb = [at(f"kwb{i}", [128, NB, DHM], f32, o) for i, o in enumerate((slots + 12288, R + 6 * D * 4))]
        nst = at("nst", [NB, HM, DHM], f32, slots + 20480)
        nrow = at("nrow", [NS, DHM], f32, slots + 24576)
        cpo = at("cpo", [128, HM, 2, DHM], f32, slots + 12288)
        npo = at("npo", [1, D], f32, slots + 27648)
        assert slots + 27648 + 4096 <= slots_end
        hm_hi = at("hm_hi", [128, DT, T], f32r, R)
        hm_lo = at("hm_lo", [128, DT, T], f32r, R + TB4)
        M = at("M", [128, DT, T], f32, RQ + TB4)
        u4 = at("u4", [128, HM, T], f32, slots + 24576)
        fac4 = at("fac4", [128, HM, T], f32, RQ + TB4)
        assert slots + 24576 + HM * T * 4 <= slots_end
        ofac = at("ofac", [128, HD, T], f32, RV)
        assert HD * T <= 6 * D
        qkv = at("qkv", [128, 3 * DT, T], f32, R)
        assert R + 3 * TB4 <= RQ + TB4
        Pat = [at(f"Pat{i}", [128, 2, NP_], f32, R + 2 * TB4 + 2 * NP_ * 4 * i if i < 2 else slots + 24576)
               for i in range(3)]
        q4 = at("q4", [128, 2, 32], f32, slots + 24576 + 2 * NP_ * 4)
        qz = at("qz", [128, 2, 2, T], f32, R + 2 * TB4 + 4 * NP_ * 4)
        assert (4 * NP_ + 4 * T) * 4 <= TB4
        Qbd = at("Qbd", [128, NB, HD, 64], f32, R + 2 * TB4)
        trig = at("trig", [128, 2, T], f32, RW)
        AT = at("AT", [128, 5, NP_], f32, RW)
        AT3 = at("AT3", [128, 2, 3, NS], f32, RW)
        Psm = at("Psm", [64, 2, PAST + NS], f32, RW + 1024)
        KT4 = 4 * (PAST + NS) * 4
        KT = [[at(f"KT{b}{i}", [128, 4, PAST + NS], f32, o) for i, o in enumerate(where)] for b, where in
              enumerate(((slots + 24576, slots + 24576 + KT4), (R - 256 - 3 * T * 4, RW + 3328)))]
        assert slots + 24576 + 2 * KT4 <= slots_end and KT4 <= 3 * T * 4 and 3328 + KT4 <= 5 * T * 4
        o_hi = at("o_hi", [128, DT, T], f32r, R + TB4)
        o_lo = at("o_lo", [128, DT, T], f32r, R + 2 * TB4)
        m_hi = at("m_hi", [128, DT, T], f32r, R)
        m_lo = at("m_lo", [128, DT, T], f32r, RV)
        assert RW + 5 * T * 4 + 2048 + 64 <= REND, (RW + 5 * T * 4 + 2112, REND)
        assert R + 2 * FT * T * 4 <= REND

        ps = ctx.enter_context(nc.psum_tensor("ps", [128, 8, 512], f32))

        neglam = small[:, 0:1]
        mv = small[0:64, 1:2]
        bgate = small[0:HM, 2:4]
        lam2 = small[0:1, 4:7]
        m0row = small[0:HM, 8:16]
        mout = small[0:HM, 16:25]
        gsub = small[:, 25:26]
        rowmax = small[:, 26:34]
        rowsum = small[:, 34:42]
        rinv = small[:, 42:50]
        mq = small[0:32, 58:59]
        srm = small[0:64, 50:56]
        acol = small2[:, 0:48].rearrange("p (k w h) -> p k w h", k=6, w=2)
        wrow = small2[0:HM, 48:80]
        wlast = wrow.rearrange("p (b t) -> p b t", t=DSEQ)[:, :, DSEQ - 1]
        wbc = small2[:, 80:208].rearrange("p (h s) -> p h s", h=HM)
        dec8 = small2[0:NB, 208:212]
        nT = small2[:, 244:308].rearrange("p (k s) -> p k s", k=2)
        qs = at("qs", [128, DT, NS], f32, slots + 31744)
        nqs = tB[:, 0:256].rearrange("p (i s) -> p i s", i=DT)
        inter = tB[:, 256:512].rearrange("p (i s) -> p i s", i=DT)
        assert slots + 31744 + 1024 <= slots_end

        ident = con[:, C_ID:C_ID + 128]

        def sem(name):
            return ctx.enter_context(nc.semaphore(name))

        pe_stage, act_stage, dve_stage = sem("pe_stage"), sem("act_stage"), sem("dve_stage")
        loaded = [sem(f"loaded{s}") for s in range(2)]
        hi_done = [sem(f"hi_done{s}") for s in range(2)]
        lo_done = [sem(f"lo_done{s}") for s in range(2)]
        mm_done = [sem(f"mm_done{s}") for s in range(2)]
        ring_full, ring_act, ring_dve = sem("ring_full"), sem("ring_act"), sem("ring_dve")
        evac = [sem(f"evac{s}") for s in range(2)]
        tile_hi, tile_lo, om_prod = sem("tile_hi"), sem("tile_lo"), sem("om_prod")
        act_step, dve_step = sem("act_step"), sem("dve_step")

        def panel(w, row0, nk, col):
            return w[row0:row0 + 128 * nk, bass.ds(col, 128)].rearrange("(k p) n -> p k n", p=128)

        win = ins["w_in"][0]

        in_c = sem("in_c")

        class Phase:
            def __init__(self, name, n, nk, w, width, col=(0, 0), row=(0, 0)):
                self.n, self.nk, self.w, self.width, self.col, self.row = n, nk, w, width, col, row

        def feed_forward(tag):
            wg, wu, wd = (ins[f"ffn{tag}_{x}"][0] for x in ("w_gate", "w_up", "w_down"))
            return (Phase(f"up{tag}", FT, DT, (wg, wu), 128),
                    Phase(f"down{tag}", DT, KD, (wd, wd), 128, row=(0, KD * 128)))

        def two_tiles(name, n, w, off):
            return Phase(name, n, DT, (w, w), 256, (off, off + 128))

        up1, down1 = feed_forward(1)
        up2, down2 = feed_forward(2)
        p_xm = two_tiles("xm", DT // 2, win, OFF_XM)
        p_om = two_tiles("om", DT // 2, win, OFF_OM)
        p_qkv = two_tiles("qkv", 3 * DT // 2, win, OFF_QKV)
        p_wo = two_tiles("wo", DT // 2, ins["w_out"][0], 0)
        p_a = Phase("pa", DT, DT, (win, ins["w_proj_a"][0]), 128, (OFF_GA, 0))
        p_b = Phase("pb", DT, DT, (win, ins["w_proj_b"][0]), 128, (OFF_GB, 0))
        order = [up1, down1, p_xm, p_om, p_a, p_qkv, p_b, p_wo, up2, down2]
        panels = evs = los = 1
        his = 0
        for i, p in enumerate(order):
            p.before, panels = panels, panels + p.n
            p.ev0, evs = evs, evs + (p.n // 2 if p in (down1, down2) else p.n)
            p.lo0, los = los, los + {up1: 1, up2: 1, p_om: 2, p_b: 2}.get(p, 0) * p.n
            p.hi0, his = his, his + (p.n if p in (up1, up2, p_b) else 0)
            p.next = order[i + 1] if i + 1 < len(order) else None
        def late(p):
            return p in (p_om, p_b)

        def load(sp, p, j, s):
            col = j * p.width + p.col[s]
            if not isinstance(j, int):
                col = sp.snap(col)
            sp.wait_ge(lo_done[s], j + p.before)
            sp.dma_start(raw[s][:, 0:p.nk, :], panel(p.w[s], p.row[s], p.nk, col)).then_inc(loaded[s], 16)

        def split_hi(act, p, j, s):
            act.wait_ge(loaded[s], (j + p.before) * 16)
            act.wait_ge(mm_done[s], j + p.before)
            act.activation(w_hi[s][:, 0:p.nk, :], raw[s][:, 0:p.nk, :], ACT.Copy).then_inc(hi_done[s], 1)

        def split_lo(v, p, j, s):
            v.wait_ge(hi_done[s], j + p.before)
            v.tensor_tensor(w_lo[s][:, 0:p.nk, :], raw[s][:, 0:p.nk, :],
                            w_hi[s][:, 0:p.nk, :].bitcast(f32), ALU.subtract).then_inc(lo_done[s], 1)

        def first_products(pe, p, r):
            for s in range(2):
                pe.wait_ge(evac[s], p.ev0)
                pe.wait_ge(lo_done[s], p.before + 1)
            for k in range(DT):
                pe.wait_ge(xlo_done, DT * r + k + 1)
                for s in range(2):
                    for half in range(2):
                        cols = slice(half * H2, (half + 1) * H2)
                        for a, (w, x) in enumerate(((w_hi, xn_hi), (w_hi, xn_lo), (w_lo, xn_hi))):
                            mm = pe.matmul(ps[:, 2 * s + half, 0:H2], w[s][:, k, :], x[:, k, cols],
                                           start=k == 0 and a == 0, stop=k == DT - 1 and a == 2)
                    if k == DT - 1:
                        mm.then_inc(mm_done[s], 1)

        def product(pe, p, j, s, bank, x_hi, x_lo, k0=0, first=True, last=True, tiles=None):
            pe.wait_ge(lo_done[s], j + (p.before + 1))
            for half in range(2):
                cols = slice(half * H2, (half + 1) * H2)
                for k in range(p.nk):
                    if tiles is not None and half == 0:
                        pe.wait_ge(tiles, k + 1)
                    for a, (w, x) in enumerate(((w_hi, x_hi), (w_hi, x_lo), (w_lo, x_hi))):
                        mm = pe.matmul(ps[:, bank + half, 0:H2], w[s][:, k, :], x[:, k0 + k, cols],
                                       start=first and k == 0 and a == 0,
                                       stop=last and k == p.nk - 1 and a == 2)
            mm.then_inc(mm_done[s], 1)

        def two(bank):
            return ps[:, bank:bank + 2, 0:H2]

        def tok(t):
            return t.rearrange("p (b n) -> p b n", b=2)

        def dyn(t, j):
            return t[:, bass.ds(j, 1), :].rearrange("p o (b n) -> p (o b) n", b=2)

        def loop(eng, p, body, step=1, first=0):
            n = p.n // step
            with eng.Fori(first, n - 1) as j:
                body(j, p, j + 1)
            body(n - 1, *((p.next, 0) if p.next is not None and not late(p.next) else (None, 0)))

        STAGES = ["load", "norm1", "up1", "down1", "norm2", "xm", "project", "states", "heads", "om",
                  "a_qkv", "rotary", "attend", "sample", "subln", "b", "out", "norm3", "up2", "down2", "last"]

        def begin(eng, name):
            for s in (pe_stage, act_stage, dve_stage):
                eng.wait_ge(s, STAGES.index(name))

        def end(eng, s):
            eng.drain().then_inc(s, 1)

        ROTARY = [("rope", DT), ("rope", DT + 1)]
        for i in range(6):
            ROTARY += [("v", i), ("rope", DT + 2 + i)]
        for i in range(6):
            ROTARY += [("rope", i), ("k", i)]
        ROTARY += [("rope", 6), ("rope", 7)]

        RING = {
            "load": ["a" if i % 2 else "d" for i in range(DT)] + ["d"],
            "project": (["d"] + ["a"] * 6 + ["a"] + ["d"]
                        + ["a", "a"] * DT + ["d"] * 6),
            "states": ["a"],
            "rotary": ["d" if kind == "rope" else "a" for kind, _ in ROTARY],
            "sample": (["a", "d", "a", "d", "a"] + ["a", "d", "a", "d", "d", "a", "d"] * (NB - 1) + ["d", "d"]),
            "subln": ["a"] * HD,
            "last": ["a", "d", "a", "d", "a"],
        }
        jobs, first_job = [], {}
        for key, who in RING.items():
            first_job[key] = len(jobs)
            jobs += who

        def ring_bank(n):
            return 2 * (n % 4)

        def key_job(b):
            return first_job["sample"] + (7 * b - 2 if b else 0)

        def score_job(b):
            return key_job(b) + (5 if b else 4)

        def at_job(b):
            return key_job(b + 1) + 4 if b < NB - 1 else key_job(b) + 7

        def out_job(b):
            return at_job(b) + (2 if b < NB - 1 else 1)

        PAGES = [(0, 0), (0, 1)]
        for b in range(2, NB):
            PAGES += [(1, b - 2), (0, b)]
        PAGES += [(1, NB - 2), (1, NB - 1)]

        def page_slot(item):
            return PAGES.index(item) % 3

        def page_wait(pe, item):
            i = PAGES.index(item)
            pe.wait_ge(in_page_slot[i % 3], 32 * (i // 3 + 1))

        def ring_done(eng, n):
            eng.wait_ge(ring_act if jobs[n] == "a" else ring_dve, jobs[:n + 1].count(jobs[n]))

        def ring_free(pe, n):
            if n >= 4:
                ring_done(pe, n - 4)

        def ring_wait(eng, n):
            eng.wait_ge(ring_full, n + 1)
            return ring_bank(n)

        def wide(bank, rows_, cols):
            return ps[0:rows_, bank:bank + 2, :].rearrange("p b n -> p (b n)")[:, 0:cols]

        in_x, in_small = sem("in_x"), sem("in_small")
        in_mv = sem("in_mv")
        in_g, in_mlw, in_page, in_sc = sem("in_g"), sem("in_mlw"), sem("in_page"), sem("in_sc")
        in_state = [sem(f"in_state{i}") for i in range(4)]
        in_page_slot = [sem(f"in_page_slot{i}") for i in range(3)]
        in_n, in_trig = sem("in_n"), sem("in_trig")
        stored = sem("stored")
        st_state = [sem(f"st_state{i}") for i in range(4)]
        st_k = [sem(f"st_k{i}") for i in range(2)]
        st_c = sem("st_c")
        ones_ready, lam_row, lam_exp, lam_neg = sem("ones_ready"), sem("lam_row"), sem("lam_exp"), sem("lam_neg")
        sq_ready, sq_used, rstd_ready = sem("sq_ready"), sem("sq_used"), sem("rstd_ready")
        xt_ready, xhi_ready = sem("xt_ready"), sem("xhi_ready")
        xlo_done, olo_done = sem("xlo_done"), sem("olo_done")
        gw_zero, ghi, glo, gates_full, gates_read = (sem("gw_zero"), sem("ghi"), sem("glo"), sem("gates_full"),
                                                     sem("gates_read"))
        xs_ready, cvt_ready, conv_ready, c_ready = sem("xs_ready"), sem("cvt_ready"), sem("conv_ready"), sem("c_ready")
        row_arg, row_fun, m_ready = sem("row_arg"), sem("row_fun"), sem("m_ready")
        qs_ready, kwb_ready = sem("qs_ready"), sem("kwb_ready")
        ct_full, ct_ready, cu_full, c_new, iq_full = sem("ct_full"), sem("ct_ready"), sem("cu_full"), sem("c_new"), sem("iq_full")
        nn_full, n_new, nf_full, n_fin, cf_full, c_fin = (sem("nn_full"), sem("n_new"), sem("nf_full"), sem("n_fin"),
                                                          sem("cf_full"), sem("c_fin"))
        bM_full, bM_ready, bm_full, bm_ready = sem("bM_full"), sem("bM_ready"), sem("bm_full"), sem("bm_ready")
        wt_ready, we_ready, om_gated = sem("wt_ready"), sem("we_ready"), sem("om_gated")
        sc_full, p_ready, num_full, sqh_ready = sem("sc_full"), sem("p_ready"), sem("num_full"), sem("sqh_ready")
        ssh_full, u_ready, ln_ready, fac_ready, hm_ready = (sem("ssh_full"), sem("u_ready"), sem("ln_ready"),
                                                            sem("fac_ready"), sem("hm_ready"))
        rot_ready, qz_ready, s_full, max_ready, e_ready = (sem("rot_ready"), sem("qz_ready"), sem("s_full"),
                                                           sem("max_ready"), sem("e_ready"))
        a_ready, at_full, at_ready, o_full, o_ready = (sem("a_ready"), sem("at_full"), sem("at_ready"),
                                                       sem("o_full"), sem("o_ready"))
        qbd_ready, smax_ready, sp_ready = sem("qbd_ready"), sem("smax_ready"), sem("sp_ready")
        osq_ready, ofac_ready, on_ready, ohi_ready = sem("osq_ready"), sem("ofac_ready"), sem("on_ready"), sem("ohi_ready")
        t2 = [tA, tB]
        FINAL = (7, 0, 1, 0)
        pairs = [(h, b) for h in range(HM) for b in range(NB)]
        block = ctx.enter_context(nc.Block())

        @block.sync
        def _(sp):
            xp = ins["x_prompt"][0]
            sp.dma_start(con[:, :], const_ap[:, 0:C_N]).then_inc(in_c, 16)
            sp.dma_start(xtok[0:16, 0, :], ins["meta_tokens"]).then_inc(in_x, 16)
            sp.dma_start(xtok[16:112, 0, :], xp[0:96, :]).then_inc(in_x, 16)
            for t in range(1, 4):
                sp.dma_start(xtok[:, t, :], xp[112 * t - 16:112 * t + 96, :]).then_inc(in_x, 16)
            sp.dma_start(xtok[0:80, 4, :], xp[432:512, :]).then_inc(in_x, 16)
            sp.dma_start(xtok[80:112, 4, :], ins["x_sample"].rearrange("b t d -> (b t) d")).then_inc(in_x, 16)
            for col, a in ((G_FFN1, ins["ffn1_norm"][0]), (G_MIX, ins["mix_norm"][0]),
                           (G_FFN2, ins["ffn2_norm"][0]), (G_FINAL, ins["final_norm"]),
                           (G_CB, ins["conv_b"][0])):
                sp.dma_start(vecs[col:col + 8, :], a.rearrange("(i p) -> i p", p=128)).then_inc(in_small, 16)
            sp.dma_start(vecs[G_CW:G_CW + 32, :],
                         ins["conv_w"][0].rearrange("j (i p) -> (j i) p", p=128)).then_inc(in_small, 16)
            sp.dma_start(vecs[G_ML:G_ML + 8, :],
                         ins["mlstm_norm"][0].rearrange("h (i p) -> (h i) p", p=128)).then_inc(in_small, 16)
            sp.dma_start(vecs[G_SUB:G_SUB + 1, :], ins["subln"]).then_inc(in_small, 16)
            for i, name in enumerate(("lambda_q1", "lambda_k1", "lambda_q2", "lambda_k2")):
                sp.dma_start(lrow[0:1, i, :], ins[name]).then_inc(in_small, 16)
            with nc.allow_non_contiguous_dma(reason="a few words"):
                sp.dma_start(bgate[:, 0:1], ins["b_igate"].rearrange("a h -> h a")).then_inc(in_small, 16)
                sp.dma_start(bgate[:, 1:2], ins["b_fgate"].rearrange("a h -> h a")).then_inc(in_small, 16)
                sp.dma_start(m0row, ins["state_m"][0].rearrange("b h -> h b")).then_inc(in_small, 16)

            def stream(p, first=0):
                with sp.Fori(first, p.n) as j:
                    load(sp, p, j, 0)
                    load(sp, p, j, 1)

            def stream_short(p):
                for j in range(p.n):
                    load(sp, p, j, 0)
                    load(sp, p, j, 1)

            stream(up1)
            stream(down1)
            load(sp, p_xm, 0, 0)
            load(sp, p_xm, 0, 1)
            begin(sp, "norm2")
            sp.wait_ge(gw_zero, 1)
            for c, o in ((0, OFF_GATE), (32, OFF_GATE + HM)):
                sp.dma_start(gw[:, :, c:c + HM],
                             win[:, o:o + HM].rearrange("(k p) n -> p k n", p=128)).then_inc(in_g, 16)
            stream(p_xm, 1)
            sp.dma_start(sconv[:, :], ins["state_conv"][0].rearrange("b j d -> (b j) d")).then_inc(in_sc, 16)
            sp.dma_start(page_sb[0:1, :], ins["page_table"].rearrange("b g -> (b g)").unsqueeze(0)).then_inc(in_page, 16)

            def load_state(n):
                h, b = pairs[n]
                if n >= 4:
                    sp.wait_ge(st_state[n % 4], 16 * (n // 4))
                sp.dma_start(Cb[:, n % 4, :, :], ins["state_C"][0, b, h].rearrange("(v p) k -> p v k", p=128)
                             ).then_inc(in_state[n % 4], 16)

            for s in range(2):
                sp.wait_ge(lo_done[s], p_xm.before + p_xm.n)
            sp.dma_start(mlw[:, 0, :, :], ins["w_mv"][0].rearrange("h (k p) n -> p (h k) n", p=128)).then_inc(in_mv, 16)
            begin(sp, "project")
            for i, name in ((1, "w_mq"), (2, "w_mk")):
                sp.dma_start(mlw[:, i, :, :], ins[name][0].rearrange("h (k p) n -> p (h k) n", p=128)).then_inc(in_mlw, 16)
            ring_done(sp, first_job["project"] + 7)
            sp.dma_start(conv_prompt[0, 0], cvo[0:3, :]).then_inc(stored, 16)
            sp.dma_start(conv_sample[0].rearrange("b j d -> (b j) d"), cvo[3:27, :]).then_inc(stored, 16)
            sp.wait_ge(m_ready, 1)
            with nc.allow_non_contiguous_dma(reason="a few words"):
                sp.dma_start(m_prompt[0].rearrange("a h -> h a"), mout[:, 0:1]).then_inc(stored, 16)
                sp.dma_start(m_sample[0].rearrange("b h -> h b"), mout[:, 1:9]).then_inc(stored, 16)
            sp.wait_ge(ring_full, first_job["project"] + 7)
            load_state(0)
            load_state(1)
            begin(sp, "states")
            sp.wait_ge(stored, 64)
            sp.dma_start(nst[:, :, :], ins["state_n"][0]).then_inc(in_n, 16)
            sp.dma_start(nrow[:, :], ins["state_n"][0].rearrange("b h d -> (b h) d")).then_inc(in_n, 16)
            for n in range(2, len(pairs) + 2):
                if n < len(pairs):
                    load_state(n)
                if n >= 2:
                    h, b = pairs[n - 2]
                    sp.wait_ge(c_new, n - 1)
                    sp.dma_start(C_sample[0, b, h].rearrange("(v p) k -> p v k", p=128),
                                 Cb[:, (n - 2) % 4, :, :]).then_inc(st_state[(n - 2) % 4], 16)
            sp.wait_ge(n_new, 1)
            sp.dma_start(n_sample[0], nst[:, :, :]).then_inc(stored, 16)
            for h in range(HM):
                sp.wait_ge(c_fin, h + 1)
                sp.dma_start(C_prompt[0, 0, h].rearrange("(v p) k -> p v k", p=128), cpo[:, h, :, :]).then_inc(st_c, 16)
            sp.wait_ge(n_fin, 1)
            sp.dma_start(n_prompt[0].rearrange("a h d -> a (h d)"), npo[:, :]).then_inc(stored, 16)
            for i in range(4):
                sp.wait_ge(st_state[i], 16 * len(pairs) // 4)
            sp.wait_ge(st_c, 16 * HM)
            sp.wait_ge(stored, 16 * 6)
            begin(sp, "heads")
            stream(p_om)
            stream_short(p_a)
            begin(sp, "om")
            sp.dma_start(trig[:, :, :], const_ap[:, C_COS:C_ALL].rearrange("p (c t) -> p c t", c=2)).then_inc(in_trig, 16)
            stream(p_qkv)
            for part in range(2):
                for i, (t0, n) in enumerate(BLOCKS):
                    ring_done(sp, first_job["rotary"] + ROTARY.index(("vk"[part], i)))
                    if part == 0:
                        dst = v_prompt[0, 0, t0:t0 + n] if i < 5 else v_sample[0].rearrange("b t h d -> (b t) h d")
                        sp.dma_start(dst.rearrange("t h d -> t (h d)"), vtok[0:n, i, :]).then_inc(stored, 16)
                    else:
                        dst = k_prompt[0, 0, t0:t0 + n] if i < 5 else k_sample[0].rearrange("b t h d -> (b t) h d")
                        sp.dma_start(dst.rearrange("t h d -> t (h d)"), kout[0:n, i % 2, :]).then_inc(st_k[i % 2], 16)
            sp.wait_ge(st_k[0], 48)
            sp.wait_ge(st_k[1], 48)
            begin(sp, "attend")
            sp.wait_ge(in_page, 16)

            def page(b, g):
                return bass.ds(sp.value_load(page_sb[0:1, 2 * b + g:2 * b + g + 1], min_val=0, max_val=N_POOL - 1), 1)

            for i, (is_v, b) in enumerate(PAGES):
                if i >= 3:
                    was_v, c = PAGES[i - 3]
                    sp.wait_ge(ring_full, out_job(c) + 1 if was_v else key_job(c) + 4)
                for g in range(2):
                    sp.dma_start(pages[:, i % 3, g, :], ins["cache_v" if is_v else "cache_k"][0][page(b, g)]
                                 .rearrange("o t h d -> (o t) (h d)")).then_inc(in_page_slot[i % 3], 16)
            begin(sp, "subln")
            stream_short(p_b)
            stream(p_wo)
            stream(up2)
            stream(down2)
            for t in range(5):
                ring_done(sp, first_job["last"] + t)
                if t == 0:
                    sp.dma_start(y_prompt[0, 0:96, :], xtok[16:112, 0, :]).then_inc(stored, 16)
                elif t < 4:
                    sp.dma_start(y_prompt[0, 112 * t - 16:112 * t + 96, :], xtok[:, t, :]).then_inc(stored, 16)
                else:
                    sp.dma_start(y_prompt[0, 432:512, :], xtok[0:80, 4, :]).then_inc(stored, 16)
                    sp.dma_start(y_sample.rearrange("b t d -> (b t) d"), xtok[80:112, 4, :]).then_inc(stored, 16)
            sp.wait_ge(stored, 16 * (6 + 6 + 6))

        @block.tensor
        def _(pe):
            def transpose(out, in_, k):
                return pe.transpose(out, in_, con[0:k, C_ID:C_ID + k])

            def transpose8(n, in_of, nt, k=128):
                for i in range(DT):
                    mm = transpose(ps[0:nt, ring_bank(n) + i // 4, 128 * (i % 4):128 * (i % 4) + 128], in_of(i), k)
                mm.then_inc(ring_full, 1)

            def norm(r):
                for i in range(DT):
                    pe.wait_ge(sq_ready, DT * r + i + 1)
                    for half in range(2):
                        mm = pe.matmul(ps[:, 4 + half, 0:H2], ones[:, :], t2[i % 2][:, half * H2:(half + 1) * H2],
                                       start=i == 0, stop=i == DT - 1)
                    mm.then_inc(sq_used, 1)

            def up(p, r):
                first_products(pe, p, r)

                def body(j, _q, _jn):
                    pe.wait_ge(evac[0], j + p.ev0)
                    product(pe, p, j, 0, 0, xn_hi, xn_lo)
                    pe.wait_ge(evac[1], j + p.ev0)
                    product(pe, p, j, 1, 2, xn_hi, xn_lo)
                loop(pe, p, body, first=1)

            def down(p):
                def body(j, _q, _jn):
                    for e in range(2):
                        pe.wait_ge(evac[e], j + p.ev0)
                        product(pe, p, j * 2 + e, 0, 2 * e, h_hi, h_lo, 0, True, False)
                        product(pe, p, j * 2 + e, 1, 2 * e, h_hi, h_lo, KD, False, True)
                loop(pe, p, body, 2)

            def pair(p, xs_, first=0):
                def body(j, _q, _jn):
                    for s in range(2):
                        pe.wait_ge(evac[s], j + p.ev0)
                        product(pe, p, j, s, 2 * s, *xs_[s])
                loop(pe, p, body, first=first)

            xn = (xn_hi, xn_lo)

            for s in range(2):
                pe.drain().then_inc(mm_done[s], 1)
            pe.wait_ge(in_c, 16)
            pe.wait_ge(in_x, 16 * 7)
            for i in range(DT):
                ring_free(pe, i)
                for t in range(5):
                    mm = transpose(ps[:, ring_bank(i) + t // 4, 112 * (t % 4):112 * (t % 4) + 112],
                                   xtok[:, t, 128 * i:128 * i + 128], 112)
                mm.then_inc(ring_full, 1)
            ring_free(pe, DT)
            pe.wait_ge(in_small, 16 * 15)
            transpose(ps[:, ring_bank(DT), 0:G_N], vecs[:, :], G_N)
            pe.wait_ge(ones_ready, 1)
            pe.wait_ge(lam_neg, 1)
            pe.matmul(ps[:, ring_bank(DT) + 1, 0:1], ones[0:1, :], lam2[:, 2:3], start=True, stop=True).then_inc(ring_full, 1)
            end(pe, pe_stage)

            begin(pe, "norm1")
            norm(0)
            end(pe, pe_stage)
            up(up1, 0)
            end(pe, pe_stage)
            begin(pe, "down1")
            down(down1)
            end(pe, pe_stage)
            begin(pe, "norm2")
            norm(1)
            end(pe, pe_stage)

            first_products(pe, p_xm, 1)
            pair(p_xm, (xn, xn), first=1)
            pe.wait_ge(glo, 1)
            for half in range(2):
                cols = slice(half * H2, (half + 1) * H2)
                for k in range(DT):
                    for a, (w, x) in enumerate(((gw_hi, xn_hi), (gw_hi, xn_lo), (gw_lo, xn_hi))):
                        mm = pe.matmul(ps[0:36, 4 + half, 0:H2], w[:, k, :], x[:, k, cols],
                                       start=k == 0 and a == 0, stop=k == DT - 1 and a == 2)
            mm.then_inc(gates_full, 1)
            end(pe, pe_stage)

            begin(pe, "project")
            n = first_job["project"]
            ring_free(pe, n)
            pe.wait_ge(in_sc, 16)
            pe.wait_ge(gates_read, 2)
            for i in range(DT):
                mm = transpose(ps[:, ring_bank(n), 24 * i:24 * i + 24], sconv[:, 128 * i:128 * i + 128], 24)
            mm.then_inc(ring_full, 1)
            n += 1
            pe.wait_ge(in_mv, 16)
            for blk, (t0, nt) in enumerate(BLOCKS):
                ring_free(pe, n)
                if blk == 5:
                    pe.wait_ge(xs_ready, 1)
                for h in range(HM):
                    for k in range(2):
                        i = 2 * h + k
                        x = E[:, i, 3 + t0:3 + t0 + nt] if blk < 5 else xs[:, i, :]
                        mm = pe.matmul(ps[0:nt, ring_bank(n) + h // 2, DHM * (h % 2):DHM * (h % 2) + DHM],
                                       x, mlw[:, 0, i, :], start=k == 0, stop=k == 1)
                mm.then_inc(ring_full, 1)
                n += 1
            ring_free(pe, n)
            pe.wait_ge(cvt_ready, 1)
            transpose8(n, lambda i: cvt[:, i, :], 27)
            n += 1
            ring_free(pe, n)
            pe.wait_ge(row_fun, 4)
            for blk, (t0, nt) in enumerate(BLOCKS):
                for w, r in enumerate((1, 0)):
                    transpose(ps[0:nt, ring_bank(n), 8 * blk + 4 * w:8 * blk + 4 * w + 4], rows[:, r, t0:t0 + nt], HM)
            transpose(ps[0:NB, ring_bank(n), 64:68], wlast, HM)
            for h in range(HM):
                mm = pe.matmul(ps[:, ring_bank(n) + 1, 32 * h:32 * h + 32],
                               con[0:HM, C_SEL + 128 * h:C_SEL + 128 * h + 128], wrow, start=True, stop=True)
            mm.then_inc(ring_full, 1)
            n += 1
            pe.wait_ge(in_mlw, 32)
            for i in range(DT):
                h, m = i // 2, i % 2
                pe.wait_ge(c_ready, 2 * h + 2)
                for w in range(2):
                    ring_free(pe, n)
                    for half in range(2):
                        for k in range(2):
                            mm = pe.matmul(ps[:, ring_bank(n) + half, 0:H2],
                                           mlw[:, 1 + w, 2 * h + k, 128 * m:128 * m + 128],
                                           cc[:, 2 * h + k, half * H2:(half + 1) * H2], start=k == 0, stop=k == 1)
                    mm.then_inc(ring_full, 1)
                    n += 1
            ring_done(pe, n - 1)
            for blk, (t0, nt) in enumerate(BLOCKS):
                ring_free(pe, n)
                transpose8(n, lambda i: km[:, i, t0:t0 + nt], nt)
                n += 1
            end(pe, pe_stage)

            begin(pe, "states")
            pe.wait_ge(in_n, 32)
            for k in range(2):
                mm = transpose(ps[:, ring_bank(n), 32 * k:32 * k + 32], nrow[:, 128 * k:128 * k + 128], NS)
            mm.then_inc(ring_full, 1)
            ring_done(pe, n)
            pe.wait_ge(qs_ready, 1)

            def state_q(n):
                h, b = pairs[n]
                pe.wait_ge(ct_ready, n + 1)
                for vt in range(2):
                    for kt in range(2):
                        c0 = NS * (2 * h + vt) + DSEQ * b
                        mm = pe.matmul(ps[:, 6, c0:c0 + DSEQ], CT[:, n % 2, kt, 128 * vt:128 * vt + 128],
                                       qs[:, 2 * h + kt, DSEQ * b:DSEQ * b + DSEQ], start=kt == 0, stop=kt == 1)
                mm.then_inc(iq_full, 1)

            for n, (h, b) in enumerate(pairs):
                pe.wait_ge(in_state[n % 4], 16 * (n // 4 + 1))
                if n >= 2:
                    pe.wait_ge(ct_ready, n - 1)
                for vt in range(2):
                    for kt in range(2):
                        c0 = kt * DHM + vt * 128
                        mm = transpose(ps[:, n % 2, c0:c0 + 128], Cb[:, n % 4, vt, 128 * kt:128 * kt + 128], 128)
                mm.then_inc(ct_full, 1)
                if n >= 2:
                    pe.wait_ge(c_new, n - 1)
                pe.wait_ge(kwb_ready, n + 1)
                for vt in range(2):
                    mm = pe.matmul(ps[:, 2 + n % 2, DHM * vt:DHM * vt + DHM],
                                   vtok[:, 5, DHM * h + 128 * vt:DHM * h + 128 * vt + 128],
                                   kwb[h % 2][:, b, :], start=True, stop=True)
                mm.then_inc(cu_full, 1)
                if n >= 1:
                    state_q(n - 1)
            state_q(len(pairs) - 1)
            for half in range(2):
                mm = pe.matmul(ps[0:NB, 4 + half, :], con[0:NS, C_BM:C_BM + NB],
                               ktok[0:NS, 5, 512 * half:512 * half + 512], start=True, stop=True)
            mm.then_inc(nn_full, 1)
            for h in range(HM):
                if h == 3:
                    pe.wait_ge(c_fin, 2)
                for vt in range(2):
                    for blk in range(5):
                        nt = 128
                        mm = pe.matmul(ps[:, FINAL[h], DHM * vt:DHM * vt + DHM],
                                       vtok[0:nt, blk, DHM * h + 128 * vt:DHM * h + 128 * vt + 128],
                                       ktok[0:nt, blk, DHM * h:DHM * h + DHM], start=blk == 0, stop=blk == 4)
                mm.then_inc(cf_full, 1)
            pe.wait_ge(n_new, 1)
            for half in range(2):
                for blk in range(5):
                    nt = BLOCKS[blk][1]
                    mm = pe.matmul(ps[0:1, 4 + half, :], ones[0:nt, 0:1],
                                   ktok[0:nt, blk, 512 * half:512 * half + 512], start=blk == 0, stop=blk == 4)
            mm.then_inc(nf_full, 1)
            end(pe, pe_stage)

            begin(pe, "heads")

            def spread(h, row):
                for half in range(2):
                    mm = pe.matmul(ps[:, half, 0:H2], con[0:HM, C_SEL + 128 * h:C_SEL + 128 * h + 128],
                                   rows[:, row, half * H2:(half + 1) * H2], start=True, stop=True)
                return mm

            for h in range(HM):
                if h == 0:
                    spread(0, 2).then_inc(bM_full, 1)
                    pe.wait_ge(bM_ready, 1)
                else:
                    pe.wait_ge(u_ready, h)

                def score(out, blk, q0, nq):
                    t0, nt = BLOCKS[blk]
                    for k in range(2):
                        mm = pe.matmul(out, km[:, 2 * h + k, t0:t0 + nt], qm[:, 2 * h + k, q0:q0 + nq],
                                       start=k == 0, stop=k == 1)
                    return mm
                score(ps[:, 0, 0:SPLIT], 0, 0, SPLIT)
                score(ps[:, 1, 0:NP_ - SPLIT], 0, SPLIT, NP_ - SPLIT).then_inc(sc_full, 1)
                for blk in range(1, 6):
                    t0, nt = BLOCKS[blk]
                    nq = NP_ - t0 if blk < 5 else NS
                    pe.wait_ge(p_ready, 6 * h + max(blk - 1, 1))
                    score(ps[0:nt, (blk + 1) % 2, 0:nq], blk, t0, nq).then_inc(sc_full, 1)
                if h >= 1:
                    pe.wait_ge(hm_ready, h)
                for blk, (t0, nt) in enumerate(BLOCKS):
                    pe.wait_ge(p_ready, 6 * h + blk + 1)
                    if blk == 3:
                        pe.wait_ge(p_ready, 6 * h + 6)
                        spread(h, 3).then_inc(bm_full, 1)
                    if blk == 5 and h + 1 < HM:
                        pe.wait_ge(bm_ready, h + 1)
                        spread(h + 1, 2).then_inc(bM_full, 1)
                    for o in range(3):
                        w = vtok[0:nt, blk, DHM * h + 128 * o:DHM * h + 128 * o + 128] if o < 2 else ones[0:nt, :]
                        b = 2 + 2 * o
                        if blk == 5:
                            out = ps[:, b + 1, NP_ - SPLIT:T - SPLIT]
                            pe.matmul(out, w, P6[0:nt, WOFF[5]:WOFF[5] + NS], start=False, stop=True,
                                      skip_group_check=True)
                            if o < 2:
                                mm = pe.matmul(out, ident, inter[:, 2 * h + o, :], start=False, stop=True,
                                               skip_group_check=True)
                            else:
                                for k in range(2):
                                    mm = pe.matmul(out, ones[:, :], nqs[:, 2 * h + k, :], start=False, stop=k == 1,
                                                   skip_group_check=True)
                            continue
                        if t0 < SPLIT:
                            pe.matmul(ps[:, b, t0:SPLIT], w, P6[0:nt, WOFF[blk]:WOFF[blk] + SPLIT - t0],
                                      start=blk == 0, stop=True, skip_group_check=True)
                        q0 = max(t0, SPLIT)
                        pe.matmul(ps[:, b + 1, q0 - SPLIT:NP_ - SPLIT], w,
                                  P6[0:nt, WOFF[blk] + q0 - t0:WOFF[blk] + NP_ - t0],
                                  start=blk == 0, stop=True, skip_group_check=True)
                mm.then_inc(num_full, 1)
                if h + 1 < HM:
                    pe.wait_ge(bM_ready, h + 2)
                else:
                    pe.wait_ge(bm_ready, h + 1)
                for o in range(2):
                    pe.wait_ge(sqh_ready, 2 * h + o + 1)
                    for half in range(2):
                        mm = pe.matmul(ps[:, half, 0:H2], ones[:, :], tC[:, o, half * H2:(half + 1) * H2],
                                       start=o == 0, stop=o == 1, skip_group_check=True)
                mm.then_inc(ssh_full, 1)
            end(pe, pe_stage)

            begin(pe, "om")
            pair(p_om, (xn, xn))
            end(pe, pe_stage)
            begin(pe, "a_qkv")
            pair(p_a, (xn, (hm_hi, hm_lo)))
            for s in range(2):
                pe.wait_ge(evac[s], p_a.ev0 + p_a.n)
            pair(p_qkv, (xn, xn))
            end(pe, pe_stage)

            begin(pe, "rotary")
            n = first_job["rotary"]
            for kind, i in ROTARY:
                if kind == "k":
                    pe.wait_ge(rot_ready, DT)
                ring_free(pe, n)
                if kind == "rope":
                    for half in range(2):
                        mm = pe.matmul(ps[:, ring_bank(n) + half, 0:H2], con[:, C_ROT:C_ROT + 128],
                                       qkv[:, i, half * H2:(half + 1) * H2], start=True, stop=True)
                    mm.then_inc(ring_full, 1)
                else:
                    t0, nt = BLOCKS[i]
                    tile = 2 * DT if kind == "v" else DT
                    transpose8(n, lambda f: qkv[:, tile + f, t0:t0 + nt], nt)
                n += 1
            end(pe, pe_stage)

            begin(pe, "attend")
            def scores(g):
                h, i = divmod(g, 5)
                q0, nq = BLOCKS[i]
                nk = q0 + nq
                pe.wait_ge(qz_ready, h + 1)
                if i < 2 and h >= 1:
                    pe.wait_ge(e_ready, g - 2)
                elif i in (2, 3):
                    pe.wait_ge(e_ready, g - 1)
                elif i == 4 and h >= 1:
                    pe.wait_ge(o_ready, h)
                if i == 4:
                    pe.matmul(ps[0:32, 6, 0:264], q4[:, h % 2, :], qkv[:, DT + h, 0:264], start=True, stop=True)
                    pe.matmul(ps[0:32, 7, 0:264], q4[:, h % 2, :], qkv[:, DT + h, 264:NP_], start=True, stop=True)
                    pe.matmul(ps[0:32, 7, 248:264], con[0:16, C_Q:C_Q + 32], con[0:16, C_NEG:C_NEG + 16],
                              start=False, stop=True, skip_group_check=True).then_inc(s_full, 1)
                    return
                for m in range(2):
                    q = qz[:, h % 2, m, q0:q0 + nq]
                    out = ps[0:nq, 2 * (i % 2) + m, :]
                    pe.matmul(out[:, 0:nk], q, qkv[:, DT + h, 0:nk], start=True, stop=True)
                    mm = pe.matmul(out[:, q0:nk], ident, con[:, C_NEG:C_NEG + nq],
                                   start=False, stop=True, skip_group_check=True)
                mm.then_inc(s_full, 1)

            def transposed(g):
                h, i = divmod(g, 5)
                q0, nq = BLOCKS[i]
                pe.wait_ge(a_ready, g + 1)
                if g >= 2:
                    pe.wait_ge(at_ready, g - 1)
                for j in range(i + 1):
                    nk = BLOCKS[j][1]
                    if i == 4:
                        mm = pe.matmul(ps[0:nk, 4 + g % 2, nq * j:nq * j + nq],
                                       Pat[g % 3][0:32, 0, 128 * j:128 * j + nk], con[0:32, C_QT:C_QT + 16],
                                       start=True, stop=True)
                        continue
                    mm = transpose(ps[0:nk, 4 + g % 2, nq * j:nq * j + nq],
                                   Pat[g % 3][0:nq, 0, 128 * j:128 * j + nk], nq)
                mm.then_inc(at_full, 1)

            def output(h):
                pe.wait_ge(at_ready, 5 * h + 5)
                if h >= 1:
                    pe.wait_ge(o_ready, h)
                for blk in range(5):
                    t0, nt = BLOCKS[blk]
                    w = vtok[0:nt, blk, 128 * h:128 * h + 128]
                    if t0 < SPLIT:
                        pe.matmul(ps[:, 6, t0:SPLIT], w, AT[0:nt, blk, t0:SPLIT], start=blk == 0, stop=True,
                                  skip_group_check=True)
                    q0 = max(t0, SPLIT)
                    mm = pe.matmul(ps[:, 7, q0 - SPLIT:NP_ - SPLIT], w, AT[0:nt, blk, q0:NP_],
                                   start=blk == 0, stop=True, skip_group_check=True)
                mm.then_inc(o_full, 1)

            G = 5 * HD
            for g in range(G + 3):
                if g < G:
                    scores(g)
                if g >= 3 and (g - 3) % 5 == 4:
                    output((g - 3) // 5)
                if 2 <= g < G + 2:
                    transposed(g - 2)
            end(pe, pe_stage)

            begin(pe, "sample")

            def keys(b):
                n = key_job(b)
                page_wait(pe, (0, b))
                for g in range(2):
                    for q in range(2):
                        ring_free(pe, n)
                        for i in range(4):
                            hh = 4 * q + i
                            mm = transpose(ps[:, ring_bank(n), 128 * i:128 * i + 128],
                                           pages[:, page_slot((0, b)), g, 128 * hh:128 * hh + 128], 128)
                        mm.then_inc(ring_full, 1)
                        n += 1

            def score(b, hh):
                n = score_job(b)
                if hh == 0:
                    ring_free(pe, n)
                    ring_done(pe, key_job(b) + 2)
                    ring_done(pe, key_job(b) + 3)
                pe.matmul(ps[0:64, ring_bank(n), 0:PAST + NS], Qbd[:, b, hh, :], KT[b % 2][hh // 4][:, hh % 4, :],
                          start=hh == 0, stop=hh == HD - 1, skip_group_check=True)
                if hh == HD - 1:
                    pe.matmul(ps[0:64, ring_bank(n), PAST:PAST + NS], con[0:64, C_ID:C_ID + 64],
                              con[0:64, C_WM + 28 - 4 * b:C_WM + 60 - 4 * b], start=False, stop=True,
                              skip_group_check=True).then_inc(ring_full, 1)

            def probabilities(b):
                n = at_job(b)
                ring_free(pe, n)
                pe.wait_ge(sp_ready, b + 1)
                for g in range(3):
                    nk = 128 if g < 2 else NS
                    mm = pe.matmul(ps[0:nk, ring_bank(n), NS * g:NS * g + NS], Psm[:, b % 2, 128 * g:128 * g + nk],
                                   con[0:64, C_SA:C_SA + NS], start=True, stop=True)
                mm.then_inc(ring_full, 1)

            def values(b, hh):
                n = out_job(b)
                if hh == 0:
                    ring_free(pe, n)
                    ring_done(pe, at_job(b))
                    page_wait(pe, (1, b))
                for g in range(3):
                    nk = 128 if g < 2 else NS
                    w = (pages[:, page_slot((1, b)), g, 128 * hh:128 * hh + 128] if g < 2
                         else vtok[0:NS, 5, 128 * hh:128 * hh + 128])
                    mm = pe.matmul(ps[:, ring_bank(n), DSEQ * hh:DSEQ * hh + DSEQ], w,
                                   AT3[0:nk, b % 2, g, DSEQ * hh:DSEQ * hh + DSEQ], start=g == 0, stop=g == 2)
                if hh == HD - 1:
                    mm.then_inc(ring_full, 1)

            for b in range(NB + 1):
                if b < NB:
                    keys(b)
                if b >= 1:
                    probabilities(b - 1)
                if b == 0:
                    pe.wait_ge(qbd_ready, 1)
                for hh in range(HD):
                    if b < NB:
                        score(b, hh)
                    if b >= 1:
                        values(b - 1, hh)
            end(pe, pe_stage)
            n = first_job["subln"]

            begin(pe, "subln")
            for h in range(HD):
                ring_free(pe, n)
                pe.wait_ge(osq_ready, h + 1)
                for half in range(2):
                    mm = pe.matmul(ps[:, ring_bank(n) + half, 0:H2], ones[:, :], t2[h % 2][:, half * H2:(half + 1) * H2],
                                   start=True, stop=True)
                mm.then_inc(ring_full, 1)
                n += 1
            end(pe, pe_stage)

            for k in range(4):
                ring_done(pe, n - 4 + k)
            pe.wait_ge(evac[0], p_b.ev0)
            product(pe, p_b, 0, 0, 0, *xn)
            pe.wait_ge(evac[1], p_b.ev0)
            product(pe, p_b, 0, 1, 2, o_hi, o_lo, tiles=olo_done)
            pair(p_b, (xn, (o_hi, o_lo)), first=1)
            end(pe, pe_stage)
            begin(pe, "out")
            pair(p_wo, ((m_hi, m_lo), (m_hi, m_lo)))
            end(pe, pe_stage)
            begin(pe, "norm3")
            norm(2)
            end(pe, pe_stage)
            up(up2, 2)
            end(pe, pe_stage)
            begin(pe, "down2")
            down(down2)
            end(pe, pe_stage)
            begin(pe, "last")
            norm(3)
            pe.wait_ge(xt_ready, 4 * DT)
            for t in range(5):
                ring_free(pe, n)
                transpose8(n, lambda i: X[:, i, 112 * t:112 * t + 112], 112)
                n += 1

        @block.scalar
        def _(act):
            def copy(out, in_, scale=1.0):
                return act.activation(out, in_, ACT.Copy, scale=scale)

            def prepare(p, j, s):
                if p is not None:
                    split_hi(act, p, j, s)

            def norm(r, final=False, p=None):
                for i in range(DT):
                    if i == 4:
                        for s in range(2):
                            prepare(p, 0, s)
                    if i >= 2:
                        act.wait_ge(sq_used, DT * r + i - 1)
                    act.activation(t2[i % 2][:, :], X[:, i, :], ACT.Square).then_inc(sq_ready, 1)
                act.wait_ge(sq_used, DT * (r + 1))
                act.activation(tok(rstd[:, :]), two(4), ACT.Ln, bias=con[:, C_EPS:C_EPS + 1],
                               scale=1.0 / D).then_inc(rstd_ready, 1)
                act.wait_ge(rstd_ready, 2 * r + 1)
                act.activation(rstd[:, :], rstd[:, :], ACT.Exp, scale=-0.5).then_inc(rstd_ready, 1)
                if not final:
                    for i in range(DT):
                        act.wait_ge(xt_ready, DT * r + i + 1)
                        copy(xn_hi[:, i, :], t2[i % 2][:, :]).then_inc(xhi_ready, 1)

            def gated(p, func, to_hi):
                act.activation(small[0:1, 60:61], con[0:1, 0:1], func)

                def body(j, q, jn):
                    prepare(q, jn, 0)
                    act.wait_ge(mm_done[0], j + (p.before + 1))
                    act.wait_ge(evac[1], j + p.ev0)
                    act.activation(tok(tA[:, :]), two(0), func).then_inc(evac[0], 1)
                    prepare(q, jn, 1)
                    if to_hi is not None:
                        act.wait_ge(evac[1], j + (p.ev0 + 1))
                        copy(dyn(to_hi, j), tok(tB[:, :])).then_inc(tile_hi, 1)
                loop(act, p, body)

            def down(p):
                def body(j, q, jn):
                    for s in range(2):
                        split_hi(act, p, j * 2 + 1, s)
                    for s in range(2):
                        prepare(q, jn * 2, s)
                loop(act, p, body, 2)

            def plain(p, out=None):
                def body(j, q, jn):
                    prepare(q, jn, 0)
                    if out is not None:
                        act.wait_ge(mm_done[0], j + (p.before + 1))
                        out(j)
                    prepare(q, jn, 1)
                loop(act, p, body)

            def at_copy(h, i):
                q0, nq = BLOCKS[i]
                g = 5 * h + i
                act.wait_ge(at_full, g + 1)
                if i == 0 and h >= 1:
                    act.wait_ge(o_full, h)
                src = ps[:, 4 + g % 2, :]
                nj = min(i + 1, 4)
                c = copy(AT[:, 0:nj, q0:q0 + nq], src[:, 0:nq * nj].rearrange("p (j q) -> p j q", q=nq))
                if i == 4:
                    c = copy(AT[0:nq, 4, q0:q0 + nq], src[0:nq, 4 * nq:5 * nq])
                c.then_inc(at_ready, 1)

            for i in range(DT):
                if jobs[i] == "a":
                    b = ring_wait(act, i)
                    copy(X[:, i, 0:448], ps[:, b, 0:448])
                    copy(X[:, i, 448:560], ps[:, b + 1, 0:112]).then_inc(ring_act, 1)
            act.wait_ge(lam_row, 1)
            act.activation(lam2[:, 0:2], lam2[:, 0:2], ACT.Exp).then_inc(lam_exp, 1)
            end(act, act_stage)
            begin(act, "norm1")
            norm(0, p=up1)
            end(act, act_stage)
            begin(act, "up1")
            gated(up1, ACT.Silu, h_hi)
            end(act, act_stage)
            begin(act, "down1")
            down(down1)
            end(act, act_stage)
            begin(act, "norm2")
            norm(1)
            act.wait_ge(in_g, 32)
            copy(gw_hi[:, :, :], gw[:, :, :]).then_inc(ghi, 1)
            end(act, act_stage)

            begin(act, "xm")

            def xm_out(j):
                e = E[:, bass.ds(j * 2, 1), :].rearrange("p o n -> p (o n)")
                copy(e[:, 3:3 + H2], ps[:, 0, 0:H2])
                copy(e[:, 3 + H2:3 + NP_], ps[:, 1, 0:NP_ - H2])
                copy(e[:, 3 + NP_:EXT].rearrange("p (b s) -> p b s", s=7)[:, :, 3:7],
                     ps[:, 1, NP_ - H2:H2].rearrange("p (b t) -> p b t", t=DSEQ)).then_inc(evac[0], 1)
            plain(p_xm, xm_out)
            end(act, act_stage)

            begin(act, "project")
            n = first_job["project"]
            act.wait_ge(row_arg, 1)
            act.activation(rows[:, 2, :], rows[:, 2, :], ACT.Exp).then_inc(row_fun, 1)
            act.wait_ge(row_fun, 1)
            act.activation(rows[:, 2, :], rows[:, 2, :], ACT.Ln, bias=1.0).then_inc(row_fun, 1)
            act.wait_ge(row_arg, 2)
            act.activation(rows[:, 0, :], rows[:, 0, :], ACT.Exp).then_inc(row_fun, 1)
            act.activation(wrow, wrow, ACT.Exp).then_inc(row_fun, 1)
            for m in range(1, 8):
                if jobs[n + m] == "a":
                    b = ring_wait(act, n + m)
                    nt = BLOCKS[m - 1][1] if m < 7 else 27
                    copy(vtok[0:nt, m - 1, :] if m < 7 else cvo[:, :], wide(b, nt, D)).then_inc(ring_act, 1)
            for h in range(HM + 1):
                if h < HM:
                    for i in (2 * h, 2 * h + 1):
                        act.wait_ge(conv_ready, i + 1)
                        act.activation(cc[:, i, :], cc[:, i, :], ACT.Silu).then_inc(c_ready, 1)
                if h >= 1:
                    for i in (2 * h - 2, 2 * h - 1):
                        b = ring_wait(act, n + 9 + 2 * i)
                        copy(tok(qm[:, i, :]), two(b)).then_inc(ring_act, 1)
                        b = ring_wait(act, n + 10 + 2 * i)
                        copy(tok(km[:, i, :]), two(b), DHM ** -0.5).then_inc(ring_act, 1)
            end(act, act_stage)

            begin(act, "states")
            b = ring_wait(act, first_job["states"])
            copy(nT, ps[:, b, 0:64].rearrange("p (k s) -> p k s", k=2)).then_inc(ring_act, 1)
            for n in range(len(pairs)):
                act.wait_ge(ct_full, n + 1)
                if n >= 2:
                    act.wait_ge(iq_full, n - 1)
                copy(CT[:, n % 2, :, :].rearrange("p a b -> p (a b)"), ps[:, n % 2, :]).then_inc(ct_ready, 1)
            act.wait_ge(iq_full, len(pairs))
            copy(inter.rearrange("p i s -> p (i s)"), ps[:, 6, 0:256])
            for h in range(HM):
                act.wait_ge(cf_full, h + 1)
                copy(cpo[:, h, :, :].rearrange("p a b -> p (a b)"), ps[:, FINAL[h], :]).then_inc(c_fin, 1)
            end(act, act_stage)

            begin(act, "heads")
            act.wait_ge(bM_full, 1)
            copy(tok(tA[:, :]), two(0)).then_inc(bM_ready, 1)

            def factors(h0, h1):
                act.wait_ge(u_ready, h1)
                act.activation(u4[:, h0:h1, :], u4[:, h0:h1, :], ACT.Ln).then_inc(ln_ready, 1)
                act.wait_ge(ln_ready, 1 if h0 == 0 else 2)
                act.activation(fac4[:, h0:h1, :], u4[:, h0:h1, :], ACT.Exp, scale=-0.5).then_inc(fac_ready, 1)

            for h in range(HM):
                if h == HM - 1:
                    for s in range(2):
                        split_hi(act, p_om, 0, s)
                act.wait_ge(wt_ready, h + 1)
                act.activation(P6[:, 0:WOFF[4]], P6[:, 0:WOFF[4]], ACT.Exp)
                act.activation(P6[0:16, WOFF[4]:WOFF[5]], P6[0:16, WOFF[4]:WOFF[5]], ACT.Exp)
                act.activation(P6[0:NS, WOFF[5]:], P6[0:NS, WOFF[5]:], ACT.Exp).then_inc(we_ready, 1)
                if h == HM - 1:
                    factors(0, h)
                act.wait_ge(bm_full, h + 1)
                act.activation(tok(rstd[:, :]), two(0), ACT.Exp).then_inc(bm_ready, 1)
                if h + 1 < HM:
                    act.wait_ge(bM_full, h + 2)
                    copy(tok(tA[:, :]), two(0)).then_inc(bM_ready, 1)
                act.wait_ge(num_full, h + 1)
                for o in range(2):
                    act.activation(tC[:, o, 0:SPLIT], ps[:, 2 + 2 * o, 0:SPLIT], ACT.Square)
                    act.activation(tC[:, o, SPLIT:T], ps[:, 3 + 2 * o, 0:T - SPLIT], ACT.Square).then_inc(sqh_ready, 1)
            factors(HM - 1, HM)
            end(act, act_stage)

            begin(act, "om")

            def om_body(j, q, jn):
                for s in range(2):
                    prepare(q, jn, s)
                    act.wait_ge(mm_done[s], j + (p_om.before + 1))
                    act.wait_ge(tile_lo, j * 2 + (s + p_om.lo0))
                    act.activation(tok(t2[s][:, :]), two(2 * s), ACT.Sigmoid).then_inc(evac[s], 1)
                    act.wait_ge(om_prod, j * 2 + (s + 1))
                    copy(dyn(hm_hi, j * 2 + s), tok(t2[s][:, :])).then_inc(ohi_ready, 1)
            loop(act, p_om, om_body)
            end(act, act_stage)
            begin(act, "a_qkv")
            gated(p_a, ACT.Sigmoid, None)
            act.wait_ge(mm_done[1], p_a.before + p_a.n)
            plain(p_qkv, lambda j: copy(dyn(qkv, j * 2), two(0)).then_inc(evac[0], 1))
            end(act, act_stage)

            begin(act, "rotary")
            for n, (kind, blk) in enumerate(ROTARY, first_job["rotary"]):
                if kind != "rope":
                    nt = BLOCKS[blk][1]
                    b = ring_wait(act, n)
                    if kind == "k" and blk >= 2:
                        act.wait_ge(st_k[blk % 2], 16 * (blk // 2))
                    copy(vtok[0:nt, blk, :] if kind == "v" else kout[0:nt, blk % 2, :], wide(b, nt, D)).then_inc(ring_act, 1)
            end(act, act_stage)

            begin(act, "attend")
            for g in range(5 * HD + 3):
                if g < 5 * HD:
                    h, i = divmod(g, 5)
                    q0, nq = BLOCKS[i]
                    act.wait_ge(max_ready, g + 1)
                    if g >= 3:
                        act.wait_ge(at_full, g - 2)
                    c = 2 * (g % 4)
                    for m in range(2 if i < 4 else 1):
                        src = ps[0:nq, 2 * (i % 2) + m, 0:q0 + nq] if i < 4 else ps[0:32, 6:8, 0:264]
                        dst = Pat[g % 3][0:nq, m, 0:q0 + nq]
                        if i == 4:
                            nq = 32
                            dst = Pat[g % 3][0:32, 0, :].rearrange("p (b n) -> p b n", b=2)
                        e = act.activation(dst, src, ACT.Exp, bias=rowmax[0:nq, c + m:c + m + 1],
                                           accum_out=rowsum[0:nq, c + m:c + m + 1])
                    e.then_inc(e_ready, 1)
                if 2 <= g < 5 * HD + 2:
                    at_copy(*divmod(g - 2, 5))
                if g >= 3 and (g - 3) % 5 == 4:
                    h = (g - 3) // 5
                    act.wait_ge(o_full, h + 1)
                    copy(qkv[:, h, 0:SPLIT], ps[:, 6, 0:SPLIT])
                    copy(qkv[:, h, SPLIT:NP_], ps[:, 7, 0:NP_ - SPLIT]).then_inc(o_ready, 1)
            end(act, act_stage)

            begin(act, "sample")
            for b in range(NB):
                n = key_job(b)
                for g in range(2):
                    bank = ring_wait(act, n + 2 * g)
                    copy(KT[b % 2][0][:, :, 128 * g:128 * g + 128],
                         ps[:, bank, :].rearrange("p (h n) -> p h n", h=4)).then_inc(ring_act, 1)
                act.wait_ge(smax_ready, b + 1)
                if b >= 2:
                    act.wait_ge(ring_full, at_job(b - 2) + 1)
                c = 3 * (b % 2)
                act.activation(Psm[:, b % 2, :], ps[0:64, ring_bank(score_job(b)), 0:PAST + NS], ACT.Exp,
                               bias=srm[:, c:c + 1], accum_out=srm[:, c + 1:c + 2]).then_inc(ring_act, 1)
            end(act, act_stage)

            begin(act, "subln")
            for half in range(2):
                for h in range(4 * half, 4 * half + 4):
                    if h >= 2:
                        act.wait_ge(ring_full, first_job["subln"] + h - 1)
                    act.activation(t2[h % 2][:, :], qkv[:, h, :], ACT.Square).then_inc(osq_ready, 1)
                for h in range(4 * half, 4 * half + 4):
                    bank = ring_wait(act, first_job["subln"] + h)
                    act.activation(tok(ofac[:, h, :]), two(bank), ACT.Ln, bias=con[:, C_EPS:C_EPS + 1],
                                   scale=1.0 / 128).then_inc(ring_act, 1)
                if half == 0:
                    for s in range(2):
                        split_hi(act, p_b, 0, s)
            for h in range(HD):
                ring_done(act, first_job["subln"] + h)
                act.activation(ofac[:, h, :], ofac[:, h, :], ACT.Exp, scale=-0.5).then_inc(ofac_ready, 1)
                if h >= 1:
                    act.wait_ge(on_ready, h)
                    copy(o_hi[:, h - 1, :], qkv[:, h - 1, :]).then_inc(xhi_ready, 1)
            act.wait_ge(on_ready, HD)
            copy(o_hi[:, HD - 1, :], qkv[:, HD - 1, :]).then_inc(xhi_ready, 1)
            end(act, act_stage)

            begin(act, "b")
            gated(p_b, ACT.Sigmoid, m_hi)
            end(act, act_stage)
            begin(act, "out")
            plain(p_wo)
            end(act, act_stage)
            begin(act, "norm3")
            norm(2)
            end(act, act_stage)
            begin(act, "up2")
            gated(up2, ACT.Silu, h_hi)
            end(act, act_stage)
            begin(act, "down2")
            down(down2)
            end(act, act_stage)
            begin(act, "last")
            norm(3, final=True)
            for t in range(5):
                n = first_job["last"] + t
                if jobs[n] == "a":
                    copy(xtok[:, t, :], wide(ring_wait(act, n), 112, D)).then_inc(ring_act, 1)

        @block.vector
        def _(v):
            steps = [0]

            def link(ins_):
                steps[0] += 1
                ins_.then_inc(dve_step, 1)
                v.wait_ge(dve_step, steps[0])

            def prepare(p, j, s):
                if p is not None:
                    split_lo(v, p, j, s)

            def norm(r, gain, hi0, final=False):
                v.wait_ge(rstd_ready, 2 * r + 2)

                def lo(i):
                    v.wait_ge(xhi_ready, hi0 + i + 1)
                    v.tensor_tensor(xn_lo[:, i, :], t2[i % 2][:, :], xn_hi[:, i, :].bitcast(f32),
                                    ALU.subtract).then_inc(xlo_done, 1)
                for i in range(DT):
                    out = X[:, i, :] if final else t2[i % 2][:, :]
                    if i >= 2 and not final:
                        v.wait_ge(xlo_done, DT * r + i - 1)
                    v.scalar_tensor_tensor(out, X[:, i, :], gcol[:, gain + i:gain + i + 1], rstd[:, :],
                                           ALU.mult, ALU.mult).then_inc(xt_ready, 1)
                    if i >= 1 and not final:
                        lo(i - 1)
                if not final:
                    lo(DT - 1)

            def up(p, lo_of):
                def body(j, q, jn):
                    prepare(q, jn, 0)
                    v.wait_ge(evac[0], j + (p.ev0 + 1))
                    v.wait_ge(mm_done[1], j + (p.before + 1))
                    v.wait_ge(tile_lo, j + p.lo0)
                    v.tensor_tensor(tok(tB[:, :]), two(2), tok(tA[:, :]), ALU.mult).then_inc(evac[1], 1)
                    prepare(q, jn, 1)
                    v.wait_ge(tile_hi, j + (p.hi0 + 1))
                    v.tensor_tensor(dyn(h_lo, j), tok(tB[:, :]), dyn(h_hi, j).bitcast(f32),
                                    ALU.subtract).then_inc(tile_lo, 1)
                loop(v, p, body)

            def down(p):
                def add(j, e):
                    v.wait_ge(mm_done[1], j * 2 + (e + p.before + 1))
                    v.scalar_tensor_tensor(dyn(X, j * 2 + e), two(2 * e), 0.5, dyn(X, j * 2 + e),
                                           ALU.mult, ALU.add).then_inc(evac[e], 1)

                def body(j, q, jn):
                    for s in range(2):
                        split_lo(v, p, j * 2 + 1, s)
                    add(j, 0)
                    for s in range(2):
                        prepare(q, jn * 2, s)
                    add(j, 1)
                loop(v, p, body, 2)

            for s in range(2):
                v.drain().then_inc(lo_done[s], 1)
                v.drain().then_inc(evac[s], 1)
            v.drain().then_inc(tile_lo, 1)
            v.memset(ones[:, :], 1.0).then_inc(ones_ready, 1)
            for i in range(DT):
                if jobs[i] == "d":
                    b = ring_wait(v, i)
                    v.tensor_copy(X[:, i, 0:448], ps[:, b, 0:448])
                    v.tensor_copy(X[:, i, 448:560], ps[:, b + 1, 0:112]).then_inc(ring_dve, 1)
            v.wait_ge(in_small, 16 * 15)
            lr = lrow[:, :, :].rearrange("p (a c) d -> p a c d", c=2)
            lp = lprod[:, 0:2 * DHD].rearrange("p (a d) -> p a d", a=2)
            link(v.tensor_tensor(lp, lr[:, :, 0, :], lr[:, :, 1, :], ALU.mult))
            v.reduce_sum(lam2[:, 0:2], lp, AX.X).then_inc(lam_row, 1)
            v.wait_ge(lam_exp, 1)
            v.scalar_tensor_tensor(lam2[:, 2:3], lam2[:, 1:2], LAMBDA_INIT, lam2[:, 0:1],
                                   ALU.subtract, ALU.subtract).then_inc(lam_neg, 1)
            b = ring_wait(v, DT)
            v.tensor_copy(neglam, ps[:, b + 1, 0:1])
            link(v.tensor_copy(gcol[:, :], ps[:, b, 0:G_N]))
            v.tensor_scalar(gsub, gcol[:, G_SUB:G_SUB + 1], 1.0 - LAMBDA_INIT, None, ALU.mult)
            v.scalar_tensor_tensor(mq, con[0:32, C_Q1:C_Q1 + 1], neglam[0:32, :], con[0:32, C_Q0:C_Q0 + 1],
                                   ALU.mult, ALU.add)
            v.scalar_tensor_tensor(mv, con[0:64, C_M1:C_M1 + 1], neglam[0:64, :], con[0:64, C_M0:C_M0 + 1],
                                   ALU.mult, ALU.add).then_inc(ring_dve, 1)
            end(v, dve_stage)
            begin(v, "norm1")
            for s in range(2):
                split_lo(v, up1, 0, s)
            norm(0, G_FFN1, 0)
            end(v, dve_stage)
            begin(v, "up1")
            up(up1, h_lo)
            end(v, dve_stage)
            begin(v, "down1")
            down(down1)
            end(v, dve_stage)
            begin(v, "norm2")
            v.memset(gw[:, :, :], 0.0).then_inc(gw_zero, 1)
            norm(1, G_MIX, DT)
            v.wait_ge(ghi, 1)
            v.tensor_tensor(gw_lo[:, :, :], gw[:, :, :], gw_hi[:, :, :].bitcast(f32), ALU.subtract).then_inc(glo, 1)
            v.memset(E[:, :, 0:3], 0.0)
            end(v, dve_stage)

            begin(v, "xm")

            def xm_body(j, q, jn):
                prepare(q, jn, 0)
                prepare(q, jn, 1)
                v.wait_ge(mm_done[1], j + (p_xm.before + 1))
                e = E[:, bass.ds(j * 2 + 1, 1), :].rearrange("p o n -> p (o n)")
                v.tensor_copy(e[:, 3:3 + H2], ps[:, 2, 0:H2])
                v.tensor_copy(e[:, 3 + H2:3 + NP_], ps[:, 3, 0:NP_ - H2])
                v.tensor_copy(e[:, 3 + NP_:EXT].rearrange("p (b s) -> p b s", s=7)[:, :, 3:7],
                              ps[:, 3, NP_ - H2:H2].rearrange("p (b t) -> p b t", t=DSEQ)).then_inc(evac[1], 1)
            loop(v, p_xm, xm_body)
            end(v, dve_stage)

            begin(v, "project")
            n = first_job["project"]
            r = [rows[:, i, :] for i in range(5)]
            v.wait_ge(gates_full, 1)
            v.tensor_scalar(tok(r[4]), ps[0:4, 4:6, 0:H2], bgate[:, 0:1], None, ALU.add).then_inc(gates_read, 1)
            v.tensor_copy(tok(r[0]), ps[32:36, 4:6, 0:H2]).then_inc(gates_read, 1)
            es = E[:, :, 3 + NP_:EXT].rearrange("p i (b s) -> p i b s", s=7)
            b = ring_wait(v, n)
            v.tensor_copy(es[:, :, :, 0:3], ps[:, b, 0:192].rearrange("p (i b j) -> p i b j", i=DT, j=3)).then_inc(ring_dve, 1)
            v.memset(vtok[:, 4:6, :], 0.0)
            v.tensor_copy(xs[:, :, :].rearrange("p i (b t) -> p i b t", t=DSEQ), es[:, :, :, 3:7]).then_inc(xs_ready, 1)
            v.tensor_copy(cvt[:, :, 0:3], E[:, :, NP_:NP_ + 3])
            v.tensor_copy(cvt[:, :, 3:27].rearrange("p i (b j) -> p i b j", j=3), es[:, :, :, 4:7]).then_inc(cvt_ready, 1)

            def sam(x):
                return x[:, NP_:T].rearrange("p (b t) -> p b t", t=DSEQ)
            v.wait_ge(gates_read, 2)
            link(v.tensor_scalar(r[0], r[0], bgate[:, 1:2], None, ALU.add))
            link(v.tensor_scalar(r[1], r[0], 0.0, None, ALU.min))
            v.scalar_tensor_tensor(r[2], r[1], 2.0, r[0], ALU.mult, ALU.subtract).then_inc(row_arg, 1)
            link(v.memset(r[3], 1.0))
            v.memset(sam(r[3])[:, :, 0:1], 0.0)
            v.wait_ge(row_fun, 2)
            link(v.tensor_tensor(r[1], r[1], r[2], ALU.subtract))
            link(v.tensor_tensor_scan(r[0], r[3], r[1], 0.0, ALU.mult, ALU.add))
            link(v.tensor_tensor(r[1], r[4], r[0], ALU.subtract))
            v.tensor_copy(r[2], r[1])
            link(v.memset(r[3], 0.0))
            v.memset(sam(r[3])[:, :, 0:1], NEG)
            link(v.tensor_tensor(sam(r[2])[:, :, 0], sam(r[1])[:, :, 0], m0row, ALU.max))
            link(v.tensor_tensor_scan(r[4], r[3], r[2], 0.0, ALU.add, ALU.max))
            link(v.tensor_tensor(r[3], r[0], r[4], ALU.add))
            v.tensor_copy(mout[:, 0:1], r[3][:, NP_ - 1:NP_])
            v.tensor_copy(mout[:, 1:9], sam(r[3])[:, :, DSEQ - 1]).then_inc(m_ready, 1)
            v.tensor_scalar(r[2], r[4], -1.0, None, ALU.mult)
            v.tensor_tensor(wrow.rearrange("p (b t) -> p b t", t=DSEQ),
                            m0row.unsqueeze(2).to_broadcast([HM, NB, DSEQ]), sam(r[4]), ALU.subtract)
            v.tensor_scalar(r[0][:, 0:NP_], r[1][:, 0:NP_], r[4][:, NP_ - 1:NP_], None, ALU.subtract)
            v.tensor_tensor(sam(r[0]), sam(r[1]), sam(r[4])[:, :, DSEQ - 1:DSEQ].to_broadcast([HM, NB, DSEQ]),
                            ALU.subtract).then_inc(row_arg, 1)
            v.wait_ge(m_ready, 1)
            v.tensor_scalar(r[3], r[3], -1.0, None, ALU.mult)
            for i in range(DT):
                outs_ = (cc[:, i, 0:NP_], cc[:, i, NP_:T].rearrange("p (b t) -> p b t", t=DSEQ))
                for j in range(4):
                    w = gcol[:, G_CW + 8 * j + i:G_CW + 8 * j + i + 1]
                    for k, o in enumerate(outs_):
                        x = E[:, i, j:j + NP_] if k == 0 else es[:, i, :, j:j + DSEQ]
                        if j == 0:
                            c = v.tensor_scalar(o, x, w, gcol[:, G_CB + i:G_CB + i + 1], ALU.mult, ALU.add)
                        else:
                            c = v.scalar_tensor_tensor(o, x, w, o, ALU.mult, ALU.add)
                    if j < 3:
                        link(c)
                c.then_inc(conv_ready, 1)
                if i == 3:
                    bank = ring_wait(v, n + 8)
                    a32 = small2[:, 0:48]
                    v.tensor_copy(a32[:, 0:32], ps[:, bank, 0:32])
                    v.tensor_copy(a32[0:16, 32:40], ps[0:16, bank, 32:40])
                    v.tensor_copy(a32[0:NS, 40:48], ps[0:NS, bank, 40:48])
                    v.tensor_copy(dec8, ps[0:NB, bank, 64:68])
                    v.tensor_copy(small2[:, 80:208], ps[:, bank + 1, 0:128]).then_inc(ring_dve, 1)
            v.wait_ge(ring_full, n + 25)
            link(v.memset(ktok[:, 4, :], 0.0))
            for blk, (t0, nt) in enumerate(BLOCKS):
                bank = ring_wait(v, n + 25 + blk)
                v.tensor_tensor(ktok[0:nt, blk, :].rearrange("p (h d) -> p h d", h=HM),
                                wide(bank, nt, D).rearrange("p (h d) -> p h d", h=HM),
                                acol[0:nt, blk, 1, :].unsqueeze(2).to_broadcast([nt, HM, DHM]),
                                ALU.mult).then_inc(ring_dve, 1)
            end(v, dve_stage)

            begin(v, "states")
            def masked_k(h, b):
                v.tensor_scalar(kwb[h % 2][0:NS, b, :], ktok[0:NS, 5, DHM * h:DHM * h + DHM],
                                con[0:NS, C_BM + b:C_BM + b + 1], None, ALU.mult).then_inc(kwb_ready, 1)

            link(v.memset(kwb[0][:, :, :], 0.0))
            link(v.tensor_tensor(qs[:, :, :].rearrange("p (h k) s -> p h k s", k=2),
                                 qm[:, :, NP_:T].rearrange("p (h k) s -> p h k s", k=2),
                                 wbc.unsqueeze(2).to_broadcast([128, HM, 2, NS]), ALU.mult))
            ring_done(v, first_job["states"])
            for h in range(HM):
                c = v.tensor_tensor(nqs[:, 2 * h:2 * h + 2, :].rearrange("p k (b t) -> p k b t", t=DSEQ),
                                    qs[:, 2 * h:2 * h + 2, :].rearrange("p k (b t) -> p k b t", t=DSEQ),
                                    nT.rearrange("p k (b h) -> p k b h", h=HM)[:, :, :, h:h + 1].to_broadcast([128, 2, NB, DSEQ]),
                                    ALU.mult)
            c.then_inc(qs_ready, 1)
            link(v.tensor_tensor(nst[:, :, :], nst[:, :, :], dec8.unsqueeze(2).to_broadcast([NB, HM, DHM]), ALU.mult))
            for b in range(NB):
                masked_k(0, b)
            for n, (h, b) in enumerate(pairs):
                v.wait_ge(cu_full, n + 1)
                st = Cb[:, n % 4, :, :].rearrange("p a b -> p (a b)")
                v.scalar_tensor_tensor(st, st, wbc[:, h, DSEQ * b + DSEQ - 1:DSEQ * b + DSEQ], ps[:, 2 + n % 2, :],
                                       ALU.mult, ALU.add).then_inc(c_new, 1)
                if h == 0 and b == 0:
                    link(v.memset(kwb[1][:, :, :], 0.0))
                if h + 1 < HM:
                    masked_k(h + 1, b)
            v.wait_ge(nn_full, 1)
            v.tensor_tensor(nst[:, :, :].rearrange("p h d -> p (h d)"), nst[:, :, :].rearrange("p h d -> p (h d)"),
                            wide(4, NB, D), ALU.add).then_inc(n_new, 1)
            v.wait_ge(nf_full, 1)
            v.tensor_copy(npo[:, :], wide(4, 1, D)).then_inc(n_fin, 1)
            end(v, dve_stage)

            begin(v, "heads")

            def weight_arg(h):
                v.wait_ge(bM_ready, h + 1)
                for blk, (t0, nt) in enumerate(BLOCKS):
                    nq_ = NP_ - t0 if blk < 5 else NS
                    c = v.tensor_scalar(P6[0:nt, WOFF[blk]:WOFF[blk] + nq_], tA[0:nt, t0:t0 + nq_],
                                        acol[0:nt, blk, 0, h:h + 1], 0.0, ALU.add, ALU.min)
                c.then_inc(wt_ready, 1)
            weight_arg(0)
            for h in range(HM):
                v.wait_ge(we_ready, h + 1)
                for blk, (t0, nt) in enumerate(BLOCKS):
                    mask = con[0:nt, C_CAUSAL:C_CAUSAL + nt] if blk < 5 else con[0:NS, C_BLK:C_BLK + NS]
                    d = P6[0:nt, WOFF[blk]:WOFF[blk] + nt]
                    c = v.tensor_tensor(d, d, mask, ALU.mult)
                link(c)
                for blk, (t0, nt) in enumerate(BLOCKS):
                    nq_ = NP_ - t0 if blk < 5 else NS
                    v.wait_ge(sc_full, 6 * h + blk + 1)
                    if blk == 0:
                        v.tensor_tensor(P6[:, 0:SPLIT], ps[:, 0, 0:SPLIT], P6[:, 0:SPLIT], ALU.mult)
                        v.tensor_tensor(P6[:, SPLIT:NP_], ps[:, 1, 0:NP_ - SPLIT], P6[:, SPLIT:NP_],
                                        ALU.mult).then_inc(p_ready, 1)
                    else:
                        p = P6[0:nt, WOFF[blk]:WOFF[blk] + nq_]
                        v.tensor_tensor(p, ps[0:nt, (blk + 1) % 2, 0:nq_], p, ALU.mult).then_inc(p_ready, 1)
                v.wait_ge(num_full, h + 1)
                v.wait_ge(bm_ready, h + 1)
                for half, (c0, c1) in enumerate(((0, SPLIT), (SPLIT, T))):
                    c = v.scalar_tensor_tensor(rstd[:, c0:c1], ps[:, 6 + half, 0:c1 - c0], -1.0, rstd[:, c0:c1],
                                               ALU.mult, ALU.max)
                link(c)
                for half, (c0, c1) in enumerate(((0, SPLIT), (SPLIT, T))):
                    c = v.tensor_tensor(rstd[:, c0:c1], ps[:, 6 + half, 0:c1 - c0], rstd[:, c0:c1], ALU.max)
                link(c)
                link(v.scalar_tensor_tensor(rstd[:, :], rstd[:, :], EPS, rstd[:, :], ALU.mult, ALU.mult))
                if h + 1 < HM:
                    weight_arg(h + 1)
                if h == 0:
                    v.wait_ge(st_c, 16 * HM)
                    v.wait_ge(stored, 16 * 6)
                v.wait_ge(ssh_full, h + 1)
                v.scalar_tensor_tensor(tok(u4[:, h, :]), two(0), 1.0 / DHM, tok(rstd[:, :]),
                                       ALU.mult, ALU.add).then_inc(u_ready, 1)
                for o in range(2):
                    v.wait_ge(sqh_ready, 2 * h + o + 1)
                    g = gcol[:, G_ML + 2 * h + o:G_ML + 2 * h + o + 1]
                    for half, (c0, c1) in enumerate(((0, SPLIT), (SPLIT, T))):
                        c = v.tensor_scalar(qm[:, 2 * h + o, c0:c1], ps[:, 2 + 2 * o + half, 0:c1 - c0], g, None, ALU.mult)
                c.then_inc(hm_ready, 1)
            v.wait_ge(fac_ready, 2)
            for s in range(2):
                split_lo(v, p_om, 0, s)
            end(v, dve_stage)

            begin(v, "om")

            def om_body(j, q, jn):
                for s in range(2):
                    prepare(q, jn, s)
                    v.wait_ge(evac[s], j + (p_om.ev0 + 1))
                    v.tensor_tensor(tok(t2[s][:, :]), tok(t2[s][:, :]), dyn(qm, j * 2 + s), ALU.mult).then_inc(om_gated, 1)
                    v.wait_ge(om_gated, j * 2 + (s + 1))
                    v.tensor_tensor(tok(t2[s][:, :]), tok(t2[s][:, :]), dyn(fac4, j), ALU.mult).then_inc(om_prod, 1)
                    v.wait_ge(ohi_ready, j * 2 + (s + 1))
                    v.tensor_tensor(dyn(hm_lo, j * 2 + s), tok(t2[s][:, :]), dyn(hm_hi, j * 2 + s).bitcast(f32),
                                    ALU.subtract).then_inc(tile_lo, 1)
            loop(v, p_om, om_body)
            end(v, dve_stage)

            begin(v, "a_qkv")

            def a_body(j, q, jn):
                prepare(q, jn, 0)
                v.wait_ge(evac[0], j + (p_a.ev0 + 1))
                v.wait_ge(mm_done[1], j + (p_a.before + 1))
                v.tensor_tensor(dyn(M, j), two(2), tok(tA[:, :]), ALU.mult).then_inc(evac[1], 1)
                prepare(q, jn, 1)
            loop(v, p_a, a_body)
            v.wait_ge(mm_done[1], p_a.before + p_a.n)

            def qkv_body(j, q, jn):
                prepare(q, jn, 0)
                prepare(q, jn, 1)
                v.wait_ge(mm_done[1], j + (p_qkv.before + 1))
                v.tensor_copy(dyn(qkv, j * 2 + 1), two(2)).then_inc(evac[1], 1)
            loop(v, p_qkv, qkv_body)
            end(v, dve_stage)

            begin(v, "rotary")
            v.wait_ge(in_trig, 16)
            cos, sin = trig[:, 0, :], trig[:, 1, :]
            for n, (kind, i) in enumerate(ROTARY, first_job["rotary"]):
                if kind == "rope":
                    bank = ring_wait(v, n)
                    v.tensor_tensor(tok(t2[i % 2][:, :]), two(bank), tok(sin), ALU.mult).then_inc(ring_dve, 1)
                    link(v.tensor_tensor(qkv[:, i, :], qkv[:, i, :], cos, ALU.mult))
                    v.tensor_tensor(qkv[:, i, :], qkv[:, i, :], t2[i % 2][:, :], ALU.add).then_inc(rot_ready, 1)
            end(v, dve_stage)

            begin(v, "attend")
            for b in range(2):
                v.memset(qz[64:128, b, 0, :], 0.0)
                v.memset(qz[0:64, b, 1, :], 0.0)
                v.memset(q4[64:128, b, 0:16], 0.0)
                v.memset(q4[0:64, b, 16:32], 0.0)

            def scaled_q(h):
                if h >= 2:
                    v.wait_ge(s_full, 5 * (h - 1))
                v.tensor_scalar(q4[0:64, h % 2, 0:16], qkv[0:64, h, 512:NP_], DHD ** -0.5, None, ALU.mult)
                v.tensor_scalar(q4[64:128, h % 2, 16:32], qkv[64:128, h, 512:NP_], DHD ** -0.5, None, ALU.mult)
                v.tensor_scalar(qz[0:64, h % 2, 0, 0:NP_], qkv[0:64, h, 0:NP_], DHD ** -0.5, None, ALU.mult)
                v.tensor_scalar(qz[64:128, h % 2, 1, 0:NP_], qkv[64:128, h, 0:NP_], DHD ** -0.5, None,
                                ALU.mult).then_inc(qz_ready, 1)

            def combine(g):
                i = g % 5
                q0, nq_ = BLOCKS[i]
                c = 2 * (g % 4)
                nk = q0 + nq_
                v.wait_ge(e_ready, g + 1)
                if i == 4:
                    link(v.reciprocal(rinv[0:32, c:c + 1], rowsum[0:32, c:c + 1]))
                    v.tensor_scalar(Pat[g % 3][0:32, 0, :], Pat[g % 3][0:32, 0, :], rinv[0:32, c:c + 1], mq,
                                    ALU.mult, ALU.mult).then_inc(a_ready, 1)
                    return
                link(v.reciprocal(rinv[0:nq_, c:c + 2], rowsum[0:nq_, c:c + 2]))
                v.tensor_scalar(Pat[g % 3][0:nq_, 0, 0:nk], Pat[g % 3][0:nq_, 0, 0:nk], rinv[0:nq_, c:c + 1], None, ALU.mult)
                link(v.tensor_tensor(rinv[0:nq_, c + 1:c + 2], rinv[0:nq_, c + 1:c + 2], neglam[0:nq_, :], ALU.mult))
                v.scalar_tensor_tensor(Pat[g % 3][0:nq_, 0, 0:nk], Pat[g % 3][0:nq_, 1, 0:nk], rinv[0:nq_, c + 1:c + 2],
                                       Pat[g % 3][0:nq_, 0, 0:nk], ALU.mult, ALU.add).then_inc(a_ready, 1)

            scaled_q(0)
            for g in range(5 * HD):
                h, i = g // 5, g % 5
                q0, nq_ = BLOCKS[i]
                v.wait_ge(s_full, g + 1)
                c = 2 * (g % 4)
                if i < 4:
                    v.tensor_reduce(rowmax[0:nq_, c:c + 2], ps[0:nq_, 2 * (i % 2):2 * (i % 2) + 2, 0:q0 + nq_], AX.X, ALU.max,
                                    negate=True).then_inc(max_ready, 1)
                else:
                    v.tensor_reduce(rowmax[0:32, c:c + 1], ps[0:32, 6:8, 0:264], AX.XY, ALU.max,
                                    negate=True).then_inc(max_ready, 1)
                if i == 2 and h + 1 < HD:
                    scaled_q(h + 1)
                if g >= 1:
                    combine(g - 1)
            combine(5 * HD - 1)
            end(v, dve_stage)

            begin(v, "sample")
            link(v.memset(Qbd[:, :, :, :], 0.0))
            for h in range(HD):
                for m in range(2):
                    q = qkv[64 * m:64 * m + 64, h, NP_:T].rearrange("p (b t) -> p b t", t=DSEQ)
                    v.tensor_scalar(Qbd[64 * m:64 * m + 64, :, h, 8 * h + 4 * m:8 * h + 4 * m + 4], q,
                                    DHD ** -0.5, None, ALU.mult)
            for b in range(2):
                for i in range(2):
                    c = v.tensor_copy(KT[b][i][:, :, PAST:PAST + NS], qkv[:, DT + 4 * i:DT + 4 * i + 4, NP_:T])
            c.then_inc(qbd_ready, 1)
            for b in range(NB + 1):
                if b >= 1:
                    c = 3 * ((b - 1) % 2)
                    ring_done(v, score_job(b - 1))
                    link(v.reciprocal(srm[:, c + 2:c + 3], srm[:, c + 1:c + 2]))
                    v.tensor_scalar(Psm[:, (b - 1) % 2, :], Psm[:, (b - 1) % 2, :], srm[:, c + 2:c + 3], mv, ALU.mult,
                                    ALU.mult).then_inc(sp_ready, 1)
                if b < NB:
                    for g in range(2):
                        bank = ring_wait(v, key_job(b) + 2 * g + 1)
                        v.tensor_copy(KT[b % 2][1][:, :, 128 * g:128 * g + 128],
                                      ps[:, bank, :].rearrange("p (h n) -> p h n", h=4)).then_inc(ring_dve, 1)
                if b >= 1:
                    bank = ring_wait(v, at_job(b - 1))
                    v.tensor_copy(AT3[:, (b - 1) % 2, 0:2, :], ps[:, bank, 0:64].rearrange("p (g s) -> p g s", g=2))
                    v.tensor_copy(AT3[0:NS, (b - 1) % 2, 2, :], ps[0:NS, bank, 64:96]).then_inc(ring_dve, 1)
                if b < NB:
                    bank = ring_wait(v, score_job(b))
                    c = 3 * (b % 2)
                    v.reduce_max(srm[:, c:c + 1], ps[0:64, bank, 0:PAST + NS], AX.X, negate=True).then_inc(smax_ready, 1)
                if b >= 1:
                    bank = ring_wait(v, out_job(b - 1))
                    v.tensor_copy(qkv[:, 0:DT, NP_ + 4 * b - 4:NP_ + 4 * b],
                                  ps[:, bank, 0:32].rearrange("p (h t) -> p h t", t=DSEQ)).then_inc(ring_dve, 1)
            end(v, dve_stage)

            begin(v, "subln")
            for s in range(2):
                split_lo(v, p_b, 0, s)
            for h in range(HD + 1):
                if h < HD:
                    v.wait_ge(ofac_ready, h + 1)
                    v.scalar_tensor_tensor(qkv[:, h, :], qkv[:, h, :], gsub, ofac[:, h, :], ALU.mult,
                                           ALU.mult).then_inc(on_ready, 1)
                if h >= 1:
                    v.wait_ge(xhi_ready, 2 * DT + h)
                    v.tensor_tensor(o_lo[:, h - 1, :], qkv[:, h - 1, :], o_hi[:, h - 1, :].bitcast(f32),
                                    ALU.subtract).then_inc(olo_done, 1)
            end(v, dve_stage)

            begin(v, "b")

            def b_body(j, q, jn):
                prepare(q, jn, 0)
                v.wait_ge(evac[0], j + (p_b.ev0 + 1))
                v.wait_ge(mm_done[1], j + (p_b.before + 1))
                v.wait_ge(tile_lo, j * 2 + p_b.lo0)
                v.tensor_tensor(tok(tB[:, :]), two(2), tok(tA[:, :]), ALU.mult).then_inc(tile_lo, 1)
                v.wait_ge(tile_lo, j * 2 + (p_b.lo0 + 1))
                v.tensor_tensor(tok(tB[:, :]), tok(tB[:, :]), dyn(M, j), ALU.add).then_inc(evac[1], 1)
                prepare(q, jn, 1)
                v.wait_ge(tile_hi, j + (p_b.hi0 + 1))
                v.tensor_tensor(dyn(m_lo, j), tok(tB[:, :]), dyn(m_hi, j).bitcast(f32),
                                ALU.subtract).then_inc(tile_lo, 1)
            loop(v, p_b, b_body)
            end(v, dve_stage)

            begin(v, "out")

            def wo_body(j, q, jn):
                for s in range(2):
                    prepare(q, jn, s)
                    v.wait_ge(mm_done[s], j + (p_wo.before + 1))
                    v.tensor_tensor(dyn(X, j * 2 + s), two(2 * s), dyn(X, j * 2 + s), ALU.add).then_inc(evac[s], 1)
            loop(v, p_wo, wo_body)
            end(v, dve_stage)
            begin(v, "norm3")
            norm(2, G_FFN2, 3 * DT)
            end(v, dve_stage)
            begin(v, "up2")
            up(up2, h_lo)
            end(v, dve_stage)
            begin(v, "down2")
            down(down2)
            end(v, dve_stage)
            begin(v, "last")
            norm(3, G_FINAL, 0, final=True)
            for t in range(5):
                n = first_job["last"] + t
                if jobs[n] == "d":
                    v.tensor_copy(xtok[:, t, :], wide(ring_wait(v, n), 112, D)).then_inc(ring_dve, 1)


_INS = ["x_prompt", "x_sample", "cache_k", "cache_v", "page_table", "state_C", "state_n", "state_m", "state_conv",
        "meta_tokens", "ffn1_norm", "ffn1_w_gate", "ffn1_w_up", "ffn1_w_down", "mix_norm", "w_in",
        "conv_w", "conv_b", "w_mq", "w_mk", "w_mv", "b_igate", "b_fgate", "mlstm_norm",
        "lambda_q1", "lambda_k1", "lambda_q2", "lambda_k2", "subln", "w_proj_a", "w_proj_b", "w_out",
        "ffn2_norm", "ffn2_w_gate", "ffn2_w_up", "ffn2_w_down", "final_norm"]


def kernel(**inputs):
    import concourse.bacc as _bacc
    from concourse.bass_utils import run_bass_kernel_spmd as _run

    nc = _bacc.Bacc("TRN2", target_bir_lowering=False, num_devices=1)
    arrays, aps = {}, {}
    for name in _INS:
        a = np.ascontiguousarray(inputs[name])
        arrays[f"in_{name}"] = a
        aps[name] = nc.dram_tensor(f"in_{name}", a.shape, mybir.dt.from_np(a.dtype), kind="ExternalInput").ap()
    c = constants()
    arrays["constants"] = c
    const_ap = nc.dram_tensor("constants", c.shape, mybir.dt.float32, kind="ExternalInput").ap()
    outs = [nc.dram_tensor(f"out_{i}", shape, mybir.dt.float32, kind="ExternalOutput").ap()
            for i, shape in enumerate(OUTS)]
    build(nc, aps, outs, const_ap)
    r = _run(nc, [arrays], core_ids=[0])
    return tuple(r.results[0][f"out_{i}"] for i in range(len(OUTS)))
```
